# Optimizing a Trainium2 kernel written in Bass

```python
import math
import jax, jax.numpy as jnp
from jax import lax
import numpy as np

D_MODEL = 1024
BATCH = 1
SEQ = 512
DEPTH = 2

HEAD_DIM = 64
GM_GROUPS = 4
GM_CHUNK = 128
GM_WIDTH = GM_GROUPS * HEAD_DIM
DA_HEADS = 4
DA_QK_DIM = HEAD_DIM // 2
DA_V_DIM = HEAD_DIM
DA_QK_WIDTH = DA_HEADS * 2 * DA_QK_DIM
DA_WIDTH = DA_HEADS * DA_V_DIM
NSA_HEADS = 8
NSA_KV_GROUPS = 2
NSA_WIDTH = NSA_HEADS * HEAD_DIM
NSA_KV_WIDTH = NSA_KV_GROUPS * HEAD_DIM
CMP_LEN = 32
CMP_STRIDE = 16
CMP_HIDDEN = 256
SLC_LEN = 64
SLC_TOPK = 16
WIN = 512
FORCE_BONUS = 1000.0
Q_BLOCK = 128
SLC_Q_BLOCK = 64
D_FF = 2816
ROPE_THETA = 10000.0
EPS = 1e-6
N_MOD = 9
D_MIX = GM_WIDTH + DA_WIDTH + NSA_WIDTH
IN_WIDTHS = (GM_WIDTH, GM_WIDTH,
             DA_QK_WIDTH, DA_QK_WIDTH, DA_WIDTH,
             NSA_WIDTH, NSA_KV_WIDTH, NSA_KV_WIDTH, NSA_KV_WIDTH,
             NSA_KV_WIDTH, NSA_KV_WIDTH, NSA_KV_WIDTH, 3 * NSA_HEADS)
D_IN = 2 * GM_WIDTH + 2 * DA_QK_WIDTH + DA_WIDTH + NSA_WIDTH + 6 * NSA_KV_WIDTH + 3 * NSA_HEADS


def _rmsnorm(x, g):
    xf = x.astype(jnp.float32)
    y = xf * lax.rsqrt(jnp.mean(xf * xf, axis=-1, keepdims=True) + EPS)
    return (y * g.astype(jnp.float32)).astype(x.dtype)

def _rope(x, pos):
    d = x.shape[-1]
    half = d // 2
    inv = ROPE_THETA ** (-jnp.arange(half, dtype=jnp.float32) / half)
    ang = pos.astype(jnp.float32)[:, None] * inv[None, :]
    cos, sin = jnp.cos(ang), jnp.sin(ang)
    xf = x.astype(jnp.float32)
    x1, x2 = xf[..., :half], xf[..., half:]
    return jnp.concatenate([x1 * cos - x2 * sin, x2 * cos + x1 * sin], axis=-1).astype(x.dtype)

def _masked_softmax(s, mask):
    p = jax.nn.softmax(jnp.where(mask, s, jnp.finfo(jnp.float32).min), axis=-1)
    return jnp.where(mask, p, 0.0)

def _swiglu(h, w_gate, w_up, w_down):
    return (jax.nn.silu(h @ w_gate) * (h @ w_up)) @ w_down

def _gmlp_sgu(u, v, ln_g, w_s, b_s):
    B_, S_, _ = u.shape
    u = jax.nn.gelu(u)
    vf = jax.nn.gelu(v).reshape(B_, S_, GM_GROUPS, HEAD_DIM).astype(jnp.float32)
    mu = jnp.mean(vf, axis=-1, keepdims=True)
    var = jnp.mean((vf - mu) ** 2, axis=-1, keepdims=True)
    vn = ((vf - mu) * lax.rsqrt(var + EPS)).astype(v.dtype) * ln_g.reshape(GM_GROUPS, HEAD_DIM)
    vc = vn.reshape(B_, S_ // GM_CHUNK, GM_CHUNK, GM_GROUPS, HEAD_DIM)
    causal = jnp.tril(jnp.ones((GM_CHUNK, GM_CHUNK), dtype=bool))
    w = jnp.where(causal[None], w_s, jnp.zeros_like(w_s))
    s = jnp.einsum('gts,bnsgd->bntgd', w, vc) + b_s.T[None, None, :, :, None]
    return u * s.reshape(B_, S_, GM_WIDTH)

def _diff_attention(q, k, v, lam, sub_g, lam_init):
    B_, S_, _ = q.shape
    pos = jnp.arange(S_)
    q = _rope(q.reshape(B_, S_, DA_HEADS, 2, DA_QK_DIM).transpose(0, 2, 3, 1, 4), pos)
    k = _rope(k.reshape(B_, S_, DA_HEADS, 2, DA_QK_DIM).transpose(0, 2, 3, 1, 4), pos)
    v = v.reshape(B_, S_, DA_HEADS, DA_V_DIM).transpose(0, 2, 1, 3)
    scale = DA_QK_DIM ** -0.5
    nb = S_ // Q_BLOCK
    qb = q.reshape(B_, DA_HEADS, 2, nb, Q_BLOCK, DA_QK_DIM).transpose(3, 0, 1, 2, 4, 5)

    def block(args):
        qi, i = args
        s = jnp.einsum('bhmqd,bhmkd->bhmqk', qi, k).astype(jnp.float32) * scale
        t = i * Q_BLOCK + jnp.arange(Q_BLOCK)
        p = _masked_softmax(s, t[:, None] >= pos[None, :])
        a = p[:, :, 0] - lam * p[:, :, 1]
        return jnp.einsum('bhqk,bhkd->bhqd', a.astype(v.dtype), v)

    o = lax.map(block, (qb, jnp.arange(nb)))
    o = o.transpose(1, 2, 0, 3, 4).reshape(B_, DA_HEADS, S_, DA_V_DIM)
    o = _rmsnorm(o, sub_g) * (1.0 - lam_init)
    return o.transpose(0, 2, 1, 3).reshape(B_, S_, DA_WIDTH)

def _compress(x, pe, w1, w2):
    S_ = x.shape[2]
    nc = (S_ - CMP_LEN) // CMP_STRIDE + 1
    idx = jnp.arange(nc)[:, None] * CMP_STRIDE + jnp.arange(CMP_LEN)[None, :]
    blocks = x[:, :, idx] + pe
    flat = blocks.reshape(blocks.shape[0], blocks.shape[1], nc, CMP_LEN * HEAD_DIM)
    return jax.nn.silu(flat @ w1) @ w2

def _cmp_to_slc(nc, ns):
    cs = np.arange(nc) * CMP_STRIDE
    ce = cs + CMP_LEN
    bs = np.arange(ns) * SLC_LEN
    be = bs + SLC_LEN
    ov = np.clip(np.minimum(ce[:, None], be[None, :]) - np.maximum(cs[:, None], bs[None, :]), 0, None)
    return (ov / CMP_STRIDE).astype(np.float32)

def _nsa(q, kc, vc, ks, vs, kw, vw, gates, pe, w1, w2):
    B_, S_, _ = q.shape
    G, Hg, Dh = NSA_KV_GROUPS, NSA_HEADS // NSA_KV_GROUPS, HEAD_DIM
    pos = jnp.arange(S_)
    scale = Dh ** -0.5
    q = _rope(q.reshape(B_, S_, G, Hg, Dh).transpose(0, 2, 3, 1, 4), pos)

    def kv(t):
        return t.reshape(B_, S_, G, Dh).transpose(0, 2, 1, 3)

    nc = (S_ - CMP_LEN) // CMP_STRIDE + 1
    cmp_end = jnp.arange(nc) * CMP_STRIDE + CMP_LEN - 1
    k_cmp = _rope(_compress(kv(kc), pe[0], w1[0], w2[0]), cmp_end)
    v_cmp = _compress(kv(vc), pe[1], w1[1], w2[1])
    s = jnp.einsum('bgjtd,bgcd->bgjtc', q, k_cmp).astype(jnp.float32) * scale
    p_cmp = _masked_softmax(s, cmp_end[None, :] <= pos[:, None])
    o_cmp = jnp.einsum('bgjtc,bgcd->bgjtd', p_cmp.astype(q.dtype), v_cmp)

    ns = S_ // SLC_LEN
    topk = min(SLC_TOPK, ns)
    imp = jnp.einsum('bgjtc,cn->bgtn', p_cmp, jnp.asarray(_cmp_to_slc(nc, ns)))
    blk = jnp.arange(ns)[None, :]
    cur = (pos // SLC_LEN)[:, None]
    valid = blk <= cur
    forced = valid & ((blk == 0) | (blk >= cur - 1))
    score = jnp.where(forced, FORCE_BONUS, jnp.where(valid, imp, -1.0))
    top_val, top_idx = lax.top_k(score, topk)
    top_ok = top_val >= 0.0
    k_slc = _rope(kv(ks), pos).reshape(B_, G, ns, SLC_LEN, Dh)
    v_slc = kv(vs).reshape(B_, G, ns, SLC_LEN, Dh)
    nqb = S_ // SLC_Q_BLOCK
    qs = q.reshape(B_, G, Hg, nqb, SLC_Q_BLOCK, Dh).transpose(3, 0, 1, 2, 4, 5)
    ib = top_idx.reshape(B_, G, nqb, SLC_Q_BLOCK, topk).transpose(2, 0, 1, 3, 4)
    okb = top_ok.reshape(B_, G, nqb, SLC_Q_BLOCK, topk).transpose(2, 0, 1, 3, 4)
    gather = jax.vmap(jax.vmap(lambda blocks, ix: blocks[ix]))

    def slc_block(args):
        qi, ix, ok, i = args
        kg = gather(k_slc, ix)
        vg = gather(v_slc, ix)
        t = i * SLC_Q_BLOCK + jnp.arange(SLC_Q_BLOCK)
        kpos = ix[..., None] * SLC_LEN + jnp.arange(SLC_LEN)
        mask = ok[..., None] & (kpos <= t[:, None, None])
        sc = jnp.einsum('bgjqd,bgqnld->bgjqnl', qi, kg).astype(jnp.float32) * scale
        sc = sc.reshape(B_, G, Hg, SLC_Q_BLOCK, topk * SLC_LEN)
        p = _masked_softmax(sc, mask.reshape(B_, G, 1, SLC_Q_BLOCK, topk * SLC_LEN))
        p = p.reshape(B_, G, Hg, SLC_Q_BLOCK, topk, SLC_LEN)
        return jnp.einsum('bgjqnl,bgqnld->bgjqd', p.astype(vg.dtype), vg)

    o_slc = lax.map(slc_block, (qs, ib, okb, jnp.arange(nqb)))
    o_slc = o_slc.transpose(1, 2, 3, 0, 4, 5).reshape(B_, G, Hg, S_, Dh)

    pad = ((0, 0), (0, 0), (WIN, 0), (0, 0))
    k_win = jnp.pad(_rope(kv(kw), pos), pad)
    v_win = jnp.pad(kv(vw), pad)
    nb = S_ // Q_BLOCK
    qw = q.reshape(B_, G, Hg, nb, Q_BLOCK, Dh).transpose(3, 0, 1, 2, 4, 5)

    def win_block(args):
        qi, i = args
        start = i * Q_BLOCK
        kb = lax.dynamic_slice_in_dim(k_win, start, WIN + Q_BLOCK, axis=2)
        vb = lax.dynamic_slice_in_dim(v_win, start, WIN + Q_BLOCK, axis=2)
        t = start + jnp.arange(Q_BLOCK)
        kpos = start - WIN + jnp.arange(WIN + Q_BLOCK)
        dist = t[:, None] - kpos[None, :]
        mask = (kpos[None, :] >= 0) & (dist >= 0) & (dist < WIN)
        sc = jnp.einsum('bgjqd,bgkd->bgjqk', qi, kb).astype(jnp.float32) * scale
        p = _masked_softmax(sc, mask)
        return jnp.einsum('bgjqk,bgkd->bgjqd', p.astype(vb.dtype), vb)

    o_win = lax.map(win_block, (qw, jnp.arange(nb)))
    o_win = o_win.transpose(1, 2, 3, 0, 4, 5).reshape(B_, G, Hg, S_, Dh)

    g = jax.nn.sigmoid(gates.astype(jnp.float32)).reshape(B_, S_, G, Hg, 3).transpose(0, 2, 3, 1, 4).astype(q.dtype)
    o = g[..., 0:1] * o_cmp + g[..., 1:2] * o_slc + g[..., 2:3] * o_win
    return o.transpose(0, 3, 1, 2, 4).reshape(B_, S_, NSA_WIDTH)

def _token_mix(h, w_in, w_out, gm_ln_g, gm_w_s, gm_b_s, da_lambda, da_sub_g, cmp_pe, cmp_w1, cmp_w2, lam_init):
    z = h @ w_in
    pts = np.cumsum(np.array(IN_WIDTHS))[:-1].tolist()
    (gu, gv, dq, dk, dv, nq, nkc, nvc, nks, nvs, nkw, nvw, ng) = jnp.split(z, pts, axis=-1)
    y_a = _gmlp_sgu(gu, gv, gm_ln_g, gm_w_s, gm_b_s)
    lf = da_lambda.astype(jnp.float32)
    lam = jnp.exp(jnp.sum(lf[0] * lf[1])) - jnp.exp(jnp.sum(lf[2] * lf[3])) + lam_init
    y_b = _diff_attention(dq, dk, dv, lam, da_sub_g, lam_init)
    y_c = _nsa(nq, nkc, nvc, nks, nvs, nkw, nvw, ng, cmp_pe, cmp_w1, cmp_w2)
    return jnp.concatenate([y_a, y_b, y_c], axis=-1) @ w_out

def first_inputs(seed: int = 0) -> dict:
    key = jax.random.key(seed)
    ks = jax.random.split(key, 19)
    f32 = jnp.float32

    def nrm(k, shape, std):
        return std * jax.random.normal(k, shape, f32)

    L = DEPTH
    return {
        "x": nrm(ks[0], (BATCH, SEQ, D_MODEL), 1.0),
        "c": nrm(ks[1], (BATCH, D_MODEL), 1.0),
        "w_ada": nrm(ks[2], (L, D_MODEL, N_MOD * D_MODEL), 0.02),
        "b_ada": nrm(ks[3], (L, N_MOD * D_MODEL), 0.02),
        "norm_g": 1.0 + nrm(ks[4], (L, 3, D_MODEL), 0.05),
        "ffn_w_gate": nrm(ks[5], (L, 2, D_MODEL, D_FF), D_MODEL ** -0.5),
        "ffn_w_up": nrm(ks[6], (L, 2, D_MODEL, D_FF), D_MODEL ** -0.5),
        "ffn_w_down": nrm(ks[7], (L, 2, D_FF, D_MODEL), D_FF ** -0.5),
        "w_in": nrm(ks[8], (L, D_MODEL, D_IN), D_MODEL ** -0.5),
        "w_out": nrm(ks[9], (L, D_MIX, D_MODEL), D_MIX ** -0.5),
        "gm_ln_g": 1.0 + nrm(ks[10], (L, GM_WIDTH), 0.05),
        "gm_w_s": nrm(ks[11], (L, GM_GROUPS, GM_CHUNK, GM_CHUNK), GM_CHUNK ** -0.5),
        "gm_b_s": 1.0 + nrm(ks[12], (L, GM_GROUPS, GM_CHUNK), 0.1),
        "da_lambda": nrm(ks[13], (L, 4, DA_QK_DIM), 0.1),
        "da_sub_g": 1.0 + nrm(ks[14], (L, DA_V_DIM), 0.05),
        "nsa_cmp_pe": nrm(ks[15], (L, 2, CMP_LEN, HEAD_DIM), 0.02),
        "nsa_cmp_w1": nrm(ks[16], (L, 2, CMP_LEN * HEAD_DIM, CMP_HIDDEN), (CMP_LEN * HEAD_DIM) ** -0.5),
        "nsa_cmp_w2": nrm(ks[17], (L, 2, CMP_HIDDEN, HEAD_DIM), CMP_HIDDEN ** -0.5),
        "final_g": 1.0 + nrm(ks[18], (D_MODEL,), 0.05),
    }

def first_block(x, c, w_ada, b_ada, norm_g, ffn_w_gate, ffn_w_up, ffn_w_down, w_in, w_out,
              gm_ln_g, gm_w_s, gm_b_s, da_lambda, da_sub_g, nsa_cmp_pe, nsa_cmp_w1, nsa_cmp_w2, final_g):
    c_act = jax.nn.silu(c)
    for l in range(DEPTH):
        mod = (c_act @ w_ada[l] + b_ada[l])[:, None, :]
        sh0, sc0, g0, sh1, sc1, g1, sh2, sc2, g2 = jnp.split(mod, N_MOD, axis=-1)
        lam_init = 0.8 - 0.6 * math.exp(-0.3 * l)
        h = _rmsnorm(x, norm_g[l, 0]) * (1.0 + sc0) + sh0
        x = x + 0.5 * g0 * _swiglu(h, ffn_w_gate[l, 0], ffn_w_up[l, 0], ffn_w_down[l, 0])
        h = _rmsnorm(x, norm_g[l, 1]) * (1.0 + sc1) + sh1
        x = x + g1 * _token_mix(h, w_in[l], w_out[l], gm_ln_g[l], gm_w_s[l], gm_b_s[l], da_lambda[l],
                                da_sub_g[l], nsa_cmp_pe[l], nsa_cmp_w1[l], nsa_cmp_w2[l], lam_init)
        h = _rmsnorm(x, norm_g[l, 2]) * (1.0 + sc2) + sh2
        x = x + 0.5 * g2 * _swiglu(h, ffn_w_gate[l, 1], ffn_w_up[l, 1], ffn_w_down[l, 1])
    return _rmsnorm(x, final_g)


DEPTH_2 = 1

D_MIX_2 = D_MODEL
W_CONF = D_MIX_2 // 4
W_POOL = D_MIX_2 // 4
W_SCONV = D_MIX_2 // 4
W_ATTN = D_MIX_2 - W_CONF - W_POOL - W_SCONV
CONF_WIDTH = 31
POOL_WINDOWS = (2, 4, 8, 16)
POOL_GROUP = W_POOL // len(POOL_WINDOWS)
SCONV_WIDTH = 3
ATTN_HEAD_DIM = 64
ATTN_HEADS = W_ATTN // ATTN_HEAD_DIM
ATTN_BLOCK = 128
SPLIT_SIZES = (W_CONF, W_CONF, W_POOL, W_SCONV, W_SCONV, W_SCONV, W_ATTN, W_ATTN, W_ATTN)
D_IN_2 = sum(SPLIT_SIZES)
PEER_HEADS = 8
PEER_NKEYS = 128
PEER_EXPERTS = PEER_NKEYS * PEER_NKEYS
PEER_DKEY = 256
PEER_TOPK = 16
PEER_CHUNK = 128
DEEPNORM_ALPHA = (2 * DEPTH_2) ** 0.25
DEEPNORM_BETA = (8 * DEPTH_2) ** -0.25
LN_EPS = 1e-5


def layer_norm(x, g, b):
    xf = x.astype(jnp.float32)
    mu = jnp.mean(xf, axis=-1, keepdims=True)
    xc = xf - mu
    var = jnp.mean(xc * xc, axis=-1, keepdims=True)
    return (xc * lax.rsqrt(var + LN_EPS) * g + b).astype(x.dtype)

def depthwise_causal_conv(x, w):
    k_width, ch = w.shape
    return lax.conv_general_dilated(
        x, w[:, None, :].astype(x.dtype), window_strides=(1,), padding=[(k_width - 1, 0)],
        dimension_numbers=("NWC", "WIO", "NWC"), feature_group_count=ch)

def conformer_conv(a_val, a_gate, conv_w, conv_b, norm_g, norm_b):
    u = a_val * jax.nn.sigmoid(a_gate)
    h = depthwise_causal_conv(u, conv_w) + conv_b
    return jax.nn.silu(layer_norm(h, norm_g, norm_b))

def multiscale_pool(p, pool_w, pool_scale):
    bn, s, _ = p.shape
    groups = p.reshape(bn, s, len(POOL_WINDOWS), POOL_GROUP)
    t = jnp.arange(s)
    outs = []
    for g, win in enumerate(POOL_WINDOWS):
        xg = groups[:, :, g, :].astype(jnp.float32)
        cs = jnp.cumsum(xg, axis=1)
        prev = jnp.pad(cs, ((0, 0), (win, 0), (0, 0)))[:, :s]
        count = jnp.minimum(t + 1, win).astype(jnp.float32)
        outs.append((cs - prev) / count[None, :, None] - xg)
    pooled = jnp.stack(outs, axis=2).astype(p.dtype)
    mixed = jnp.einsum("bsgc,gce->bsge", pooled, pool_w)
    return mixed.reshape(bn, s, W_POOL) * pool_scale

def stick_breaking_attention(q, k, v):
    bn, s, _ = q.shape
    nb = s // ATTN_BLOCK

    def heads(a):
        return a.reshape(bn, s, ATTN_HEADS, ATTN_HEAD_DIM).transpose(0, 2, 1, 3)

    q, k, v = heads(q), heads(k), heads(v)
    q_blocks = q.reshape(bn, ATTN_HEADS, nb, ATTN_BLOCK, ATTN_HEAD_DIM).transpose(2, 0, 1, 3, 4)
    k_pos = jnp.arange(s)
    scale = ATTN_HEAD_DIM ** -0.5

    def block(args):
        q_blk, blk = args
        z = jnp.einsum("bhqd,bhkd->bhqk", q_blk, k).astype(jnp.float32) * scale
        q_pos = blk * ATTN_BLOCK + jnp.arange(ATTN_BLOCK)
        causal = k_pos[None, :] < q_pos[:, None]
        log_stay = jnp.where(causal, jax.nn.log_sigmoid(-z), 0.0)
        cum = jnp.cumsum(log_stay, axis=-1)
        log_w = jax.nn.log_sigmoid(z) + (cum[..., -1:] - cum)
        w = jnp.where(causal, jnp.exp(log_w), 0.0)
        return jnp.einsum("bhqk,bhkd->bhqd", w.astype(v.dtype), v)

    out = lax.map(block, (q_blocks, jnp.arange(nb)))
    return out.transpose(1, 0, 3, 2, 4).reshape(bn, s, W_ATTN)

def token_mix(x, w_in, conv_a_w, conv_a_b, norm_a_g, norm_a_b, pool_w, pool_scale, conv_c_w, w_out):
    proj = jnp.einsum("bsd,de->bse", x, w_in)
    split_points = [int(i) for i in np.cumsum(SPLIT_SIZES)[:-1]]
    a_val, a_gate, p_in, c_h, c_gate_b, c_gate_c, q, k, v = jnp.split(proj, split_points, axis=-1)
    y_a = conformer_conv(a_val, a_gate, conv_a_w, conv_a_b, norm_a_g, norm_a_b)
    y_b = multiscale_pool(p_in, pool_w, pool_scale)
    y_c = c_gate_b * depthwise_causal_conv(c_gate_c * c_h, conv_c_w)
    y_d = stick_breaking_attention(q, k, v)
    y = jnp.concatenate([y_a, y_b, y_c, y_d], axis=-1)
    return jnp.einsum("bse,ed->bsd", y, w_out)

def peer_ffn(x, wq, sub_keys, u_tab, v_tab):
    bn, s, d = x.shape
    t = bn * s
    xf = x.reshape(t, d)
    q = (xf @ wq).reshape(t, PEER_HEADS, 2, PEER_DKEY // 2)
    scores = jnp.einsum("thpc,hpnc->thpn", q, sub_keys).astype(jnp.float32)
    s_top, i_top = lax.top_k(scores, PEER_TOPK)
    cand_s = (s_top[:, :, 0, :, None] + s_top[:, :, 1, None, :]).reshape(t, PEER_HEADS, PEER_TOPK * PEER_TOPK)
    cand_i = (i_top[:, :, 0, :, None] * PEER_NKEYS + i_top[:, :, 1, None, :]).reshape(t, PEER_HEADS, PEER_TOPK * PEER_TOPK)
    best_s, best_pos = lax.top_k(cand_s, PEER_TOPK)
    expert_idx = jnp.take_along_axis(cand_i, best_pos, axis=-1)
    gates = jax.nn.softmax(best_s, axis=-1)
    n_chunks = t // PEER_CHUNK

    def chunk(args):
        xc, ec, gc = args
        u = jnp.take(u_tab, ec, axis=0)
        act = jax.nn.gelu(jnp.einsum("cd,chkd->chk", xc, u).astype(jnp.float32)) * gc
        vv = jnp.take(v_tab, ec, axis=0)
        return jnp.einsum("chk,chkd->cd", act.astype(vv.dtype), vv)

    out = lax.map(chunk, (xf.reshape(n_chunks, PEER_CHUNK, d),
                          expert_idx.reshape(n_chunks, PEER_CHUNK, PEER_HEADS, PEER_TOPK),
                          gates.reshape(n_chunks, PEER_CHUNK, PEER_HEADS, PEER_TOPK)))
    return out.reshape(bn, s, d).astype(x.dtype)

def second_inputs(seed: int = 0) -> dict:
    key = jax.random.key(seed)
    ks = jax.random.split(key, 20)
    L = DEPTH_2

    def nrm(k, shape, scale):
        return jax.random.normal(k, shape, jnp.float32) * scale

    return {
        "x": nrm(ks[0], (BATCH, SEQ, D_MODEL), 1.0),
        "w_in": nrm(ks[1], (L, D_MODEL, D_IN_2), D_MODEL ** -0.5),
        "conv_a_w": nrm(ks[2], (L, CONF_WIDTH, W_CONF), CONF_WIDTH ** -0.5),
        "conv_a_b": nrm(ks[3], (L, W_CONF), 0.02),
        "norm_a_g": 1.0 + nrm(ks[4], (L, W_CONF), 0.02),
        "norm_a_b": nrm(ks[5], (L, W_CONF), 0.02),
        "pool_w": nrm(ks[6], (L, len(POOL_WINDOWS), POOL_GROUP, POOL_GROUP), POOL_GROUP ** -0.5),
        "pool_scale": 1.0 + nrm(ks[7], (L, W_POOL), 0.02),
        "conv_c_w": nrm(ks[8], (L, SCONV_WIDTH, W_SCONV), SCONV_WIDTH ** -0.5),
        "w_out": nrm(ks[9], (L, D_MIX_2, D_MODEL), D_MIX_2 ** -0.5 * DEEPNORM_BETA),
        "ln1_g": 1.0 + nrm(ks[10], (L, D_MODEL), 0.02),
        "ln1_b": nrm(ks[11], (L, D_MODEL), 0.02),
        "peer_wq": nrm(ks[12], (L, D_MODEL, PEER_HEADS * PEER_DKEY), D_MODEL ** -0.5),
        "peer_keys": nrm(ks[13], (L, PEER_HEADS, 2, PEER_NKEYS, PEER_DKEY // 2), (PEER_DKEY // 2) ** -0.5),
        "peer_u": nrm(ks[14], (L, PEER_EXPERTS, D_MODEL), D_MODEL ** -0.5),
        "peer_v": nrm(ks[15], (L, PEER_EXPERTS, D_MODEL), PEER_HEADS ** -0.5 * DEEPNORM_BETA),
        "ln2_g": 1.0 + nrm(ks[16], (L, D_MODEL), 0.02),
        "ln2_b": nrm(ks[17], (L, D_MODEL), 0.02),
    }

def second_block(x, w_in, conv_a_w, conv_a_b, norm_a_g, norm_a_b, pool_w, pool_scale, conv_c_w, w_out,
              ln1_g, ln1_b, peer_wq, peer_keys, peer_u, peer_v, ln2_g, ln2_b):
    for l in range(DEPTH_2):
        m = token_mix(x, w_in[l], conv_a_w[l], conv_a_b[l], norm_a_g[l], norm_a_b[l],
                      pool_w[l], pool_scale[l], conv_c_w[l], w_out[l])
        x = layer_norm(DEEPNORM_ALPHA * x + m, ln1_g[l], ln1_b[l])
        f = peer_ffn(x, peer_wq[l], peer_keys[l], peer_u[l], peer_v[l])
        x = layer_norm(DEEPNORM_ALPHA * x + f, ln2_g[l], ln2_b[l])
    return x


_first_inputs = second_inputs


def second_inputs(seed=0):
    import zlib

    import numpy as np

    out = dict(_first_inputs(seed))
    spreads = {}
    factors = {'conv_a_b': 6.54,
     'norm_a_g': 8.0,
     'norm_a_b': 8.0,
     'pool_scale': 7.699,
     'ln2_g': 2.855,
     'ln2_b': 2.874}
    for name, (base, spread) in spreads.items():
        noise = np.random.default_rng([zlib.crc32(name.encode()), seed]).standard_normal(out[name].shape)
        drawn = base * np.exp(spread * noise) if base else spread * noise
        out[name] = __import__('jax').numpy.asarray(drawn.astype(out[name].dtype))
    for name, factor in factors.items():
        out[name] = (out[name] * factor).astype(out[name].dtype)
    return out


_narrow_inputs = second_inputs


def second_inputs(seed=0):

    out = dict(_narrow_inputs(seed))
    wider = {'norm_a_g': 4.25, 'norm_a_b': 3.93, 'pool_scale': 3.59, 'ln2_g': 3.21, 'ln2_b': 3.21}
    for name, times in wider.items():
        mean = out[name].mean()
        out[name] = (mean + times * (out[name] - mean)).astype(out[name].dtype)
    return out


def setup_inputs(seed=0):
    out = dict(first_inputs(seed))
    for name, value in second_inputs(seed + 1).items():
        if name != "x":
            out[name + "_2"] = value
    return out


def reference(
    x, c, w_ada, b_ada, norm_g, ffn_w_gate, ffn_w_up, ffn_w_down, w_in, w_out, gm_ln_g, gm_w_s,
    gm_b_s, da_lambda, da_sub_g, nsa_cmp_pe, nsa_cmp_w1, nsa_cmp_w2, final_g, w_in_2,
    conv_a_w_2, conv_a_b_2, norm_a_g_2, norm_a_b_2, pool_w_2, pool_scale_2, conv_c_w_2, w_out_2,
    ln1_g_2, ln1_b_2, peer_wq_2, peer_keys_2, peer_u_2, peer_v_2, ln2_g_2, ln2_b_2,
):
    x = first_block(
        x, c, w_ada, b_ada, norm_g, ffn_w_gate, ffn_w_up, ffn_w_down, w_in, w_out, gm_ln_g,
        gm_w_s, gm_b_s, da_lambda, da_sub_g, nsa_cmp_pe, nsa_cmp_w1, nsa_cmp_w2, final_g,
    )
    return second_block(
        x, w_in_2, conv_a_w_2, conv_a_b_2, norm_a_g_2, norm_a_b_2, pool_w_2, pool_scale_2,
        conv_c_w_2, w_out_2, ln1_g_2, ln1_b_2, peer_wq_2, peer_keys_2, peer_u_2, peer_v_2,
        ln2_g_2, ln2_b_2,
    )


_drawn_inputs = setup_inputs


def setup_inputs(seed=0):
    import zlib

    import numpy as np

    out = dict(_drawn_inputs(seed))
    spreads = {}
    factors = {'gm_ln_g': 5.217, 'da_lambda': 8.0, 'da_sub_g': 4.984, 'nsa_cmp_pe': 28.253}
    for name, (base, spread) in spreads.items():
        noise = np.random.default_rng([zlib.crc32(name.encode()), seed]).standard_normal(out[name].shape)
        drawn = base * np.exp(spread * noise) if base else spread * noise
        out[name] = __import__('jax').numpy.asarray(drawn.astype(out[name].dtype))
    for name, factor in factors.items():
        out[name] = (out[name] * factor).astype(out[name].dtype)
    return out
```

```python
import math
from contextlib import ExitStack

import numpy as np
import concourse.bass as bass
from concourse import mybir

F32 = mybir.dt.float32
U32 = mybir.dt.uint32
F32R = mybir.dt.float32r
ALU = mybir.AluOpType
ACT = mybir.ActivationFunctionType
X = mybir.AxisListType.X

P = 128
D = 1024
S = 512
L = 2
KD = D // P
TT = S // P
FF = 2816
KF = FF // P
HD = 64
NMOD = 9
NC = (S - 32) // 16 + 1
EPS = 1e-6
LN_EPS = 1e-5
NEG = -1e30
ALPHA = 2 ** 0.25
KEYS = 128
TOP = 16
PH = 8
NSEL = PH * TOP

C_IDENT, C_ONES, C_BLK, C_MASK, C_ROTD, C_ROTN = 0, 128, 256, 384, 512, 640
C_CADD, C_CMUL, C_LAM, C_STRICT, C_BLK256, C_INVC, C_IOTA = 768, 892, 1016, 1020, 1148, 1276, 1308
C_ALL = 1324
C_COSD, C_SIND, C_COSN, C_SINN = 0, 512, 1024, 1536

P_BADA, P_NG, P_LNG, P_BS, P_SUBG, P_LAMV, P_PE, P_ALL = 0, 72, 96, 352, 608, 609, 737, 769
Q_CAW, Q_CAB, Q_NG, Q_NB, Q_PSC, Q_CCW, Q_L1G, Q_L1B, Q_FG, Q_ALL = 0, 62, 64, 66, 68, 70, 76, 84, 92, 100

GU, DQ, DK, NQ, KC, VC, KS, KW, NZ = 0, 2, 4, 6, 10, 12, 14, 15, 16
TG, TD, TVS, TVW, TGT, NTOK = 0, 256, 512, 640, 768, 792


class Chain:

    def __init__(self, eng, sem, passed=None):
        self.eng, self.sem, self.base, self.n, self.passed = eng, sem, 0, 0, passed

    def __call__(self, ins):
        ins.then_inc(self.sem, 1)
        self.n += 1
        self.eng.wait_ge(self.sem, self.base + self.n)
        if self.passed is not None:
            self.eng.sem_inc(self.passed, 1)

    def enter(self, i, per):
        self.outer, self.n, self.per = self.n, 0, per
        self.base = i * per + self.outer

    def leave(self, turns):
        assert self.n == self.per, (self.n, self.per)
        self.base, self.n = 0, self.outer + turns * self.per


def semaphores(nc, ctx, names):
    sems = {}
    for n in names.split():
        n, _, many = n.partition("*")
        own = [ctx.enter_context(nc.semaphore(f"{n}{k}" if many else n)) for k in range(int(many or 1))]
        sems[n] = own if many else own[0]
    return sems


def clear(nc, sems):
    with nc.Block() as block:
        @block.sync
        def _(sp):
            for own in sems.values():
                for s in own if isinstance(own, list) else [own]:
                    sp.sem_clear(s)


def load_constants(nc, T):
    with ExitStack() as ctx:
        M = semaphores(nc, ctx, "lc_loaded lc_silu")
        with nc.Block() as block:
            @block.sync
            def _(sp):
                sp.dma_start(T.const[:, :], T.d["const"]).then_inc(M["lc_loaded"], 16)
                sp.dma_start(T.xT[:, :, :], T.d["xT"]).then_inc(M["lc_loaded"], 16)
                sp.dma_start(T.crow[:, :], T.d["c"]).then_inc(M["lc_loaded"], 16)
                sp.dma_start(T.q1[:, :], T.d["q1"]).then_inc(M["lc_loaded"], 16)

            @block.vector
            def _(dve):
                nc.vector.memset(T.eps[:, 0:1], EPS)
                nc.vector.memset(T.eps[:, 1:2], LN_EPS)
                nc.vector.memset(T.zero[:, :], 0.0)

            @block.scalar
            def _(act):
                act.wait_ge(M["lc_loaded"], 64)
                nc.scalar.activation(T.crow[:, :], T.crow[:, :], ACT.Silu).then_inc(M["lc_silu"], 1)
                act.wait_ge(M["lc_silu"], 1)
        clear(nc, M)


def mod_dots(nc, T, sp, dve, M, wrow, prod, some, layer, col0, turns, per):
    RING = 3

    def load(i):
        for j in range(per // 2):
            sp.wait_ge(M["m_dot"], i * per + 2 * j + 2)
            sp.sem_inc(M["m_passed"], 1)
            sp.dma_start(wrow[:, j % RING], T.d["ada"][layer, i * (per // 2) + (col0 // 2 + j)]
                         ).then_inc(M["m_row"][j % RING], 16)

    def dots(i):
        for j in range(per // 2):
            dve.wait_ge(M["m_row"][j % RING], i * (16 * (per // 2 // RING)) + 16 * (j // RING) + 16)
            for h in range(2):
                dve.wait_ge(M["m_dot"], i * per + 2 * j + h + 2 * RING)
                nc.vector.tensor_tensor_reduce(prod[:, :], wrow[:, j % RING, h], T.crow[:, :], 1.0, 0.0,
                                               ALU.mult, ALU.add,
                                               some[:, 2 * j + h:2 * j + h + 1]).then_inc(M["m_dot"], 1)
        dve.wait_ge(M["m_dot"], i * per + per + 2 * RING)
        nc.vector.tensor_copy(T.raw[:, bass.ds(i * per + col0, per)], some[:, 0:per]).then_inc(M["m_raw"], 1)
        dve.wait_ge(M["m_raw"], i + 1)

    return load if sp is not None else dots


def first_modulation(nc, T):
    with ExitStack() as ctx:
        M = semaphores(nc, ctx, "m_row*3 m_dot m_raw m_passed")
        wrow = ctx.enter_context(nc.sbuf_tensor("m0_wrow", [P, 3, 2, D], F32))
        prod = ctx.enter_context(nc.sbuf_tensor("m0_prod", [P, D], F32))
        some = ctx.enter_context(nc.sbuf_tensor("m0_some", [P, 12], F32))
        with nc.Block() as block:
            @block.sync
            def _(sp):
                load = mod_dots(nc, T, sp, None, M, wrow, prod, some, 0, 0, 2, 12)
                with sp.Fori(0, 2) as i:
                    load(i)

            @block.vector
            def _(dve):
                dve.sem_inc(M["m_dot"], 6)
                dots = mod_dots(nc, T, None, dve, M, wrow, prod, some, 0, 0, 2, 12)
                with dve.Fori(0, 2) as i:
                    dots(i)
        clear(nc, M)


def modulation(nc, T, layer, chunks):
    with ExitStack() as ctx:
        M = semaphores(nc, ctx, "mo_par mo_chain mo_lam mo_exp")
        tag = str(chunks[0])
        prod = ctx.enter_context(nc.sbuf_tensor("mo_prod" + tag, [P, 32], F32))
        lt = ctx.enter_context(nc.sbuf_tensor("mo_lt" + tag, [P, 4], F32))
        with nc.Block() as block:
            @block.sync
            def _(sp):
                if 0 in chunks:
                    sp.dma_start(T.par[:, :], T.d["par"][layer]).then_inc(M["mo_par"], 16)

            @block.vector
            def _(dve):
                if 0 in chunks:
                    dve.wait_ge(M["mo_par"], 16)
                link = Chain(dve, M["mo_chain"])
                for n in chunks:
                    c = slice(24 * n, 24 * n + 24)
                    link(nc.vector.tensor_tensor(T.mod[:, c], T.raw[:, c], T.par[:, P_BADA + 24 * n:P_BADA + 24 * n + 24],
                                                 ALU.add))
                    link(nc.vector.scalar_tensor_tensor(
                        T.gain[:, 8 * n:8 * n + 8], T.mod[:, 24 * n + 8:24 * n + 16], 1.0,
                        T.par[:, P_NG + 8 * n:P_NG + 8 * n + 8], ALU.add, ALU.mult))
                    if n != 1:
                        link(nc.vector.tensor_scalar(T.mod[:, 24 * n + 16:24 * n + 24],
                                                     T.mod[:, 24 * n + 16:24 * n + 24], 0.5, None, ALU.mult))
                if 0 not in chunks:
                    return
                lv = T.par[:, P_LAMV:P_LAMV + 128]
                for m in range(2):
                    link(nc.vector.tensor_tensor_reduce(prod[:, 0:32], lv[:, 64 * m:64 * m + 32],
                                                        lv[:, 64 * m + 32:64 * m + 64], 1.0, 0.0,
                                                        ALU.mult, ALU.add, lt[:, m:m + 1]))
                nc.vector.memset(lt[:, 2:3], 0.0).then_inc(M["mo_lam"], 1)
                dve.wait_ge(M["mo_exp"], 1)
                link(nc.vector.tensor_tensor(lt[:, 2:3], lt[:, 0:1], lt[:, 1:2], ALU.subtract))
                link(nc.vector.tensor_tensor(T.lam[:, 0:1], lt[:, 2:3],
                                             T.const[:, bass.ds(layer * 2 + C_LAM, 1)], ALU.add))
                link(nc.vector.tensor_tensor(T.lam[:, 1:2], T.par[:, P_SUBG:P_SUBG + 1],
                                             T.const[:, bass.ds(layer * 2 + C_LAM + 1, 1)], ALU.mult))

            @block.scalar
            def _(act):
                if 0 in chunks:
                    act.wait_ge(M["mo_lam"], 1)
                    nc.scalar.activation(lt[:, 0:2], lt[:, 0:2], ACT.Exp).then_inc(M["mo_exp"], 1)
        clear(nc, M)


W_SEMS = "w_in*4 w_hi w_lo w_mm "


class Weights:
    def __init__(self, nc, ctx, M, tag, kt, w_of):
        self.nc, self.M, self.kt, self.w_of = nc, M, kt, w_of
        self.raw = ctx.enter_context(nc.sbuf_tensor("wraw" + tag, [P, 4, kt * P], F32))
        self.hi = ctx.enter_context(nc.sbuf_tensor("whi" + tag, [P, 2, kt * P], F32R))
        self.lo = ctx.enter_context(nc.sbuf_tensor("wlo" + tag, [P, 2, kt * P], F32R))

    def load(self, sp, i, j):
        sp.wait_ge(self.M["w_lo"], i * 4 + j + 1)
        sp.dma_start(self.raw[:, j], self.w_of(i, j)).then_inc(self.M["w_in"][j], 16)

    def round(self, act, i, j):
        act.wait_ge(self.M["w_in"][j], i * 16 + 16)
        act.wait_ge(self.M["w_mm"], i * 4 + j + 1)
        self.nc.scalar.activation(self.hi[:, j % 2], self.raw[:, j], ACT.Copy).then_inc(self.M["w_hi"], 1)

    def rest(self, pool, i, j):
        pool.wait_ge(self.M["w_hi"], i * 4 + j + 1)
        self.nc.gpsimd.tensor_tensor(self.lo[:, j % 2], self.raw[:, j], self.hi[:, j % 2].bitcast(F32),
                                     ALU.subtract).then_inc(self.M["w_lo"], 1)

    def times(self, pe, i, j, out, xh, xl, k0=0, first=True, last=True):
        pe.wait_ge(self.M["w_lo"], i * 4 + j + 5)
        hi, lo = self.hi[:, j % 2], self.lo[:, j % 2]
        for k in range(self.kt):
            w = slice(k * P, (k + 1) * P)
            self.nc.tensor.matmul(out, hi[:, w], xh[:, k0 + k], start=first and k == 0, stop=False)
            self.nc.tensor.matmul(out, hi[:, w], xl[:, k0 + k], start=False, stop=False)
            mm = self.nc.tensor.matmul(out, lo[:, w], xh[:, k0 + k], start=False, stop=last and k == self.kt - 1)
        mm.then_inc(self.M["w_mm"], 1)


def square_sums(nc, T, act, pe, M, sq, ps, rstd):
    for k in range(KD):
        if act is not None:
            if k >= 2:
                act.wait_ge(M["n_sum"], k - 1)
            nc.scalar.activation(sq[:, k % 2], T.xT[:, k], ACT.Square).then_inc(M["n_sq"], 1)
        if pe is not None:
            pe.wait_ge(M["n_sq"], k + 1)
            nc.tensor.matmul(ps, T.const[:, C_ONES:C_ONES + P], sq[:, k % 2],
                             start=k == 0, stop=k == KD - 1).then_inc(M["n_sum"], 1)
    if act is not None:
        act.wait_ge(M["n_sum"], KD)
        nc.scalar.activation(rstd, ps, ACT.Sqrt, bias=T.eps[:, 0:1]).then_inc(M["n_root"], 1)


N_SEMS = "n_sq n_sum n_root n_rstd n_t n_h n_hi n_lo "


def norm_split(nc, T, M, rstd, tmp, h, hi, lo, gain, shift, act=None, dve=None, pool=None):
    slots = h.shape[1]
    if dve is not None:
        dve.wait_ge(M["n_root"], 1)
        nc.vector.reciprocal(rstd, rstd).then_inc(M["n_rstd"], 1)
        dve.wait_ge(M["n_rstd"], 1)
    for k in range(KD + 1):
        if dve is not None:
            if k < KD:
                if k >= 2:
                    dve.wait_ge(M["n_h"], k - 1)
                nc.vector.tensor_tensor(tmp[:, k % 2], T.xT[:, k], rstd, ALU.mult).then_inc(M["n_t"], 1)
            if k:
                dve.wait_ge(M["n_h"], k)
                nc.vector.tensor_copy(hi[:, k - 1], h[:, (k - 1) % slots]).then_inc(M["n_hi"], 1)
        if act is not None and k < KD:
            act.wait_ge(M["n_t"], k + 1)
            if slots == 2 and k >= 2:
                act.wait_ge(M["n_lo"], k - 1)
            nc.scalar.activation(h[:, k % slots], tmp[:, k % 2], ACT.Identity, scale=gain[:, k:k + 1],
                                 bias=shift[:, k:k + 1]).then_inc(M["n_h"], 1)
        if pool is not None and k < KD:
            pool.wait_ge(M["n_hi"], k + 1)
            nc.gpsimd.tensor_tensor(lo[:, k], h[:, k % slots], hi[:, k].bitcast(F32),
                                    ALU.subtract).then_inc(M["n_lo"], 1)


def split(nc, M, x, hi, lo, act=None, pool=None, n=KD):
    for k in range(n):
        if act is not None:
            nc.scalar.activation(hi[:, k], x[:, k], ACT.Copy).then_inc(M["x_hi"], 1)
        if pool is not None:
            pool.wait_ge(M["x_hi"], k + 1)
            nc.gpsimd.tensor_tensor(lo[:, k], x[:, k], hi[:, k].bitcast(F32), ALU.subtract).then_inc(M["x_lo"], 1)


def ffn_up(nc, T, layer, which, ah, al):
    m = 2 * which
    with ExitStack() as ctx:
        M = semaphores(nc, ctx, N_SEMS + W_SEMS + "f_silu f_prod f_ahi f_act")
        sb = lambda n, s, t=F32: ctx.enter_context(nc.sbuf_tensor(n + str(which), s, t))
        hh = sb("f_hh", [P, KD, S], F32R)
        hl = sb("f_hl", [P, KD, S], F32R)
        rstd = sb("f_rstd", [P, S])
        sg = sb("f_sg", [P, 2, S])
        a32 = sb("f_a32", [P, 2, S])
        h = sb("f_h", [P, 2, S])
        W = Weights(nc, ctx, M, "u" + str(which), KD,
                    lambda i, j: T.d["gu"][layer * 2 + which, i * 2 + j // 2, j % 2])
        psN = ctx.enter_context(nc.psum_tensor("f_psN" + str(which), [P, S], F32))
        ps = ctx.enter_context(nc.psum_tensor("f_ps" + str(which), [P, 4, S], F32))
        norm = (nc, T, M, rstd[:, :], sg, h, hh, hl, T.gain[:, 8 * m:8 * m + 8], T.mod[:, 24 * m:24 * m + 8])
        with nc.Block() as block:
            @block.sync
            def _(sp):
                with sp.Fori(0, KF // 2) as i:
                    for j in range(4):
                        W.load(sp, i, j)

            @block.gpsimd
            def _(pool):
                pool.sem_inc(M["w_lo"], 4)
                norm_split(*norm, pool=pool)
                with pool.Fori(0, KF // 2) as i:
                    for j in range(4):
                        W.rest(pool, i, j)

            @block.scalar
            def _(act):
                square_sums(nc, T, act, None, M, a32, psN[:, :], rstd[:, :])
                norm_split(*norm, act=act)

                def silu(i, g):
                    act.wait_ge(M["w_mm"], i * 4 + 2 * g + 3)
                    act.wait_ge(M["f_prod"], i * 2 + g + 1)
                    nc.scalar.activation(sg[:, g], ps[:, 2 * g], ACT.Silu).then_inc(M["f_silu"], 1)

                with act.Fori(0, KF // 2) as i:
                    W.round(act, i, 0)
                    W.round(act, i, 1)
                    W.round(act, i, 2)
                    silu(i, 0)
                    W.round(act, i, 3)
                    silu(i, 1)

            @block.tensor
            def _(pe):
                pe.sem_inc(M["w_mm"], 2)
                square_sums(nc, T, None, pe, M, a32, psN[:, :], None)
                pe.wait_ge(M["n_lo"], KD)
                with pe.Fori(0, KF // 2) as i:
                    for j in range(4):
                        pe.wait_ge(M["f_prod"], i * 2 + j // 2 + 1)
                        W.times(pe, i, j, ps[:, j], hh, hl)

            @block.vector
            def _(dve):
                dve.sem_inc(M["f_prod"], 2)
                norm_split(*norm, dve=dve)
                with dve.Fori(0, KF // 2) as i:
                    for g in range(2):
                        dve.wait_ge(M["f_silu"], i * 2 + g + 1)
                        dve.wait_ge(M["w_mm"], i * 4 + 2 * g + 4)
                        nc.vector.tensor_tensor(a32[:, g], sg[:, g], ps[:, 2 * g + 1], ALU.mult).then_inc(M["f_prod"], 1)
                        dve.wait_ge(M["f_prod"], i * 2 + g + 3)
                        nc.vector.tensor_copy(ah[:, i * 2 + g], a32[:, g]).then_inc(M["f_ahi"], 1)
                        dve.wait_ge(M["f_ahi"], i * 2 + g + 1)
                        nc.vector.tensor_tensor(al[:, i * 2 + g], a32[:, g], ah[:, i * 2 + g].bitcast(F32),
                                                ALU.subtract).then_inc(M["f_act"], 1)
        clear(nc, M)


def ffn_down(nc, T, layer, which, ah, al):
    gate = T.mod[:, 48 * which + 16:48 * which + 24]
    H = KF // 2
    per = 6 if which else 12
    mod_layer, col0 = (1 - layer, 0) if which else (layer, 24)
    with ExitStack() as ctx:
        M = semaphores(nc, ctx, W_SEMS + "f_res m_row*3 m_dot m_raw m_passed")
        sb = lambda n, s, t=F32: ctx.enter_context(nc.sbuf_tensor(n + str(which), s, t))
        wrow = sb("m_wrow", [P, 3, 2, D])
        prod = sb("m_prod", [P, D])
        some = sb("m_some", [P, 12])
        W = Weights(nc, ctx, M, "d" + str(which), H,
                    lambda i, j: T.d["dn"][layer * 2 + which, i * 2 + j // 2][:, (j % 2) * H * P:(j % 2 + 1) * H * P])
        ps = ctx.enter_context(nc.psum_tensor("f_psD" + str(which), [P, 2, S], F32))
        with nc.Block() as block:
            @block.sync
            def _(sp):
                rows = mod_dots(nc, T, sp, None, M, wrow, prod, some, mod_layer, col0, KD // 2, per)
                with sp.Fori(0, KD // 2) as i:
                    for j in range(4):
                        W.load(sp, i, j)
                    rows(i)

            @block.gpsimd
            def _(pool):
                pool.sem_inc(M["w_lo"], 4)
                with pool.Fori(0, KD // 2) as i:
                    for j in range(4):
                        W.rest(pool, i, j)

            @block.scalar
            def _(act):
                with act.Fori(0, KD // 2) as i:
                    for j in range(4):
                        W.round(act, i, j)

            @block.tensor
            def _(pe):
                pe.sem_inc(M["w_mm"], 2)
                with pe.Fori(0, KD // 2) as i:
                    for j in range(4):
                        pe.wait_ge(M["f_res"], i * 2 + j // 2 + 1)
                        W.times(pe, i, j, ps[:, j // 2], ah, al, k0=(j % 2) * H, first=j % 2 == 0, last=j % 2 == 1)

            @block.vector
            def _(dve):
                dve.sem_inc(M["f_res"], 2)
                dve.sem_inc(M["m_dot"], 6)
                dots = mod_dots(nc, T, None, dve, M, wrow, prod, some, mod_layer, col0, KD // 2, per)
                with dve.Fori(0, KD // 2) as i:
                    dots(i)
                    for g in range(2):
                        dve.wait_ge(M["w_mm"], i * 4 + 2 * g + 4)
                        x = T.xT[:, i * 2 + g]
                        nc.vector.scalar_tensor_tensor(x, ps[:, g], gate[:, bass.ds(i * 2 + g, 1)], x,
                                                       ALU.mult, ALU.add).then_inc(M["f_res"], 1)
        clear(nc, M)


def ffn(nc, T, layer, which):
    with ExitStack() as ctx:
        ah = ctx.enter_context(nc.sbuf_tensor("f_ah" + str(which), [P, KF, S], F32R))
        al = ctx.enter_context(nc.sbuf_tensor("f_al" + str(which), [P, KF, S], F32R))
        ffn_up(nc, T, layer, which, ah, al)
        ffn_down(nc, T, layer, which, ah, al)


def proj(nc, T, layer):
    with ExitStack() as ctx:
        M = semaphores(nc, ctx, N_SEMS + W_SEMS + "p_rope p_wt p_out p_tmm p_tout")
        sb = lambda n, s, t=F32: ctx.enter_context(nc.sbuf_tensor(n, s, t))
        h = sb("p_h", [P, KD, S])
        hh = sb("p_hh", [P, KD, S], F32R)
        hl = sb("p_hl", [P, KD, S], F32R)
        tmp = sb("p_tmp", [P, 2, S])
        rstd = sb("p_rstd", [P, S])
        wt = sb("p_wt", [P, KD, NTOK])
        W = Weights(nc, ctx, M, "p", KD, lambda i, j: T.d["win"][layer, i * 4 + j])
        psN = ctx.enter_context(nc.psum_tensor("p_psN", [P, S], F32))
        psZ = ctx.enter_context(nc.psum_tensor("p_psZ", [P, 4, S], F32))
        psT = ctx.enter_context(nc.psum_tensor("p_psT", [P, 2, S], F32))
        chunks = ((0, 512), (512, NTOK - 512))
        norm = (nc, T, M, rstd[:, :], tmp, h, hh, hl, T.gain[:, 8:16], T.mod[:, 24:32])
        with nc.Block() as block:
            @block.sync
            def _(sp):
                for j in range(4):
                    W.load(sp, 0, j)
                sp.dma_start(wt[:, :, :], T.d["wtok"][layer]).then_inc(M["p_wt"], 16)
                sp.dma_start(T.rope[:, :], T.d["rope"]).then_inc(M["p_rope"], 16)
                with sp.Fori(1, NZ // 4) as i:
                    for j in range(4):
                        W.load(sp, i, j)
                sp.wait_ge(M["p_rope"], 16)

            @block.gpsimd
            def _(pool):
                pool.sem_inc(M["w_lo"], 4)
                norm_split(*norm, pool=pool)
                with pool.Fori(0, NZ // 4) as i:
                    for j in range(4):
                        W.rest(pool, i, j)

            @block.scalar
            def _(act):
                square_sums(nc, T, act, None, M, h[:, 0:2], psN[:, :], rstd[:, :])
                norm_split(*norm, act=act)
                with act.Fori(0, NZ // 4) as i:
                    for j in range(4):
                        W.round(act, i, j)

            @block.tensor
            def _(pe):
                pe.sem_inc(M["w_mm"], 2)
                square_sums(nc, T, None, pe, M, h[:, 0:2], psN[:, :], None)
                pe.wait_ge(M["n_lo"], KD)
                with pe.Fori(0, NZ // 4) as i:
                    for j in range(4):
                        pe.wait_ge(M["p_out"], i * 4 + j + 1)
                        W.times(pe, i, j, psZ[:, j], hh, hl)
                pe.wait_ge(M["p_wt"], 16)
                for t in range(TT):
                    for c, (c0, cn) in enumerate(chunks):
                        if t:
                            pe.wait_ge(M["p_tout"], 2 * (t - 1) + c + 1)
                        for k in range(KD):
                            mm = nc.tensor.matmul(psT[:, c, 0:cn], h[:, k, t * P:(t + 1) * P],
                                                  wt[:, k, c0:c0 + cn], start=k == 0, stop=k == KD - 1)
                        mm.then_inc(M["p_tmm"], 1)

            @block.vector
            def _(dve):
                dve.sem_inc(M["p_out"], 4)
                norm_split(*norm, dve=dve)
                with dve.Fori(0, NZ // 4) as i:
                    for j in range(4):
                        dve.wait_ge(M["w_mm"], i * 4 + j + 3)
                        nc.vector.tensor_copy(T.z[:, i * 4 + j], psZ[:, j]).then_inc(M["p_out"], 1)
                for t in range(TT):
                    for c, (c0, cn) in enumerate(chunks):
                        dve.wait_ge(M["p_tmm"], 2 * t + c + 1)
                        nc.vector.tensor_copy(T.tok[:, t, c0:c0 + cn], psT[:, c, 0:cn]).then_inc(M["p_tout"], 1)
        clear(nc, M)


def rope_gate_cmp(nc, T, layer):
    NR = 10
    with ExitStack() as ctx:
        M = semaphores(nc, ctx, "r_w r_rot r_rope r_ch r_var r_root r_tri r_vn r_gelu r_v r_sg r_sgo r_sig "
                          "c_pe c_mm1 c_silu c_mm2 c_k c_rot c_fin c_ch")
        sb = lambda n, s: ctx.enter_context(nc.sbuf_tensor(n, s, F32))
        t1 = sb("r_t1", [P, 2, S])
        wsT = sb("r_wsT", [P, 4, P])
        st = sb("r_st", [P, 3, 16])
        sqv = sb("r_sqv", [P, TT, 256])
        w1 = sb("c_w1", [P, 2, 16, 256])
        w2 = sb("c_w2", [P, 2, 2, HD])
        w2d = sb("c_w2d", [P, 2, 2 * HD])
        blk = sb("c_blk", [P, 2, 16, 2, NC])
        hid = sb("c_hid", [P, 2, 2, 2, NC])
        kr = sb("c_kr", [P, NC])
        kt = sb("c_kt", [P, 2, NC])
        psR = ctx.enter_context(nc.psum_tensor("r_psR", [P, 2, S], F32))
        psS = ctx.enter_context(nc.psum_tensor("r_psS", [P, 2, S], F32))
        psH = ctx.enter_context(nc.psum_tensor("c_psH", [P, 2, 2 * NC], F32))
        psK = ctx.enter_context(nc.psum_tensor("c_psK", [P, 4, P], F32))
        roped = [DQ, DQ + 1, DK, DK + 1, NQ, NQ + 1, NQ + 2, NQ + 3, KS, KW]
        v = T.tok[:, :, TG:TG + 256]
        with nc.Block() as block:
            @block.sync
            def _(sp):
                sp.dma_start(wsT[:, :, :], T.d["ws"][layer]).then_inc(M["r_w"], 16)
                sp.dma_start(w1[:, :, :, :], T.d["w1"][layer]).then_inc(M["r_w"], 16)
                sp.dma_start(w2[:, :, :, :], T.d["w2"][layer]).then_inc(M["r_w"], 16)
                sp.dma_start(w2d[:, :, :], T.d["w2d"][layer]).then_inc(M["r_w"], 16)

            @block.gpsimd
            def _(pool):
                pool.wait_ge(M["r_w"], 64)
                nc.gpsimd.affine_select(out=wsT[:, :, :], in_=wsT[:, :, :], compare_op=ALU.is_ge, fill=0.0,
                                        base=0, pattern=[[0, 4], [1, P]], channel_multiplier=-1).then_inc(M["r_tri"], 1)
                pool.wait_ge(M["r_tri"], 1)
                made = 0
                for kv, z in ((0, KC), (1, VC)):
                    for g in range(2):
                        src = T.z[:, z + g, :].rearrange("p (c l two) -> p l c two", two=2, l=8)
                        for par in range(2):
                            rows = slice(64 * par, 64 * par + 64)
                            for lo in range(2):
                                if made:
                                    pool.wait_ge(M["c_pe"], made)
                                made += 1
                                col = P_PE + 16 * kv + 8 * lo
                                pos = T.par[rows, col:col + 8].unsqueeze(2).to_broadcast([64, 8, NC])
                                nc.gpsimd.tensor_tensor(blk[rows, kv, 8 * lo:8 * lo + 8, g, :],
                                                        src[rows, :, lo:lo + NC, par], pos,
                                                        ALU.add).then_inc(M["c_pe"], 1)

            @block.scalar
            def _(act):
                nc.scalar.activation(v, v, ACT.Gelu_apprx_tanh).then_inc(M["r_gelu"], 1)
                nc.scalar.activation(T.z[:, GU:GU + 2], T.z[:, GU:GU + 2], ACT.Gelu_apprx_tanh).then_inc(M["r_gelu"], 1)
                nc.scalar.activation(T.tok[:, :, TGT:TGT + 24], T.tok[:, :, TGT:TGT + 24],
                                     ACT.Sigmoid).then_inc(M["r_sig"], 1)
                act.wait_ge(M["r_var"], 1)
                nc.scalar.activation(st[:, 1], st[:, 1], ACT.Sqrt).then_inc(M["r_root"], 1)
                for kv in range(2):
                    act.wait_ge(M["c_mm1"], kv + 1)
                    nc.scalar.activation(hid[:, kv].rearrange("p a g c -> p (a g c)"),
                                         psH[:, :, :].rearrange("p a c -> p (a c)"), ACT.Silu).then_inc(M["c_silu"], 1)

            @block.tensor
            def _(pe):
                pe.wait_ge(M["r_w"], 64)
                for n, z in enumerate(roped):
                    if n >= 2:
                        pe.wait_ge(M["r_rope"], n - 1)
                    r = C_ROTD if n < 4 else C_ROTN
                    nc.tensor.matmul(psR[:, n % 2], T.const[:, r:r + P], T.z[:, z], start=True,
                                     stop=True).then_inc(M["r_rot"], 1)
                pe.wait_ge(M["c_pe"], 16)
                for kv in range(2):
                    if kv:
                        pe.wait_ge(M["c_silu"], 1)
                    for a in range(2):
                        for l in range(16):
                            mm = nc.tensor.matmul(psH[:, a], w1[:, kv, l, a * P:(a + 1) * P],
                                                  blk[:, kv, l].rearrange("p g c -> p (g c)"),
                                                  start=l == 0, stop=l == 15)
                    mm.then_inc(M["c_mm1"], 1)
                pe.wait_ge(M["c_silu"], 2)
                for g in range(2):
                    for a in range(2):
                        nc.tensor.matmul(psK[:, g, 0:NC], w2d[:, a], hid[:, 0, a, g], start=a == 0, stop=a == 1)
                for g in range(2):
                    for a in range(2):
                        mm = nc.tensor.matmul(psK[0:NC, 2 + g, 0:HD], hid[:, 1, a, g], w2[:, 1, a],
                                              start=a == 0, stop=a == 1)
                mm.then_inc(M["c_mm2"], 1)
                pe.wait_ge(M["c_k"], 3)
                nc.tensor.matmul(psH[:, 0, 0:NC], T.const[:, C_ROTN:C_ROTN + P], kr[:, :], start=True,
                                 stop=True).then_inc(M["c_rot"], 1)
                pe.wait_ge(M["r_tri"], 1)
                pe.wait_ge(M["r_vn"], 1)
                for t in range(TT):
                    for g in range(4):
                        mm = nc.tensor.matmul(psS[64 * (g % 2):64 * (g % 2) + 64, g // 2, t * P:(t + 1) * P],
                                              T.tok[:, t, TG + 64 * g:TG + 64 * g + 64], wsT[:, g],
                                              start=True, stop=True)
                mm.then_inc(M["r_sg"], 1)

            @block.vector
            def _(dve):
                link = Chain(dve, M["r_ch"])
                for n, z in enumerate(roped):
                    cos, sin = (C_COSD, C_SIND) if n < 4 else (C_COSN, C_SINN)
                    dve.wait_ge(M["r_rot"], n + 1)
                    link(nc.vector.tensor_tensor(t1[:, n % 2], psR[:, n % 2], T.rope[:, sin:sin + S], ALU.mult))
                    link(nc.vector.tensor_tensor(T.z[:, z], T.z[:, z], T.rope[:, cos:cos + S], ALU.mult))
                    nc.vector.tensor_tensor(T.z[:, z], T.z[:, z], t1[:, n % 2], ALU.add).then_inc(M["r_rope"], 1)
                dve.wait_ge(M["r_gelu"], 2)
                v4 = v.rearrange("p t (g d) -> p t g d", g=4)
                mu = st[:, 0].rearrange("p (t g) -> p t g", t=TT)
                va = st[:, 1].rearrange("p (t g) -> p t g", t=TT)
                q4 = sqv[:, :, :].rearrange("p t (g d) -> p t g d", g=4)
                for t in range(TT):
                    link(nc.vector.tensor_reduce(mu[:, t], v4[:, t], X, ALU.add))
                link(nc.vector.tensor_scalar(st[:, 0], st[:, 0], 1.0 / HD, None, ALU.mult))
                for t in range(TT):
                    link(nc.vector.tensor_tensor(v4[:, t], v4[:, t], mu[:, t].unsqueeze(2).to_broadcast([P, 4, HD]),
                                                 ALU.subtract))
                    link(nc.vector.tensor_tensor(q4[:, t], v4[:, t], v4[:, t], ALU.mult))
                    link(nc.vector.tensor_reduce(va[:, t], q4[:, t], X, ALU.add))
                nc.vector.tensor_scalar(st[:, 1], st[:, 1], 1.0 / HD, EPS, ALU.mult, ALU.add).then_inc(M["r_var"], 1)
                dve.wait_ge(M["r_root"], 1)
                link(nc.vector.reciprocal(st[:, 2], st[:, 1]))
                rs = st[:, 2].rearrange("p (t g) -> p t g", t=TT)
                lng = T.par[:, P_LNG:P_LNG + 256].rearrange("p (g d) -> p g d", g=4)
                for t in range(TT):
                    link(nc.vector.tensor_tensor(v4[:, t], v4[:, t], rs[:, t].unsqueeze(2).to_broadcast([P, 4, HD]),
                                                 ALU.mult))
                    ins = nc.vector.tensor_tensor(v4[:, t], v4[:, t], lng, ALU.mult)
                    if t < TT - 1:
                        link(ins)
                ins.then_inc(M["r_vn"], 1)
                dve.wait_ge(M["c_mm2"], 1)
                nc.vector.tensor_copy(kr[0:64, :], psK[0:64, 0, 0:NC]).then_inc(M["c_k"], 1)
                nc.vector.tensor_copy(kr[64:128, :], psK[64:128, 1, 0:NC]).then_inc(M["c_k"], 1)
                nc.vector.tensor_copy(T.vcmp[0:NC, :, :], psK[0:NC, 2:4, 0:HD]).then_inc(M["c_k"], 1)
                dve.wait_ge(M["c_rot"], 1)
                dve.wait_ge(M["c_k"], 3)
                ends = slice(31, 31 + 16 * (NC - 1) + 1, 16)
                cosn = T.rope[:, C_COSN:C_COSN + S]
                sinn = T.rope[:, C_SINN:C_SINN + S]
                link(nc.vector.tensor_tensor(kt[:, 0], psH[:, 0, 0:NC], sinn[:, ends], ALU.mult))
                link(nc.vector.tensor_tensor(kt[:, 1], kr[:, :], cosn[:, ends], ALU.mult))
                link(nc.vector.tensor_tensor(T.kcmp[:, :], kt[:, 0], kt[:, 1], ALU.add))
                dve.wait_ge(M["r_sg"], 1)
                for a in range(2):
                    b = T.par[:, P_BS + a * P:P_BS + (a + 1) * P]
                    s4 = t1[:, a].rearrange("p (n t) -> p n t", n=TT)
                    link(nc.vector.tensor_tensor(s4, psS[:, a].rearrange("p (n t) -> p n t", n=TT),
                                                 b.unsqueeze(1).to_broadcast([P, TT, P]), ALU.add))
                    link(nc.vector.tensor_tensor(T.y[:, a], T.z[:, GU + a], t1[:, a], ALU.mult))
        clear(nc, M)


def soft_attention(nc, T, layer, kind):
    da = kind == "da"
    TILES = 2 if da else 4
    ST = 3 if da else 1
    scale = 32 ** -0.5 if da else 64 ** -0.5
    NP_ = 1 if da else 2
    with ExitStack() as ctx:
        M = semaphores(nc, ctx, "a_st a_s a_nm a_e a_pr a_ch a_t a_te a_pv a_o a_cs a_cm a_ce a_cp a_ct a_cte")
        sb = lambda n, s: ctx.enter_context(nc.sbuf_tensor(n, s, F32))
        qs = sb("a_q" + kind, [P, S])
        ks = sb("a_k" + kind, [P, 2, S])
        vs = sb("a_v" + kind, [P, 2, TT, 2, HD])
        pb = sb("a_p" + kind, [P, 2, 2, S])
        PT = sb("a_pt" + kind, [P, 2, NP_, TT, S])
        mx = sb("a_mx" + kind, [P, 2, 2])
        nm = sb("a_nm" + kind, [P, 2, 2])
        sm = sb("a_sm" + kind, [P, 2, 2])
        rc = sb("a_rc" + kind, [P, 2, 2])
        cs = sb("a_cs" + kind, [P, TT, NC])
        cst = sb("a_cst" + kind, [P, 3, TT])
        ctp = sb("a_ctp" + kind, [NC, 2, S])
        oT = sb("a_o" + kind, [P, 2, S])
        psS = ctx.enter_context(nc.psum_tensor("a_psS" + kind, [P, 2, 2, S], F32))
        psT = ctx.enter_context(nc.psum_tensor("a_psT" + kind, [P, 2, S], F32))
        psO = ctx.enter_context(nc.psum_tensor("a_psO" + kind, [P, S], F32))
        psC = ctx.enter_context(nc.psum_tensor("a_psC" + kind, [P, S], F32))
        U = 2 * TT
        units = [(r, i) for r in range(2) for i in range(TT)]
        mask = T.const[:, C_MASK:C_MASK + P]
        with nc.Block() as block:
            @block.gpsimd
            def _(pool):
                pool.sem_inc(M["a_st"], 1)
                with pool.Fori(0, TILES) as t:
                    pool.wait_ge(M["a_pv"], t * 2 + 1)
                    pool.wait_ge(M["a_st"], t * ST + 1)
                    if da:
                        nc.gpsimd.tensor_copy(qs[:, :], T.z[:, t + DQ]).then_inc(M["a_st"], 1)
                        pool.wait_ge(M["a_st"], t * ST + 2)
                        nc.gpsimd.tensor_copy(ks[:, 0], T.z[:, t + DK]).then_inc(M["a_st"], 1)
                        pool.wait_ge(M["a_st"], t * ST + 2 + 1)
                        nc.gpsimd.tensor_copy(vs[:, 0].rearrange("p t r d -> p t (r d)"),
                                              T.tok[:, :, bass.ds(t * P + TD, P)]).then_inc(M["a_st"], 1)
                    else:
                        nc.gpsimd.tensor_copy(qs[:, :], T.z[:, t + NQ]).then_inc(M["a_st"], 1)

            @block.tensor
            def _(pe):
                pe.sem_inc(M["a_pv"], 1)
                pe.sem_inc(M["a_t"], 1)
                pe.sem_inc(M["a_ct"], 1)
                with pe.Fori(0, TILES) as t:
                    pe.wait_ge(M["a_st"], t * ST + ST + 1)

                    def cmp_scores(r):
                        if r:
                            pe.wait_ge(M["a_cte"], t * 2 + r + 1)
                        else:
                            pe.wait_ge(M["a_cte"], t * 2 + 1)
                        for i in range(TT):
                            mm = nc.tensor.matmul(psC[:, 32 * i:32 * i + NC],
                                                  qs[64 * r:64 * r + 64, i * P:(i + 1) * P],
                                                  T.kcmp[64 * r:64 * r + 64, :], start=True, stop=True)
                        mm.then_inc(M["a_cs"], 1)

                    def scores(u):
                        r, i = units[u]
                        pe.wait_ge(M["a_e"], t * 2 * U + (2 * (u - 1) if u >= 2 else 0) + 1)
                        n = P * (i + 1)
                        for m in range(2):
                            if da:
                                p0 = 64 * r + 32 * m
                                lhs, rhs = qs[p0:p0 + 32, i * P:(i + 1) * P], ks[p0:p0 + 32, 0, 0:n]
                                tp = (p0, 0)
                            else:
                                p0 = 64 * r
                                lhs = qs[p0:p0 + 64, i * P:(i + 1) * P]
                                rhs = T.z[p0:p0 + 64, (KS, KW)[m], 0:n]
                                tp = (p0, 0)
                            mm = nc.tensor.matmul(psS[:, u % 2, m, 0:n], lhs, rhs, start=True, stop=True,
                                                  tile_position=tp)
                        mm.then_inc(M["a_s"], 1)

                    def turn_probs(u):
                        r, i = units[u]
                        pe.wait_ge(M["a_pr"], t * U + u + 1)
                        for b in range(NP_):
                            n = NP_ * u + b
                            if n >= 2:
                                pe.wait_ge(M["a_te"], t * NP_ * U + n - 1 + 1)
                            else:
                                pe.wait_ge(M["a_te"], t * NP_ * U + 1)
                            for k in range(i + 1):
                                mm = nc.tensor.transpose(psT[:, n % 2, k * P:(k + 1) * P],
                                                         pb[:, u % 2, b, k * P:(k + 1) * P],
                                                         T.const[:, C_IDENT:C_IDENT + P])
                            mm.then_inc(M["a_t"], 1)

                    def cmp_turn(r):
                        pe.wait_ge(M["a_cp"], t * 2 + r + 1)
                        for i in range(TT):
                            mm = nc.tensor.transpose(psC[0:NC, i * P:(i + 1) * P], cs[:, i, :],
                                                     T.const[:, C_IDENT:C_IDENT + P])
                        mm.then_inc(M["a_ct"], 1)

                    def values(r):
                        pe.wait_ge(M["a_te"], t * NP_ * U + NP_ * TT * (r + 1) + 1)
                        pe.wait_ge(M["a_o"], t + 1)
                        o = psO[64 * r:64 * r + 64, :]
                        for b in range(NP_):
                            for k in range(TT):
                                lhs = vs[:, 0, k, r] if da else \
                                    T.tok[:, k, (TVS, TVW)[b] + 64 * r:(TVS, TVW)[b] + 64 * r + 64]
                                mm = nc.tensor.matmul(o[:, k * P:S], lhs, PT[:, r, b, k, k * P:S],
                                                      start=b == 0 and k == 0,
                                                      stop=da and k == TT - 1, skip_group_check=True)
                        if not da:
                            pe.wait_ge(M["a_cte"], t * 2 + r + 2)
                            mm = nc.tensor.matmul(o, T.vcmp[0:NC, r, :], ctp[:, r, :], start=False, stop=True,
                                                  skip_group_check=True)
                        mm.then_inc(M["a_pv"], 1)

                    for u in range(U + 1):
                        if u < U:
                            scores(u)
                        if not da and u % TT == 0 and u < U:
                            cmp_scores(u // TT)
                        if u:
                            turn_probs(u - 1)
                        if not da and u % TT == 2:
                            cmp_turn(u // TT)
                        if u and u % TT == 0:
                            values(u // TT - 1)

            @block.scalar
            def _(act):
                act.sem_inc(M["a_e"], 1)
                act.sem_inc(M["a_te"], 1)
                with act.Fori(0, TILES) as t:
                    def exps(u):
                        r, i = units[u]
                        n = P * (i + 1)
                        act.wait_ge(M["a_nm"], t * U + u + 1)
                        if u >= 2:
                            act.wait_ge(M["a_t"], t * NP_ * U + NP_ * (u - 1) + 1)
                        else:
                            act.wait_ge(M["a_t"], t * NP_ * U + 1)
                        for m in range(2):
                            nc.scalar.activation(pb[:, u % 2, m, 0:n], psS[:, u % 2, m, 0:n], ACT.Exp,
                                                 bias=nm[:, u % 2, m:m + 1], scale=scale,
                                                 accum_out=sm[:, u % 2, m:m + 1]).then_inc(M["a_e"], 1)

                    def take_turned(u):
                        r, i = units[u]
                        for b in range(NP_):
                            n = NP_ * u + b
                            act.wait_ge(M["a_t"], t * NP_ * U + n + 2)
                            act.wait_ge(M["a_pv"], t * 2 + 1)
                            nc.scalar.activation(PT[:, r, b, 0:i + 1, i * P:(i + 1) * P],
                                                 psT[:, n % 2, 0:(i + 1) * P].rearrange("p (k q) -> p k q", q=P),
                                                 ACT.Copy).then_inc(M["a_te"], 1)

                    for u in range(U + 1):
                        if u < U:
                            exps(u)
                        if not da and u % TT == 1:
                            act.wait_ge(M["a_cm"], t * 2 + u // TT + 1)
                            nc.scalar.activation(cs[:, :, :], cs[:, :, :], ACT.Exp, scale=scale).then_inc(M["a_ce"], 1)
                        if u:
                            take_turned(u - 1)

            @block.vector
            def _(dve):
                dve.sem_inc(M["a_cte"], 1)
                dve.sem_inc(M["a_o"], 1)
                link = Chain(dve, M["a_ch"])
                per = 6 * U if da else 6 * U + 2 * 6
                with dve.Fori(0, TILES) as t:
                    link.enter(t, per)

                    def maxima(u):
                        r, i = units[u]
                        n = P * (i + 1)
                        dve.wait_ge(M["a_s"], t * U + u + 1)
                        for m in range(2):
                            d = psS[:, u % 2, m, i * P:n]
                            link(nc.vector.tensor_tensor(d, d, mask, ALU.add))
                        link(nc.vector.tensor_reduce(mx[:, u % 2], psS[:, u % 2, :, 0:n], X, ALU.max))
                        nc.vector.tensor_scalar(nm[:, u % 2], mx[:, u % 2], -scale, None,
                                                ALU.mult).then_inc(M["a_nm"], 1)

                    def weigh(u):
                        r, i = units[u]
                        n = P * (i + 1)
                        dve.wait_ge(M["a_e"], t * 2 * U + 2 * u + 2 + 1)
                        link(nc.vector.reciprocal(rc[:, u % 2], sm[:, u % 2]))
                        if da:
                            link(nc.vector.tensor_tensor(rc[:, u % 2, 1:2], rc[:, u % 2, 1:2], T.lam[:, 0:1], ALU.mult))
                            link(nc.vector.tensor_scalar(pb[:, u % 2, 1, 0:n], pb[:, u % 2, 1, 0:n],
                                                         rc[:, u % 2, 1:2], None, ALU.mult))
                            nc.vector.scalar_tensor_tensor(pb[:, u % 2, 0, 0:n], pb[:, u % 2, 0, 0:n],
                                                           rc[:, u % 2, 0:1], pb[:, u % 2, 1, 0:n],
                                                           ALU.mult, ALU.subtract).then_inc(M["a_pr"], 1)
                        else:
                            link(nc.vector.tensor_tensor(rc[:, u % 2], rc[:, u % 2],
                                                         T.tok[:, i, bass.ds(t * 3 + TGT + 12 * r + 1, 2)], ALU.mult))
                            link(nc.vector.tensor_scalar(pb[:, u % 2, 0, 0:n], pb[:, u % 2, 0, 0:n],
                                                         rc[:, u % 2, 0:1], None, ALU.mult))
                            nc.vector.tensor_scalar(pb[:, u % 2, 1, 0:n], pb[:, u % 2, 1, 0:n],
                                                    rc[:, u % 2, 1:2], None, ALU.mult).then_inc(M["a_pr"], 1)

                    def cmp_maxima(r):
                        dve.wait_ge(M["a_cs"], t * 2 + r + 1)
                        dve.wait_ge(M["a_ct"], t * 2 + r + 1)
                        add = T.const[:, C_CADD:C_CADD + TT * NC].rearrange("p (i c) -> p i c", i=TT)
                        sc = psC[:, 0:TT * 32].rearrange("p (i c) -> p i c", i=TT)[:, :, 0:NC]
                        link(nc.vector.tensor_tensor(cs[:, :, :], sc, add, ALU.add))
                        link(nc.vector.tensor_reduce(cst[:, 0], cs[:, :, :], X, ALU.max))
                        nc.vector.tensor_tensor(cs[:, :, :], cs[:, :, :],
                                                cst[:, 0].unsqueeze(2).to_broadcast([P, TT, NC]),
                                                ALU.subtract).then_inc(M["a_cm"], 1)

                    def cmp_weigh(r):
                        dve.wait_ge(M["a_ce"], t * 2 + r + 1)
                        link(nc.vector.tensor_reduce(cst[:, 1], cs[:, :, :], X, ALU.add))
                        link(nc.vector.reciprocal(cst[:, 2], cst[:, 1]))
                        g = T.tok[:, :, bass.ds(t * 3 + TGT + 12 * r, 1)]
                        link(nc.vector.tensor_tensor(cst[:, 2].unsqueeze(2), cst[:, 2].unsqueeze(2), g, ALU.mult))
                        mul = T.const[:, C_CMUL:C_CMUL + TT * NC].rearrange("p (i c) -> p i c", i=TT)
                        link(nc.vector.tensor_tensor(cs[:, :, :], cs[:, :, :], mul, ALU.mult))
                        nc.vector.tensor_tensor(cs[:, :, :], cs[:, :, :],
                                                cst[:, 2].unsqueeze(2).to_broadcast([P, TT, NC]),
                                                ALU.mult).then_inc(M["a_cp"], 1)

                    for u in range(U + 1):
                        if u < U:
                            maxima(u)
                        if not da and u % TT == 0 and u < U:
                            cmp_maxima(u // TT)
                        if u:
                            weigh(u - 1)
                        if not da and u % TT == 1:
                            cmp_weigh(u // TT)
                        if not da and u % TT == 3:
                            dve.wait_ge(M["a_ct"], t * 2 + u // TT + 2)
                            dve.wait_ge(M["a_pv"], t * 2 + 1)
                            nc.vector.tensor_copy(ctp[:, u // TT, :], psC[0:NC, :]).then_inc(M["a_cte"], 1)
                    dve.wait_ge(M["a_pv"], t * 2 + 2 + 1)
                    if not da:
                        nc.vector.tensor_copy(T.y[:, t + 4], psO[:, :]).then_inc(M["a_o"], 1)
                    else:
                        nc.vector.tensor_copy(oT[:, t], psO[:, :]).then_inc(M["a_o"], 1)
                    link.leave(TILES)
        clear(nc, M)
        if not da:
            return
        N = semaphores(nc, ctx, "b_sq b_mm b_root b_ch")
        with nc.Block() as block:
            @block.scalar
            def _(act):
                for a in range(2):
                    nc.scalar.activation(pb[:, 0, a], oT[:, a], ACT.Square).then_inc(N["b_sq"], 1)
                for a in range(2):
                    act.wait_ge(N["b_mm"], a + 1)
                    nc.scalar.activation(pb[:, 1, a], psS[:, 0, a], ACT.Sqrt,
                                         bias=T.eps[:, 0:1]).then_inc(N["b_root"], 1)

            @block.tensor
            def _(pe):
                for a in range(2):
                    pe.wait_ge(N["b_sq"], a + 1)
                    nc.tensor.matmul(psS[:, 0, a], T.const[:, C_BLK:C_BLK + P], pb[:, 0, a], start=True,
                                     stop=True).then_inc(N["b_mm"], 1)

            @block.vector
            def _(dve):
                link = Chain(dve, N["b_ch"])
                for a in range(2):
                    dve.wait_ge(N["b_root"], a + 1)
                    link(nc.vector.reciprocal(pb[:, 1, a], pb[:, 1, a]))
                    link(nc.vector.scalar_tensor_tensor(T.y[:, 2 + a], oT[:, a], T.lam[:, 1:2], pb[:, 1, a],
                                                        ALU.mult, ALU.mult))
        clear(nc, N)


def out_proj(nc, T, w_of, first, tag):
    with ExitStack() as ctx:
        M = semaphores(nc, ctx, W_SEMS + "x_hi x_lo o_res")
        yh = ctx.enter_context(nc.sbuf_tensor("o_yh" + tag, [P, KD, S], F32R))
        yl = ctx.enter_context(nc.sbuf_tensor("o_yl" + tag, [P, KD, S], F32R))
        W = Weights(nc, ctx, M, "o" + tag, KD, lambda i, j: w_of(i * 4 + j))
        ps = ctx.enter_context(nc.psum_tensor("o_ps" + tag, [P, 4, S], F32))
        with nc.Block() as block:
            @block.sync
            def _(sp):
                with sp.Fori(0, KD // 4) as i:
                    for j in range(4):
                        W.load(sp, i, j)

            @block.scalar
            def _(act):
                split(nc, M, T.y, yh, yl, act=act)
                with act.Fori(0, KD // 4) as i:
                    for j in range(4):
                        W.round(act, i, j)

            @block.gpsimd
            def _(pool):
                pool.sem_inc(M["w_lo"], 4)
                split(nc, M, T.y, yh, yl, pool=pool)
                with pool.Fori(0, KD // 4) as i:
                    for j in range(4):
                        W.rest(pool, i, j)

            @block.tensor
            def _(pe):
                pe.sem_inc(M["w_mm"], 2)
                pe.wait_ge(M["x_lo"], KD)
                with pe.Fori(0, KD // 4) as i:
                    for j in range(4):
                        pe.wait_ge(M["o_res"], i * 4 + j + 1)
                        W.times(pe, i, j, ps[:, j], yh, yl)

            @block.vector
            def _(dve):
                dve.sem_inc(M["o_res"], 4)
                with dve.Fori(0, KD // 4) as i:
                    for j in range(4):
                        dve.wait_ge(M["w_mm"], i * 4 + j + 3)
                        xt = T.xT[:, i * 4 + j]
                        if first:
                            nc.vector.scalar_tensor_tensor(xt, ps[:, j], T.mod[:, bass.ds(i * 4 + j + 40, 1)],
                                                           xt, ALU.mult, ALU.add).then_inc(M["o_res"], 1)
                        else:
                            nc.vector.scalar_tensor_tensor(xt, xt, ALPHA, ps[:, j],
                                                           ALU.mult, ALU.add).then_inc(M["o_res"], 1)
        clear(nc, M)


def final_norm(nc, T):
    with ExitStack() as ctx:
        M = semaphores(nc, ctx, "n_sq n_sum n_root n_rstd n_t n_h")
        sb = lambda n, s: ctx.enter_context(nc.sbuf_tensor(n, s, F32))
        sq = sb("z_sq", [P, 2, S])
        tmp = sb("z_tmp", [P, 2, S])
        rstd = sb("z_rstd", [P, S])
        psN = ctx.enter_context(nc.psum_tensor("z_psN", [P, S], F32))
        with nc.Block() as block:
            @block.scalar
            def _(act):
                square_sums(nc, T, act, None, M, sq, psN[:, :], rstd[:, :])

            @block.tensor
            def _(pe):
                square_sums(nc, T, None, pe, M, sq, psN[:, :], None)

            @block.vector
            def _(dve):
                dve.wait_ge(M["n_root"], 1)
                nc.vector.reciprocal(rstd[:, :], rstd[:, :]).then_inc(M["n_rstd"], 1)
                dve.wait_ge(M["n_rstd"], 1)
                for k in range(KD):
                    nc.vector.scalar_tensor_tensor(T.xT[:, k], T.xT[:, k], T.q1[:, Q_FG + k:Q_FG + k + 1],
                                                   rstd[:, :], ALU.mult, ALU.mult).then_inc(M["n_h"], 1)
        clear(nc, M)


def proj2(nc, T):
    with ExitStack() as ctx:
        M = semaphores(nc, ctx, W_SEMS + "x_hi x_lo p_wt p_out p_tmm p_tout")
        sb = lambda n, s, t=F32: ctx.enter_context(nc.sbuf_tensor(n, s, t))
        wt = sb("p2_wt", [P, KD, 256])
        xh = sb("p2_xh", [P, KD, S], F32R)
        xl = sb("p2_xl", [P, KD, S], F32R)
        W = Weights(nc, ctx, M, "p2", KD, lambda i, j: T.d["win2"][i * 4 + j])
        psZ = ctx.enter_context(nc.psum_tensor("p2_psZ", [P, 4, S], F32))
        psT = ctx.enter_context(nc.psum_tensor("p2_psT", [P, 2, S], F32))
        with nc.Block() as block:
            @block.sync
            def _(sp):
                with sp.Fori(0, 4) as i:
                    for j in range(4):
                        W.load(sp, i, j)
                sp.dma_start(wt[:, :, :], T.d["wtok2"]).then_inc(M["p_wt"], 16)

            @block.scalar
            def _(act):
                split(nc, M, T.xT, xh, xl, act=act)
                with act.Fori(0, 4) as i:
                    for j in range(4):
                        W.round(act, i, j)

            @block.gpsimd
            def _(pool):
                pool.sem_inc(M["w_lo"], 4)
                split(nc, M, T.xT, xh, xl, pool=pool)
                with pool.Fori(0, 4) as i:
                    for j in range(4):
                        W.rest(pool, i, j)

            @block.tensor
            def _(pe):
                pe.sem_inc(M["w_mm"], 2)
                pe.wait_ge(M["x_lo"], KD)
                with pe.Fori(0, 4) as i:
                    for j in range(4):
                        pe.wait_ge(M["p_out"], i * 4 + j + 1)
                        W.times(pe, i, j, psZ[:, j], xh, xl)
                pe.wait_ge(M["p_wt"], 16)
                for t in range(TT):
                    if t >= 2:
                        pe.wait_ge(M["p_tout"], t - 1)
                    for k in range(KD):
                        mm = nc.tensor.matmul(psT[:, t % 2, 0:256], T.xT[:, k, t * P:(t + 1) * P],
                                              wt[:, k, :], start=k == 0, stop=k == KD - 1)
                    mm.then_inc(M["p_tmm"], 1)

            @block.vector
            def _(dve):
                dve.sem_inc(M["p_out"], 4)
                with dve.Fori(0, 4) as i:
                    for j in range(4):
                        dve.wait_ge(M["w_mm"], i * 4 + j + 3)
                        nc.vector.tensor_copy(T.z[:, i * 4 + j], psZ[:, j]).then_inc(M["p_out"], 1)
                for t in range(TT):
                    dve.wait_ge(M["p_tmm"], t + 1)
                    nc.vector.tensor_copy(T.tok[:, t], psT[:, t % 2, 0:256]).then_inc(M["p_tout"], 1)
        clear(nc, M)


def convs(nc, T):
    A, G, PI, CH, GB, GC = 0, 2, 4, 6, 8, 10
    W31, PADA, PADP, PADC = 31, 32, 16, 2
    with ExitStack() as ctx:
        M = semaphores(nc, ctx, "v_w v_sig v_pad v_ch v_conv v_mu v_sq v_var v_root v_cen v_nrm v_pool v_pmm")
        sb = lambda n, s: ctx.enter_context(nc.sbuf_tensor(n, s, F32))
        u = sb("v_u", [P, 2, PADA + S])
        h = sb("v_h", [P, 2, S])
        sq = sb("v_sq", [P, 2, S])
        rstd = sb("v_rstd", [P, S])
        wa = sb("v_wa", [P, 2, PADP + S])
        wb = sb("v_wb", [P, 2, PADP + S])
        pin = sb("v_pin", [P, 2, PADP + S])
        pooled = sb("v_pooled", [P, 2, S])
        first = sb("v_first", [P, 16])
        cp = sb("v_cp", [P, 2, PADC + S])
        ch = sb("v_ch_", [P, 2, S])
        pw = sb("v_pw", [P, 2, HD])
        psM = ctx.enter_context(nc.psum_tensor("v_psM", [P, 2, S], F32))
        psP = ctx.enter_context(nc.psum_tensor("v_psP", [P, 2, S], F32))
        q1 = T.q1
        with nc.Block() as block:
            @block.sync
            def _(sp):
                sp.dma_start(pw[:, :, :], T.d["pw"]).then_inc(M["v_w"], 16)

            @block.gpsimd
            def _(pool):
                for n, (buf, pad) in enumerate(((u, PADA), (wa, PADP), (wb, PADP), (pin, PADP), (cp, PADC))):
                    if n:
                        pool.wait_ge(M["v_pad"], n)
                    nc.gpsimd.memset(buf[:, :, 0:pad], 0.0).then_inc(M["v_pad"], 1)

            @block.scalar
            def _(act):
                nc.scalar.activation(T.z[:, G:G + 2], T.z[:, G:G + 2], ACT.Sigmoid).then_inc(M["v_sig"], 1)
                act.wait_ge(M["v_cen"], 1)
                for a in range(2):
                    nc.scalar.activation(sq[:, a], h[:, a], ACT.Square).then_inc(M["v_sq"], 1)
                act.wait_ge(M["v_var"], 1)
                nc.scalar.activation(rstd[:, :], psM[:, 1], ACT.Sqrt, bias=T.eps[:, 1:2]).then_inc(M["v_root"], 1)
                act.wait_ge(M["v_nrm"], 2)
                for a in range(2):
                    nc.scalar.activation(T.y[:, a], h[:, a], ACT.Silu, scale=q1[:, Q_NG + a:Q_NG + a + 1],
                                         bias=q1[:, Q_NB + a:Q_NB + a + 1])

            @block.tensor
            def _(pe):
                c256 = T.const[:, C_BLK256:C_BLK256 + P]
                pe.wait_ge(M["v_conv"], 2 * W31)
                for a in range(2):
                    mm = nc.tensor.matmul(psM[:, 0], c256, h[:, a], start=a == 0, stop=a == 1)
                mm.then_inc(M["v_mu"], 1)
                pe.wait_ge(M["v_w"], 16)
                pe.wait_ge(M["v_pool"], 1)
                for a in range(2):
                    for r in (0, 64):
                        mm = nc.tensor.matmul(psP[r:r + 64, a], pw[r:r + 64, a], pooled[r:r + 64, a],
                                              start=True, stop=True)
                mm.then_inc(M["v_pmm"], 1)
                pe.wait_ge(M["v_sq"], 2)
                for a in range(2):
                    mm = nc.tensor.matmul(psM[:, 1], c256, sq[:, a], start=a == 0, stop=a == 1)
                mm.then_inc(M["v_var"], 1)

            @block.vector
            def _(dve):
                link = Chain(dve, M["v_ch"])
                dve.wait_ge(M["v_sig"], 1)
                link(nc.vector.tensor_tensor(u[:, :, PADA:], T.z[:, A:A + 2], T.z[:, G:G + 2], ALU.mult))
                dve.wait_ge(M["v_pad"], 5)
                for n in range(2 * W31):
                    tap, a = divmod(n, 2)
                    src = u[:, a, PADA - 30 + tap:PADA - 30 + tap + S]
                    w = q1[:, Q_CAW + 31 * a + tap:Q_CAW + 31 * a + tap + 1]
                    if tap == 0:
                        ins = nc.vector.tensor_scalar(h[:, a], src, w, q1[:, Q_CAB + a:Q_CAB + a + 1],
                                                      ALU.mult, ALU.add)
                    else:
                        dve.wait_ge(M["v_conv"], n - 1)
                        ins = nc.vector.scalar_tensor_tensor(h[:, a], src, w, h[:, a], ALU.mult, ALU.add)
                    ins.then_inc(M["v_conv"], 1)
                link(nc.vector.tensor_copy(pin[:, :, PADP:], T.z[:, PI:PI + 2]))
                win = ((pin, wa, 1, 0, 0), (wa, wb, 2, 64, 0), (wb, wa, 4, 0, 1), (wa, wb, 8, 64, 1))
                for n, (src, dst, back, r, a) in enumerate(win):
                    link(nc.vector.tensor_tensor(dst[:, :, PADP:], src[:, :, PADP:],
                                                 src[:, :, PADP - back:PADP + S - back], ALU.add))
                    rows = slice(r, r + 64)
                    inv = T.const[rows, C_INVC + 16 * a:C_INVC + 16 * a + 16]
                    link(nc.vector.scalar_tensor_tensor(pooled[rows, a], dst[rows, a, PADP:], inv[:, 15:16],
                                                        T.z[rows, PI + a], ALU.mult, ALU.subtract))
                    link(nc.vector.tensor_tensor(first[rows, :], dst[rows, a, PADP:PADP + 16], inv, ALU.mult))
                    link(nc.vector.tensor_tensor(pooled[rows, a, 0:16], first[rows, :],
                                                 T.z[rows, PI + a, 0:16], ALU.subtract))
                dve.wait_ge(M["v_mu"], 1)
                for a in range(2):
                    link(nc.vector.tensor_tensor(h[:, a], h[:, a], psM[:, 0], ALU.subtract))
                nc.vector.memset(first[:, 0:1], 0.0).then_inc(M["v_cen"], 1)
                nc.vector.memset(first[:, 1:2], 0.0).then_inc(M["v_pool"], 1)
                link(nc.vector.tensor_tensor(cp[:, :, PADC:], T.z[:, GC:GC + 2], T.z[:, CH:CH + 2], ALU.mult))
                for a in range(2):
                    for tap in range(3):
                        src = cp[:, a, tap:tap + S]
                        w = q1[:, Q_CCW + 3 * a + tap:Q_CCW + 3 * a + tap + 1]
                        if tap == 0:
                            link(nc.vector.tensor_scalar(ch[:, a], src, w, None, ALU.mult))
                        else:
                            link(nc.vector.scalar_tensor_tensor(ch[:, a], src, w, ch[:, a], ALU.mult, ALU.add))
                    link(nc.vector.tensor_tensor(T.y[:, 4 + a], ch[:, a], T.z[:, GB + a], ALU.mult))
                dve.wait_ge(M["v_pmm"], 1)
                for a in range(2):
                    link(nc.vector.tensor_scalar(T.y[:, 2 + a], psP[:, a], q1[:, Q_PSC + a:Q_PSC + a + 1], None,
                                                 ALU.mult))
                dve.wait_ge(M["v_root"], 1)
                link(nc.vector.reciprocal(rstd[:, :], rstd[:, :]))
                for a in range(2):
                    nc.vector.tensor_tensor(h[:, a], h[:, a], rstd[:, :], ALU.mult).then_inc(M["v_nrm"], 1)
        clear(nc, M)


def stick_attention(nc, T):
    Q, K = 12, 14
    scale = HD ** -0.5
    H = 2
    with ExitStack() as ctx:
        M = semaphores(nc, ctx, "k_st k_s k_abs k_exp k_ln k_ch k_cst k_lw k_p k_t k_te k_pv k_o")
        sb = lambda n, s: ctx.enter_context(nc.sbuf_tensor(n, s, F32))
        qs = sb("k_q", [P, S])
        ks = sb("k_k", [P, S])
        vs = sb("k_v", [P, TT, 2, HD])
        e = sb("k_e", [P, TT, S])
        sp_ = sb("k_sp", [P, TT, S])
        cum = sb("k_cum", [P, TT, S])
        ones = sb("k_ones", [P, S])
        nmask = sb("k_nmask", [P, P])
        tot = sb("k_tot", [P, TT])
        PT = sb("k_pt", [P, TT, S])
        psS = ctx.enter_context(nc.psum_tensor("k_psS", [P, TT, S], F32))
        psT = ctx.enter_context(nc.psum_tensor("k_psT", [P, 2, S], F32))
        psO = ctx.enter_context(nc.psum_tensor("k_psO", [P, S], F32))
        strict = T.const[:, C_STRICT:C_STRICT + P]
        with nc.Block() as block:
            @block.gpsimd
            def _(pool):
                pool.sem_inc(M["k_st"], 1)
                with pool.Fori(0, 2) as t:
                    pool.wait_ge(M["k_pv"], t * H + 1)
                    pool.wait_ge(M["k_st"], t * 3 + 1)
                    nc.gpsimd.tensor_copy(qs[:, :], T.z[:, t + Q]).then_inc(M["k_st"], 1)
                    pool.wait_ge(M["k_st"], t * 3 + 2)
                    nc.gpsimd.tensor_copy(ks[:, :], T.z[:, t + K]).then_inc(M["k_st"], 1)
                    pool.wait_ge(M["k_st"], t * 3 + 2 + 1)
                    nc.gpsimd.tensor_copy(vs[:, :, :, :].rearrange("p t r d -> p t (r d)"),
                                          T.tok[:, :, bass.ds(t * P, P)]).then_inc(M["k_st"], 1)

            @block.tensor
            def _(pe):
                pe.sem_inc(M["k_pv"], 1)
                pe.sem_inc(M["k_t"], 1)
                with pe.Fori(0, 2) as t:
                    pe.wait_ge(M["k_st"], t * 3 + 3 + 1)
                    for r in range(H):
                        pe.wait_ge(M["k_lw"], t * H * TT + r * TT + 1)
                        rows = slice(64 * r, 64 * r + 64)
                        for i in range(TT):
                            nc.tensor.matmul(psS[:, i, 0:P * (i + 1)], qs[rows, i * P:(i + 1) * P],
                                             ks[rows, 0:P * (i + 1)], start=True, stop=True).then_inc(M["k_s"], 1)
                        for i in range(TT):
                            pe.wait_ge(M["k_p"], t * H * TT + r * TT + i + 2)
                            n = r * TT + i
                            if n >= 2:
                                pe.wait_ge(M["k_te"], t * H * TT + n - 1 + 1)
                            else:
                                pe.wait_ge(M["k_te"], t * H * TT + 1)
                            for k in range(i + 1):
                                mm = nc.tensor.transpose(psT[:, n % 2, k * P:(k + 1) * P],
                                                         e[:, i, k * P:(k + 1) * P],
                                                         T.const[:, C_IDENT:C_IDENT + P])
                            mm.then_inc(M["k_t"], 1)
                        pe.wait_ge(M["k_te"], t * H * TT + (r + 1) * TT + 1)
                        pe.wait_ge(M["k_o"], t + 1)
                        for k in range(TT):
                            mm = nc.tensor.matmul(psO[rows, k * P:S], vs[:, k, r], PT[:, k, k * P:S],
                                                  start=k == 0, stop=k == TT - 1, skip_group_check=True)
                        mm.then_inc(M["k_pv"], 1)

            @block.scalar
            def _(act):
                act.sem_inc(M["k_te"], 1)
                act.sem_inc(M["k_p"], 1)
                with act.Fori(0, 2) as t:
                    for r in range(H):
                        b = t * H * TT + r * TT
                        act.wait_ge(M["k_t"], b + 1)
                        for i in range(TT):
                            act.wait_ge(M["k_s"], b + i + 1)
                            n = P * (i + 1)
                            nc.scalar.activation(e[:, i, 0:n], psS[:, i, 0:n], ACT.Abs).then_inc(M["k_abs"], 1)
                        for i in range(TT):
                            act.wait_ge(M["k_abs"], b + i + 1)
                            n = P * (i + 1)
                            nc.scalar.activation(e[:, i, 0:n], e[:, i, 0:n], ACT.Exp, scale=-scale).then_inc(M["k_exp"], 1)
                        for i in range(TT):
                            act.wait_ge(M["k_exp"], b + i + 1)
                            n = P * (i + 1)
                            nc.scalar.activation(e[:, i, 0:n], e[:, i, 0:n], ACT.Ln, bias=1.0).then_inc(M["k_ln"], 1)
                        for i in range(TT):
                            act.wait_ge(M["k_lw"], b + i + 2)
                            n = P * (i + 1)
                            nc.scalar.activation(e[:, i, 0:n], cum[:, i, 0:n], ACT.Exp,
                                                 bias=tot[:, i:i + 1]).then_inc(M["k_p"], 1)
                        for i in range(TT):
                            act.wait_ge(M["k_t"], b + i + 2)
                            act.wait_ge(M["k_pv"], t * H + r + 1)
                            nc.scalar.activation(PT[:, 0:i + 1, i * P:(i + 1) * P],
                                                 psT[:, (r * TT + i) % 2, 0:(i + 1) * P].rearrange(
                                                     "p (k q) -> p k q", q=P), ACT.Copy).then_inc(M["k_te"], 1)

            @block.vector
            def _(dve):
                dve.sem_inc(M["k_lw"], 1)
                dve.sem_inc(M["k_o"], 1)
                nc.vector.memset(ones[:, :], 1.0).then_inc(M["k_cst"], 1)
                nc.vector.tensor_scalar(nmask[:, :], strict, 1.0, -NEG, ALU.subtract, ALU.mult).then_inc(M["k_cst"], 1)
                dve.wait_ge(M["k_cst"], 2)
                link = Chain(dve, M["k_ch"])
                with dve.Fori(0, 2) as t:
                    link.enter(t, 7 * H * TT)
                    for r in range(H):
                        b = t * H * TT + r * TT
                        for i in range(TT):
                            n = P * (i + 1)
                            d = slice(i * P, n)
                            dve.wait_ge(M["k_abs"], b + i + 1)
                            dve.wait_ge(M["k_p"], b + 1)
                            link(nc.vector.tensor_scalar(sp_[:, i, 0:n], psS[:, i, 0:n], scale, 0.0, ALU.mult, ALU.max))
                            dve.wait_ge(M["k_ln"], b + i + 1)
                            link(nc.vector.tensor_tensor(sp_[:, i, 0:n], sp_[:, i, 0:n], e[:, i, 0:n], ALU.add))
                            link(nc.vector.tensor_tensor(sp_[:, i, d], sp_[:, i, d], strict, ALU.mult))
                            link(nc.vector.tensor_tensor_scan(cum[:, i, 0:n], ones[:, 0:n], sp_[:, i, 0:n], 0.0,
                                                              ALU.mult, ALU.add))
                            link(nc.vector.tensor_scalar(tot[:, i:i + 1], cum[:, i, n - 1:n], -1.0, None, ALU.mult))
                            link(nc.vector.tensor_tensor(cum[:, i, 0:n], cum[:, i, 0:n], sp_[:, i, 0:n], ALU.subtract))
                            link(nc.vector.tensor_tensor(cum[:, i, d], cum[:, i, d], nmask[:, :], ALU.add))
                            nc.vector.scalar_tensor_tensor(cum[:, i, 0:n], psS[:, i, 0:n], scale, cum[:, i, 0:n],
                                                           ALU.mult, ALU.add).then_inc(M["k_lw"], 1)
                    dve.wait_ge(M["k_pv"], t * H + H + 1)
                    nc.vector.tensor_copy(T.y[:, t + 6], psO[:, :]).then_inc(M["k_o"], 1)
                    link.leave(2)
        clear(nc, M)


def layer_norm_features(nc, T):
    with ExitStack() as ctx:
        M = semaphores(nc, ctx, "l_mu l_cen l_sq l_sum l_root l_r l_t l_x")
        sb = lambda n, s: ctx.enter_context(nc.sbuf_tensor(n, s, F32))
        sq = sb("l_sqb", [P, 2, S])
        tmp = sb("l_tmp", [P, 2, S])
        rstd = sb("l_rstd", [P, S])
        ps = ctx.enter_context(nc.psum_tensor("l_ps", [P, 2, S], F32))
        ones = T.const[:, C_ONES:C_ONES + P]
        with nc.Block() as block:
            @block.tensor
            def _(pe):
                for k in range(KD):
                    mm = nc.tensor.matmul(ps[:, 0], ones, T.xT[:, k], start=k == 0, stop=k == KD - 1)
                mm.then_inc(M["l_mu"], 1)
                for k in range(KD):
                    pe.wait_ge(M["l_sq"], k + 1)
                    nc.tensor.matmul(ps[:, 1], ones, sq[:, k % 2], start=k == 0,
                                     stop=k == KD - 1).then_inc(M["l_sum"], 1)

            @block.scalar
            def _(act):
                for k in range(KD):
                    act.wait_ge(M["l_cen"], k + 1)
                    if k >= 2:
                        act.wait_ge(M["l_sum"], k - 1)
                    nc.scalar.activation(sq[:, k % 2], T.xT[:, k], ACT.Square).then_inc(M["l_sq"], 1)
                act.wait_ge(M["l_sum"], KD)
                nc.scalar.activation(rstd[:, :], ps[:, 1], ACT.Sqrt, bias=T.eps[:, 1:2]).then_inc(M["l_root"], 1)

            @block.vector
            def _(dve):
                dve.wait_ge(M["l_mu"], 1)
                for k in range(KD):
                    nc.vector.tensor_tensor(T.xT[:, k], T.xT[:, k], ps[:, 0], ALU.subtract).then_inc(M["l_cen"], 1)
                dve.wait_ge(M["l_root"], 1)
                nc.vector.reciprocal(rstd[:, :], rstd[:, :]).then_inc(M["l_r"], 1)
                dve.wait_ge(M["l_r"], 1)
                for k in range(KD):
                    if k >= 2:
                        dve.wait_ge(M["l_x"], k - 1)
                    nc.vector.tensor_tensor(tmp[:, k % 2], T.xT[:, k], rstd[:, :], ALU.mult).then_inc(M["l_t"], 1)
                    dve.wait_ge(M["l_t"], k + 1)
                    nc.vector.tensor_scalar(T.xT[:, k], tmp[:, k % 2], T.q1[:, Q_L1G + k:Q_L1G + k + 1],
                                            T.q1[:, Q_L1B + k:Q_L1B + k + 1], ALU.mult,
                                            ALU.add).then_inc(M["l_x"], 1)
        clear(nc, M)


def peer_keys(nc, T):
    with ExitStack() as ctx:
        M = semaphores(nc, ctx, "e_w*2 e_keys e_passed e_mm e_q e_sc e_top e_ch e_x e_xo")
        sb = lambda n, s: ctx.enter_context(nc.sbuf_tensor(n, s, F32))
        wq = sb("e_wq", [P, 2, KD * P])
        keys = sb("e_keysb", [P, 2 * PH, KEYS])
        q = sb("e_qb", [P, 2, S])
        rest = sb("e_rest", [P, TT, KEYS])
        tv = sb("e_tv", [P, TT, TOP])
        ti = ctx.enter_context(nc.sbuf_tensor("e_ti", [P, TT, TOP], U32))
        psQ = ctx.enter_context(nc.psum_tensor("e_psQ", [P, 2, S], F32))
        psS = ctx.enter_context(nc.psum_tensor("e_psS", [P, 2, S], F32))
        psX = ctx.enter_context(nc.psum_tensor("e_psX", [P, 2, S], F32))
        with nc.Block() as block:
            @block.sync
            def _(sp):
                sp.dma_start(keys[:, :, :], T.d["keys"]).then_inc(M["e_keys"], 16)
                with sp.Fori(0, PH) as i:
                    for j in range(2):
                        sp.wait_ge(M["e_mm"], i * 2 + 1)
                        sp.dma_start(wq[:, j], T.d["wq"][i * 2 + j]).then_inc(M["e_w"][j], 16)

            @block.tensor
            def _(pe):
                pe.sem_inc(M["e_mm"], 1)
                pe.sem_inc(M["e_sc"], 1)
                for k in range(KD):
                    if k >= 2:
                        pe.wait_ge(M["e_xo"], k - 1)
                    for t in range(TT):
                        mm = nc.tensor.transpose(psX[:, k % 2, t * P:(t + 1) * P], T.xT[:, k, t * P:(t + 1) * P],
                                                 T.const[:, C_IDENT:C_IDENT + P])
                    mm.then_inc(M["e_x"], 1)
                pe.wait_ge(M["e_keys"], 16)
                with pe.Fori(0, PH) as i:
                    for j in range(2):
                        pe.wait_ge(M["e_w"][j], i * 16 + 16)
                        pe.wait_ge(M["e_q"], i * 2 + 1)
                        for k in range(KD):
                            mm = nc.tensor.matmul(psQ[:, j], wq[:, j, k * P:(k + 1) * P], T.xT[:, k],
                                                  start=k == 0, stop=k == KD - 1)
                        mm.then_inc(M["e_mm"], 1)
                    for j in range(2):
                        pe.wait_ge(M["e_q"], i * 2 + j + 2)
                        pe.wait_ge(M["e_top"], i * 2 + 1)
                        for t in range(TT):
                            mm = nc.tensor.matmul(psS[:, j, t * P:(t + 1) * P], q[:, j, t * P:(t + 1) * P],
                                                  keys[:, i * 2 + j], start=True, stop=True)
                        mm.then_inc(M["e_sc"], 1)

            @block.scalar
            def _(act):
                act.sem_inc(M["e_q"], 1)
                for k in range(KD):
                    act.wait_ge(M["e_x"], k + 1)
                    nc.scalar.activation(T.xtok[:, :, k * P:(k + 1) * P],
                                         psX[:, k % 2].rearrange("p (t d) -> p t d", d=P),
                                         ACT.Copy).then_inc(M["e_xo"], 1)
                with act.Fori(0, PH) as i:
                    for j in range(2):
                        act.wait_ge(M["e_mm"], i * 2 + j + 2)
                        act.wait_ge(M["e_sc"], i * 2 + 1)
                        nc.scalar.activation(q[:, j], psQ[:, j], ACT.Copy).then_inc(M["e_q"], 1)

            @block.vector
            def _(dve):
                dve.sem_inc(M["e_top"], 1)
                link = Chain(dve, M["e_ch"], M["e_passed"])
                with dve.Fori(0, PH) as i:
                    link.enter(i, 2 * (5 * TT + 1))
                    for j in range(2):
                        dve.wait_ge(M["e_sc"], i * 2 + j + 2)
                        dve.sem_inc(M["e_passed"], 1)
                        for t in range(TT):
                            s = psS[:, j, t * P:(t + 1) * P]
                            link(nc.vector.max(tv[:, t, 0:8], s))
                            link(nc.vector.max_index(ti[:, t, 0:8], tv[:, t, 0:8], s))
                            link(nc.vector.match_replace(rest[:, t], tv[:, t, 0:8], s, -3e38))
                            link(nc.vector.max(tv[:, t, 8:16], rest[:, t]))
                            link(nc.vector.max_index(ti[:, t, 8:16], tv[:, t, 8:16], rest[:, t]))
                        link(nc.vector.tensor_copy(T.topv[:, i * 2 + j], tv[:, :, :]))
                        nc.vector.tensor_copy(T.topi[:, i * 2 + j], ti[:, :, :]).then_inc(M["e_top"], 1)
                        dve.wait_ge(M["e_top"], i * 2 + j + 2)
                    link.leave(PH)
        clear(nc, M)


def peer_choice(nc, T):
    C = TOP * TOP
    with ExitStack() as ctx:
        M = semaphores(nc, ctx, "h_passed h_ch h_dif h_exp")
        sb = lambda n, s, t=F32: ctx.enter_context(nc.sbuf_tensor(n, s, t))
        cand = sb("h_cand", [P, PH, C])
        rest = sb("h_rest", [P, PH, C])
        best = sb("h_best", [P, PH, TOP])
        pos = sb("h_pos", [P, PH, TOP], U32)
        part = sb("h_part", [P, 2, NSEL], U32)
        partf = sb("h_partf", [P, 2, NSEL])
        key = sb("h_key", [P, 2, NSEL])
        sums = sb("h_sums", [P, PH])
        iota = T.const[:, C_IOTA:C_IOTA + TOP]
        with nc.Block() as block:
            @block.scalar
            def _(act):
                with act.Fori(0, TT) as t:
                    act.wait_ge(M["h_dif"], t + 1)
                    nc.scalar.activation(best[:, :, :], best[:, :, :], ACT.Exp).then_inc(M["h_exp"], 1)

            @block.vector
            def _(dve):
                link = Chain(dve, M["h_ch"], M["h_passed"])
                with dve.Fori(0, TT) as t:
                    link.enter(t, 5 * PH + 17)
                    tv = T.topv[:, :, t].rearrange("p (h two) k -> p h two k", two=2)
                    ti = T.topi[:, :, t].rearrange("p (h two) k -> p h two k", two=2)
                    full = [P, PH, TOP, TOP]
                    link(nc.vector.tensor_tensor(cand[:, :, :].rearrange("p h (a b) -> p h a b", b=TOP),
                                                 tv[:, :, 0].unsqueeze(3).to_broadcast(full),
                                                 tv[:, :, 1].unsqueeze(2).to_broadcast(full), ALU.add))
                    for h in range(PH):
                        link(nc.vector.max(best[:, h, 0:8], cand[:, h]))
                        link(nc.vector.max_index(pos[:, h, 0:8], best[:, h, 0:8], cand[:, h]))
                        link(nc.vector.match_replace(rest[:, h], best[:, h, 0:8], cand[:, h], -3e38))
                        link(nc.vector.max(best[:, h, 8:16], rest[:, h]))
                        link(nc.vector.max_index(pos[:, h, 8:16], best[:, h, 8:16], rest[:, h]))
                    pf = pos[:, :, :].rearrange("p h k -> p (h k)")
                    link(nc.vector.tensor_scalar(part[:, 0], pf, 4, None, ALU.logical_shift_right))
                    link(nc.vector.tensor_scalar(part[:, 1], pf, 15, None, ALU.bitwise_and))
                    link(nc.vector.tensor_copy(partf[:, 0], part[:, 0]))
                    link(nc.vector.tensor_copy(partf[:, 1], part[:, 1]))
                    eq = rest[:, :, :].rearrange("p h (k r) -> p (h k) r", r=TOP)
                    eq4 = rest[:, :, :].rearrange("p h (k r) -> p h k r", r=TOP)
                    for m in range(2):
                        link(nc.vector.tensor_tensor(eq, partf[:, m].unsqueeze(2).to_broadcast([P, NSEL, TOP]),
                                                     iota.unsqueeze(1).to_broadcast([P, NSEL, TOP]), ALU.is_equal))
                        link(nc.vector.tensor_tensor(eq4, eq4, ti[:, :, m].unsqueeze(2).to_broadcast(full), ALU.mult))
                        link(nc.vector.tensor_reduce(key[:, m], eq, X, ALU.add))
                    link(nc.vector.scalar_tensor_tensor(key[:, 0], key[:, 0], float(KEYS), key[:, 1],
                                                        ALU.mult, ALU.add))
                    link(nc.vector.tensor_copy(T.idx[:, t], key[:, 0]))
                    top = best[:, :, 0:1]
                    link(nc.vector.tensor_copy(sums[:, :].unsqueeze(2), top))
                    nc.vector.tensor_tensor(best[:, :, :], best[:, :, :],
                                            sums[:, :].unsqueeze(2).to_broadcast([P, PH, TOP]),
                                            ALU.subtract).then_inc(M["h_dif"], 1)
                    dve.wait_ge(M["h_exp"], t + 1)
                    link(nc.vector.tensor_reduce(sums[:, :], best[:, :, :], X, ALU.add))
                    link(nc.vector.reciprocal(sums[:, :], sums[:, :]))
                    link(nc.vector.tensor_tensor(T.gates[:, t].rearrange("p (h k) -> p h k", k=TOP), best[:, :, :],
                                                 sums[:, :].unsqueeze(2).to_broadcast([P, PH, TOP]), ALU.mult))
                    link.leave(TT)
        clear(nc, M)


def peer_experts(nc, T):
    G, SETS = 4, 2
    NG = NSEL // (G * SETS)
    with ExitStack() as ctx:
        M = semaphores(nc, ctx, f"g_idx g_passed g_passed_v g_x g_u*{G * SETS} g_v*{G * SETS} g_dot g_gelu g_w g_diag g_mm g_r "
                          "g_ln g_lg g_al g_ch g_free g_cp g_rt g_out g_fin")
        sb = lambda n, s, t=F32: ctx.enter_context(nc.sbuf_tensor(n, s, t))
        ub = sb("g_ub", [P, SETS, G, D])
        vb = sb("g_vb", [P, SETS, G, D])
        ix = sb("g_ix", [P, SETS, G], U32)
        prod = sb("g_prod", [P, D])
        xrow = sb("g_xrow", [P, D])
        dot = sb("g_dotb", [P, SETS, G])
        wgt = sb("g_wgt", [P, SETS, G])
        diag = sb("g_diagb", [P, SETS, G, P])
        aid = sb("g_aid", [P, P])
        r = sb("g_rb", [P, D])
        lnp = sb("g_lnp", [P, 2, D])
        st = sb("g_st", [P, 2, 6])
        mv = sb("g_mv", [P, 4])
        psF = ctx.enter_context(nc.psum_tensor("g_psF", [P, 2, S], F32))
        W = G * SETS
        per_tile = NG * W
        ident = T.const[:, C_IDENT:C_IDENT + P]
        with nc.Block() as block:
            @block.gpsimd
            def _(pool):
                with pool.Fori(0, TT) as t:
                    with pool.Fori(0, NG) as g:
                        n = t * NG + g
                        for s in range(SETS):
                            pool.wait_ge(M["g_dot"], n * W + 1)
                            pool.wait_ge(M["g_mm"], n * SETS + 1)
                            if s:
                                pool.wait_ge(M["g_idx"], n * SETS + s)
                            nc.gpsimd.tensor_copy(ix[:, s], T.idx[:, t, bass.ds(g * W + s * G, G)]).then_inc(M["g_idx"], 1)
                            pool.wait_ge(M["g_idx"], n * SETS + s + 1)
                            pool.sem_inc(M["g_passed"], 1)
                            for k in range(G):
                                nc.gpsimd.indirect_dma_start(
                                    ub[:, s, k], None, T.d["u"],
                                    bass.IndirectOffsetOnAxis(ap=ix[:, s, k:k + 1], axis=0)
                                ).then_inc(M["g_u"][s * G + k], 16)
                            for k in range(G):
                                nc.gpsimd.indirect_dma_start(
                                    vb[:, s, k], None, T.d["v"],
                                    bass.IndirectOffsetOnAxis(ap=ix[:, s, k:k + 1], axis=0)
                                ).then_inc(M["g_v"][s * G + k], 16)

            @block.sync
            def _(sp):
                sp.sem_inc(M["g_free"], 1)
                sp.dma_start(lnp[:, :, :], T.d["ln2"]).then_inc(M["g_ln"], 16)
                with sp.Fori(0, TT) as t:
                    sp.wait_ge(M["g_fin"], t + 1)
                    sp.dma_start(T.d["out"][t], r[:, :]).then_inc(M["g_out"], 16)
                    sp.wait_ge(M["g_out"], t * 16 + 16)
                    sp.sem_inc(M["g_free"], 1)
                sp.wait_ge(M["g_out"], 16 * TT)

            @block.vector
            def _(dve):
                dve.sem_inc(M["g_dot"], 1)
                dve.sem_inc(M["g_cp"], 1)
                nc.vector.tensor_scalar(aid[:, :], ident, ALPHA, None, ALU.mult).then_inc(M["g_al"], 1)
                link = Chain(dve, M["g_ch"], M["g_passed_v"])
                dve.wait_ge(M["g_ln"], 16)
                with dve.Fori(0, TT) as t:
                    dve.wait_ge(M["g_dot"], t * per_tile + 1)
                    nc.vector.tensor_copy(xrow[:, :], T.xtok[:, t]).then_inc(M["g_x"], 1)
                    dve.wait_ge(M["g_x"], t + 1)
                    dve.sem_inc(M["g_passed_v"], 1)
                    with dve.Fori(0, NG) as g:
                        n = t * NG + g
                        for s in range(SETS):
                            for k in range(G):
                                dve.wait_ge(M["g_u"][s * G + k], n * 16 + 16)
                                dve.wait_ge(M["g_dot"], n * W + s * G + k + 1)
                                nc.vector.tensor_tensor_reduce(prod[:, :], ub[:, s, k], xrow[:, :], 1.0, 0.0,
                                                               ALU.mult, ALU.add,
                                                               dot[:, s, k:k + 1]).then_inc(M["g_dot"], 1)
                            dve.wait_ge(M["g_gelu"], n * SETS + s + 1)
                            nc.vector.tensor_tensor(wgt[:, s], dot[:, s],
                                                    T.gates[:, t, bass.ds(g * W + s * G, G)],
                                                    ALU.mult).then_inc(M["g_w"], 1)
                    dve.wait_ge(M["g_r"], t + 1)
                    link.enter(t, 7)
                    for c in range(2):
                        dve.wait_ge(M["g_free"], t + 1)
                        link(nc.vector.tensor_copy(r[:, c * S:(c + 1) * S], psF[:, c]))
                        link(nc.vector.bn_stats(st[:, c], r[:, c * S:(c + 1) * S]))
                    nc.vector.bn_aggr(mv[:, 0:2], st[:, :, :]).then_inc(M["g_cp"], 1)
                    dve.wait_ge(M["g_rt"], t + 1)
                    link(nc.vector.reciprocal(mv[:, 3:4], mv[:, 2:3]))
                    link(nc.vector.tensor_scalar(r[:, :], r[:, :], mv[:, 0:1], mv[:, 3:4], ALU.subtract, ALU.mult))
                    link(nc.vector.tensor_tensor(r[:, :], r[:, :], lnp[:, 0], ALU.mult))
                    nc.vector.tensor_tensor(r[:, :], r[:, :], lnp[:, 1], ALU.add).then_inc(M["g_fin"], 1)
                    link.leave(TT)

            @block.scalar
            def _(act):
                with act.Fori(0, TT) as t:
                    with act.Fori(0, NG) as g:
                        n = t * NG + g
                        for s in range(SETS):
                            act.wait_ge(M["g_dot"], n * W + (s + 1) * G + 1)
                            nc.scalar.activation(dot[:, s], dot[:, s], ACT.Gelu_apprx_tanh).then_inc(M["g_gelu"], 1)
                            act.wait_ge(M["g_w"], n * SETS + s + 1)
                            act.wait_ge(M["g_mm"], n * SETS + 1)
                            for k in range(G):
                                nc.scalar.activation(diag[:, s, k], ident, ACT.Copy,
                                                     scale=wgt[:, s, k:k + 1]).then_inc(M["g_diag"], 1)
                    act.wait_ge(M["g_cp"], t + 2)
                    nc.scalar.activation(mv[:, 2:3], mv[:, 1:2], ACT.Sqrt, bias=T.eps[:, 1:2]).then_inc(M["g_rt"], 1)

            @block.tensor
            def _(pe):
                pe.sem_inc(M["g_mm"], 1)
                pe.wait_ge(M["g_al"], 1)
                with pe.Fori(0, TT) as t:
                    pe.wait_ge(M["g_cp"], t + 1)
                    for c in range(2):
                        nc.tensor.matmul(psF[:, c], aid[:, :], T.xtok[:, t, c * S:(c + 1) * S], start=True,
                                         stop=False, skip_group_check=True)
                    with pe.Fori(0, NG) as g:
                        n = t * NG + g
                        for s in range(SETS):
                            for k in range(G):
                                pe.wait_ge(M["g_v"][s * G + k], n * 16 + 16)
                                pe.wait_ge(M["g_diag"], n * W + s * G + k + 1)
                                for c in range(2):
                                    mm = nc.tensor.matmul(psF[:, c], diag[:, s, k], vb[:, s, k, c * S:(c + 1) * S],
                                                          start=False, stop=False, skip_group_check=True)
                            mm.then_inc(M["g_mm"], 1)
                    pe.wait_ge(M["g_mm"], t * NG * SETS + NG * SETS + 1)
                    for c in range(2):
                        mm = nc.tensor.matmul(psF[:, c], T.zero[:, :], T.xtok[:, t, c * S:(c + 1) * S], start=False,
                                              stop=True, skip_group_check=True)
                    mm.then_inc(M["g_r"], 1)


class Tensors:
    pass


def build(nc, d, dbg=None):
    T = Tensors()
    T.d = d
    with ExitStack() as ctx:
        sb = lambda n, s: ctx.enter_context(nc.sbuf_tensor(n, s, F32))
        T.const = sb("const", [P, C_ALL])
        T.xT = sb("xT", [P, KD, S])
        T.q1 = sb("q1", [P, Q_ALL])
        T.eps = sb("eps", [P, 2])
        T.zero = sb("zero", [P, P])
        with ExitStack() as c1:
            s1 = lambda n, s: c1.enter_context(nc.sbuf_tensor(n, s, F32))
            T.crow = s1("crow", [P, D])
            T.par = s1("par", [P, P_ALL])
            T.mod = s1("mod", [P, 72])
            T.gain = s1("gain", [P, 24])
            T.raw = s1("raw", [P, 72])
            T.lam = s1("lam", [P, 2])
            load_constants(nc, T)
            first_modulation(nc, T)
            with nc.Fori(0, L) as layer:
                modulation(nc, T, layer, [0])
                ffn(nc, T, layer, 0)
                modulation(nc, T, layer, [1, 2])
                with ExitStack() as c2:
                    s2 = lambda n, s: c2.enter_context(nc.sbuf_tensor(n, s, F32))
                    T.z = s2("z", [P, NZ, S])
                    T.tok = s2("tok", [P, TT, NTOK])
                    T.kcmp = s2("kcmp", [P, NC])
                    T.vcmp = s2("vcmp", [NC, 2, HD])
                    T.rope = s2("rope", [P, 4 * S])
                    proj(nc, T, layer)
                    T.y = s2("y", [P, KD, S])
                    rope_gate_cmp(nc, T, layer)
                    soft_attention(nc, T, layer, "da")
                    soft_attention(nc, T, layer, "nsa")
                    if dbg:
                        dbg(nc, T, "y")
                    out_proj(nc, T, lambda n: T.d["wout"][layer, n], True, "1")
                ffn(nc, T, layer, 1)
            final_norm(nc, T)
            if dbg:
                dbg(nc, T, "xT")
        second_block(nc, T, ctx, dbg)


def second_block(nc, T, ctx, dbg):
    with ExitStack() as c2:
        s2 = lambda n, s: c2.enter_context(nc.sbuf_tensor(n, s, F32))
        T.z = s2("z2", [P, 16, S])
        T.tok = s2("tok2", [P, TT, 256])
        T.y = s2("y2", [P, KD, S])
        proj2(nc, T)
        convs(nc, T)
        stick_attention(nc, T)
        if dbg:
            dbg(nc, T, "y")
        out_proj(nc, T, lambda n: T.d["wout2"][n], False, "2")
    layer_norm_features(nc, T)
    sb = lambda n, s, t=F32: ctx.enter_context(nc.sbuf_tensor(n, s, t))
    T.xtok = sb("xtok", [P, TT, D])
    T.idx = sb("idx", [P, TT, NSEL], U32)
    T.gates = sb("gates", [P, TT, NSEL])
    with ExitStack() as c3:
        T.topv = c3.enter_context(nc.sbuf_tensor("topv", [P, 2 * PH, TT, TOP], F32))
        T.topi = c3.enter_context(nc.sbuf_tensor("topi", [P, 2 * PH, TT, TOP], F32))
        peer_keys(nc, T)
        peer_choice(nc, T)
    if dbg:
        dbg(nc, T, "xtok")
        dbg(nc, T, "idx")
        dbg(nc, T, "gates")
    peer_experts(nc, T)


def constants():
    c = np.zeros((P, C_ALL), np.float32)
    rope = np.zeros((P, 4 * S), np.float32)
    p = np.arange(P)
    c[:, C_IDENT:C_IDENT + P] = np.eye(P)
    c[:, C_ONES:C_ONES + P] = 1.0 / D
    c[:, C_BLK:C_BLK + P] = (p[:, None] // HD == p[None] // HD) / HD
    c[:, C_MASK:C_MASK + P] = np.where(p[None] <= p[:, None], 0.0, NEG)
    c[:, C_STRICT:C_STRICT + P] = p[None] < p[:, None]
    c[:, C_BLK256:C_BLK256 + P] = 1.0 / 256
    for at, cos, sin, half in ((C_ROTD, C_COSD, C_SIND, 16), (C_ROTN, C_COSN, C_SINN, 32)):
        inv = np.float32(10000.0) ** (-np.arange(half, dtype=np.float32) / np.float32(half))
        ang = np.arange(S, dtype=np.float32)[:, None] * inv[None].astype(np.float32)
        rope[:, cos:cos + S] = np.cos(ang)[:, p % half].T
        rope[:, sin:sin + S] = np.sin(ang)[:, p % half].T
        low = p % (2 * half) < half
        rot = np.zeros((P, P), np.float32)
        rot[p[low], p[low] + half] = -1.0
        rot[p[~low], p[~low] - half] = 1.0
        c[:, at:at + P] = rot.T
    q = np.arange(TT)[None, :, None] * P + p[:, None, None]
    ok = 16 * np.arange(NC)[None, None] + 31 <= q
    c[:, C_CADD:C_CADD + TT * NC] = np.where(ok, 0.0, NEG).reshape(P, -1)
    c[:, C_CMUL:C_CMUL + TT * NC] = ok.reshape(P, -1)
    for l in range(L):
        li = 0.8 - 0.6 * math.exp(-0.3 * l)
        c[:, C_LAM + 2 * l] = li
        c[:, C_LAM + 2 * l + 1] = 1.0 - li
    for t in range(16):
        for a in range(2):
            win = np.where(p < 64, (2, 8)[a], (4, 16)[a])
            c[:, C_INVC + 16 * a + t] = 1.0 / np.minimum(t + 1, win)
    c[:, C_IOTA:C_IOTA + 16] = np.arange(16)[None]
    return c, rope


def tiles(w, cols):
    k, n = w.shape[0] // P, len(cols) // P
    return w[:, cols].reshape(k, P, n, P).transpose(2, 1, 0, 3).reshape(n, P, k * P)


def columns(v):
    return v.reshape(-1, P).T


def layouts(i):
    a = {}
    c = np.ascontiguousarray
    a["const"], a["rope"] = constants()
    a["xT"] = c(i["x"][0].T.reshape(KD, P, S).transpose(1, 0, 2))
    a["c"] = c(np.broadcast_to(i["c"], (P, D)))
    a["ada"] = c(i["w_ada"].transpose(0, 2, 1).reshape(L, 36, 2, P, D).transpose(0, 1, 3, 2, 4))
    alln = np.arange
    a["gu"] = c(np.stack([np.stack([tiles(i[w][l, f], alln(FF)) for w in ("ffn_w_gate", "ffn_w_up")], 1)
                          for l in range(L) for f in range(2)]))
    a["dn"] = c(np.stack([tiles(i["ffn_w_down"][l, f], alln(D)) for l in range(L) for f in range(2)]))
    par = np.zeros((L, P, P_ALL), np.float32)
    for l in range(L):
        par[l, :, P_BADA:P_BADA + 72] = columns(i["b_ada"][l])
        for n in range(3):
            par[l, :, P_NG + 8 * n:P_NG + 8 * n + 8] = columns(i["norm_g"][l, n])
        par[l, :, P_LNG:P_LNG + 256] = i["gm_ln_g"][l][None]
        par[l, :, P_BS:P_BS + 256] = np.repeat(i["gm_b_s"][l].reshape(2, 2, P), 64, axis=1).transpose(1, 0, 2).reshape(P, 256)
        par[l, :, P_SUBG] = np.tile(i["da_sub_g"][l], 2)
        par[l, :, P_LAMV:P_LAMV + 128] = i["da_lambda"][l].reshape(1, 128)
        par[l, :, P_PE:P_PE + 32] = i["nsa_cmp_pe"][l].reshape(2, 16, 2, HD).transpose(2, 3, 0, 1).reshape(P, 32)
    a["par"] = par
    r = np.arange
    o = 1280
    q = [np.concatenate([r(o + 64 * t, o + 64 * t + 64), r(o + 64 * (t + 4), o + 64 * (t + 4) + 64)]) for t in range(4)]
    dup = lambda s: np.concatenate([r(s, s + 64)] * 2 + [r(s + 64, s + 128)] * 2)
    zc = np.concatenate([r(0, 256), r(512, 768), r(768, 1024)] + q + [dup(1792), dup(1920), r(2048, 2176), r(2304, 2432)])
    a["win"] = c(np.stack([tiles(i["w_in"][l], zc) for l in range(L)]))
    tc = np.concatenate([r(256, 512), r(1024, 1280), r(2176, 2304), r(2432, 2560), r(2560, 2584)])
    a["wtok"] = c(i["w_in"][:, :, tc].reshape(L, KD, P, NTOK).transpose(0, 2, 1, 3))
    a["ws"] = c(i["gm_w_s"].transpose(0, 3, 1, 2))
    a["w1"] = c(i["nsa_cmp_w1"].reshape(L, 2, 16, P, 256).transpose(0, 3, 1, 2, 4))
    w2 = i["nsa_cmp_w2"].reshape(L, 2, 2, P, HD).transpose(0, 3, 1, 2, 4)
    a["w2"] = c(w2)
    a["w2d"] = c(np.concatenate([w2[:, :, 0], w2[:, :, 0]], -1))
    yr = np.concatenate([r(0, 512)] + [x - o + 512 for x in q])
    a["wout"] = c(np.stack([tiles(i["w_out"][l][yr], r(D)) for l in range(L)]))
    p2(i, a)
    return a


def p2(i, a):
    c = np.ascontiguousarray
    r = np.arange
    q1 = np.zeros((P, Q_ALL), np.float32)
    q1[:, Q_CAW:Q_CAW + 62] = i["conv_a_w_2"][0].reshape(31, 2, P).transpose(2, 1, 0).reshape(P, 62)
    q1[:, Q_CCW:Q_CCW + 6] = i["conv_c_w_2"][0].reshape(3, 2, P).transpose(2, 1, 0).reshape(P, 6)
    for at, n in ((Q_CAB, "conv_a_b_2"), (Q_NG, "norm_a_g_2"), (Q_NB, "norm_a_b_2"), (Q_PSC, "pool_scale_2"),
                  (Q_L1G, "ln1_g_2"), (Q_L1B, "ln1_b_2")):
        v = columns(i[n][0])
        q1[:, at:at + v.shape[1]] = v
    q1[:, Q_FG:Q_FG + 8] = columns(i["final_g"])
    a["q1"] = q1
    w = i["w_in_2"][0]
    a["win2"] = c(tiles(w, r(2048)))
    a["wtok2"] = c(w[:, 2048:].reshape(KD, P, 256).transpose(1, 0, 2))
    a["pw"] = c(i["pool_w_2"][0].reshape(2, P, HD).transpose(1, 0, 2))
    a["wout2"] = c(tiles(i["w_out_2"][0], r(D)))
    a["wq"] = c(tiles(i["peer_wq_2"][0], r(2048)))
    a["keys"] = c(i["peer_keys_2"][0].transpose(3, 0, 1, 2).reshape(P, 16, KEYS))
    a["u"] = i["peer_u_2"][0]
    a["v"] = i["peer_v_2"][0]
    a["ln2"] = c(np.broadcast_to(np.stack([i["ln2_g_2"][0], i["ln2_b_2"][0]])[None], (P, 2, D)))


def kernel(**inputs):
    from concourse import bacc
    from concourse.bass_utils import run_bass_kernel_spmd

    nc = bacc.Bacc("TRN2", target_bir_lowering=False, num_devices=1)
    arrays, d = {}, {}
    for n, v in layouts({k: np.asarray(v) for k, v in inputs.items()}).items():
        arrays["in_" + n] = v
        d[n] = nc.dram_tensor("in_" + n, v.shape, F32, kind="ExternalInput").ap()
    d["out"] = nc.dram_tensor("out", (TT, P, D), F32, kind="ExternalOutput").ap()
    build(nc, d)
    got = run_bass_kernel_spmd(nc, [arrays], core_ids=[0])
    return got.results[0]["out"].reshape(1, S, D)
```

```python
import math
from contextlib import ExitStack

import numpy as np
import concourse.bass as bass
from concourse import mybir

F32 = mybir.dt.float32
U32 = mybir.dt.uint32
F32R = mybir.dt.float32r
ALU = mybir.AluOpType
ACT = mybir.ActivationFunctionType
X = mybir.AxisListType.X

P = 128
D = 1024
S = 512
L = 2
KD = D // P
TT = S // P
FF = 2816
KF = FF // P
HD = 64
NMOD = 9
NC = (S - 32) // 16 + 1
EPS = 1e-6
LN_EPS = 1e-5
NEG = -1e30
ALPHA = 2 ** 0.25
KEYS = 128
TOP = 16
PH = 8
NSEL = PH * TOP

C_IDENT, C_ONES, C_BLK, C_MASK, C_ROTD, C_ROTN = 0, 128, 256, 384, 512, 640
C_CADD, C_CMUL, C_LAM, C_STRICT, C_BLK256, C_INVC, C_IOTA = 768, 892, 1016, 1020, 1148, 1276, 1308
C_ALL = 1324
C_COSD, C_SIND, C_COSN, C_SINN = 0, 512, 1024, 1536

P_BADA, P_NG, P_LNG, P_BS, P_SUBG, P_LAMV, P_PE, P_ALL = 0, 72, 96, 352, 608, 609, 737, 769
Q_CAW, Q_CAB, Q_NG, Q_NB, Q_PSC, Q_CCW, Q_L1G, Q_L1B, Q_FG, Q_ALL = 0, 62, 64, 66, 68, 70, 76, 84, 92, 100

GU, DQ, DK, NQ, KC, VC, KS, KW, NZ = 0, 2, 4, 6, 10, 12, 14, 15, 16
TG, TD, TVS, TVW, TGT, NTOK = 0, 256, 512, 640, 768, 792


class Chain:

    def __init__(self, eng, sem, passed=None):
        self.eng, self.sem, self.base, self.n, self.passed = eng, sem, 0, 0, passed

    def __call__(self, ins):
        self.add(ins)
        self.wait()

    def add(self, ins):
        ins.then_inc(self.sem, 1)
        self.n += 1

    def wait(self):
        self.eng.wait_ge(self.sem, self.base + self.n)
        if self.passed is not None:
            self.eng.sem_inc(self.passed, 1)

    def enter(self, i, per):
        self.outer, self.n, self.per = self.n, 0, per
        self.base = i * per + self.outer

    def leave(self, turns):
        assert self.n == self.per, (self.n, self.per)
        self.base, self.n = 0, self.outer + turns * self.per


def semaphores(nc, ctx, names):
    sems = {}
    for n in names.split():
        n, _, many = n.partition("*")
        own = [ctx.enter_context(nc.semaphore(f"{n}{k}" if many else n)) for k in range(int(many or 1))]
        sems[n] = own if many else own[0]
    return sems


def clear(nc, sems):
    with nc.Block() as block:
        @block.sync
        def _(sp):
            for own in sems.values():
                for s in own if isinstance(own, list) else [own]:
                    sp.sem_clear(s)


def load_constants(nc, T):
    with ExitStack() as ctx:
        M = semaphores(nc, ctx, "lc_loaded lc_silu")
        with nc.Block() as block:
            @block.sync
            def _(sp):
                sp.dma_start(T.const[:, :], T.d["const"]).then_inc(M["lc_loaded"], 16)
                sp.dma_start(T.xT[:, :, :], T.d["xT"]).then_inc(M["lc_loaded"], 16)
                sp.dma_start(T.crow[:, :], T.d["c"]).then_inc(M["lc_loaded"], 16)
                sp.dma_start(T.q1[:, :], T.d["q1"]).then_inc(M["lc_loaded"], 16)

            @block.vector
            def _(dve):
                nc.vector.memset(T.eps[:, 0:1], EPS)
                nc.vector.memset(T.eps[:, 1:2], LN_EPS)
                nc.vector.memset(T.zero[:, :], 0.0)

            @block.scalar
            def _(act):
                act.wait_ge(M["lc_loaded"], 64)
                nc.scalar.activation(T.crow[:, :], T.crow[:, :], ACT.Silu).then_inc(M["lc_silu"], 1)
                act.wait_ge(M["lc_silu"], 1)
        clear(nc, M)


def mod_dots(nc, T, sp, dve, M, wrow, prod, some, layer, col0, turns, per):
    RING = 3

    def load(i):
        for j in range(per // 2):
            sp.wait_ge(M["m_dot"], i * per + 2 * j + 2)
            sp.sem_inc(M["m_passed"], 1)
            sp.dma_start(wrow[:, j % RING], T.d["ada"][layer, i * (per // 2) + (col0 // 2 + j)]
                         ).then_inc(M["m_row"][j % RING], 16)

    def dots(i):
        for j in range(per // 2):
            dve.wait_ge(M["m_row"][j % RING], i * (16 * (per // 2 // RING)) + 16 * (j // RING) + 16)
            for h in range(2):
                dve.wait_ge(M["m_dot"], i * per + 2 * j + h + 2 * RING)
                nc.vector.tensor_tensor_reduce(prod[:, :], wrow[:, j % RING, h], T.crow[:, :], 1.0, 0.0,
                                               ALU.mult, ALU.add,
                                               some[:, 2 * j + h:2 * j + h + 1]).then_inc(M["m_dot"], 1)
        dve.wait_ge(M["m_dot"], i * per + per + 2 * RING)
        nc.vector.tensor_copy(T.raw[:, bass.ds(i * per + col0, per)], some[:, 0:per]).then_inc(M["m_raw"], 1)
        dve.wait_ge(M["m_raw"], i + 1)

    return load if sp is not None else dots


def first_modulation(nc, T):
    with ExitStack() as ctx:
        M = semaphores(nc, ctx, "m_row*3 m_dot m_raw m_passed")
        wrow = ctx.enter_context(nc.sbuf_tensor("m0_wrow", [P, 3, 2, D], F32))
        prod = ctx.enter_context(nc.sbuf_tensor("m0_prod", [P, D], F32))
        some = ctx.enter_context(nc.sbuf_tensor("m0_some", [P, 12], F32))
        with nc.Block() as block:
            @block.sync
            def _(sp):
                load = mod_dots(nc, T, sp, None, M, wrow, prod, some, 0, 0, 2, 12)
                with sp.Fori(0, 2) as i:
                    load(i)

            @block.vector
            def _(dve):
                dve.sem_inc(M["m_dot"], 6)
                dots = mod_dots(nc, T, None, dve, M, wrow, prod, some, 0, 0, 2, 12)
                with dve.Fori(0, 2) as i:
                    dots(i)
        clear(nc, M)


def modulation(nc, T, layer, chunks):
    with ExitStack() as ctx:
        M = semaphores(nc, ctx, "mo_par mo_chain mo_lam mo_exp")
        tag = str(chunks[0])
        prod = ctx.enter_context(nc.sbuf_tensor("mo_prod" + tag, [P, 32], F32))
        lt = ctx.enter_context(nc.sbuf_tensor("mo_lt" + tag, [P, 4], F32))
        with nc.Block() as block:
            @block.sync
            def _(sp):
                if 0 in chunks:
                    sp.dma_start(T.par[:, :], T.d["par"][layer]).then_inc(M["mo_par"], 16)

            @block.vector
            def _(dve):
                if 0 in chunks:
                    dve.wait_ge(M["mo_par"], 16)
                link = Chain(dve, M["mo_chain"])
                for n in chunks:
                    c = slice(24 * n, 24 * n + 24)
                    link(nc.vector.tensor_tensor(T.mod[:, c], T.raw[:, c], T.par[:, P_BADA + 24 * n:P_BADA + 24 * n + 24],
                                                 ALU.add))
                    link(nc.vector.scalar_tensor_tensor(
                        T.gain[:, 8 * n:8 * n + 8], T.mod[:, 24 * n + 8:24 * n + 16], 1.0,
                        T.par[:, P_NG + 8 * n:P_NG + 8 * n + 8], ALU.add, ALU.mult))
                    if n != 1:
                        link(nc.vector.tensor_scalar(T.mod[:, 24 * n + 16:24 * n + 24],
                                                     T.mod[:, 24 * n + 16:24 * n + 24], 0.5, None, ALU.mult))
                if 0 not in chunks:
                    return
                lv = T.par[:, P_LAMV:P_LAMV + 128]
                for m in range(2):
                    link(nc.vector.tensor_tensor_reduce(prod[:, 0:32], lv[:, 64 * m:64 * m + 32],
                                                        lv[:, 64 * m + 32:64 * m + 64], 1.0, 0.0,
                                                        ALU.mult, ALU.add, lt[:, m:m + 1]))
                nc.vector.memset(lt[:, 2:3], 0.0).then_inc(M["mo_lam"], 1)
                dve.wait_ge(M["mo_exp"], 1)
                link(nc.vector.tensor_tensor(lt[:, 2:3], lt[:, 0:1], lt[:, 1:2], ALU.subtract))
                link(nc.vector.tensor_tensor(T.lam[:, 0:1], lt[:, 2:3],
                                             T.const[:, bass.ds(layer * 2 + C_LAM, 1)], ALU.add))
                link(nc.vector.tensor_tensor(T.lam[:, 1:2], T.par[:, P_SUBG:P_SUBG + 1],
                                             T.const[:, bass.ds(layer * 2 + C_LAM + 1, 1)], ALU.mult))

            @block.scalar
            def _(act):
                if 0 in chunks:
                    act.wait_ge(M["mo_lam"], 1)
                    nc.scalar.activation(lt[:, 0:2], lt[:, 0:2], ACT.Exp).then_inc(M["mo_exp"], 1)
        clear(nc, M)


W_SEMS = "w_in*4 w_hi w_lo w_mm "


class Weights:
    def __init__(self, nc, ctx, M, tag, kt, w_of):
        self.nc, self.M, self.kt, self.w_of = nc, M, kt, w_of
        self.raw = ctx.enter_context(nc.sbuf_tensor("wraw" + tag, [P, 4, kt * P], F32))
        self.hi = ctx.enter_context(nc.sbuf_tensor("whi" + tag, [P, 2, kt * P], F32R))
        self.lo = ctx.enter_context(nc.sbuf_tensor("wlo" + tag, [P, 2, kt * P], F32R))

    def load(self, sp, i, j):
        sp.wait_ge(self.M["w_lo"], i * 4 + j + 1)
        sp.dma_start(self.raw[:, j], self.w_of(i, j)).then_inc(self.M["w_in"][j], 16)

    def round(self, act, i, j):
        act.wait_ge(self.M["w_in"][j], i * 16 + 16)
        act.wait_ge(self.M["w_mm"], i * 4 + j + 1)
        self.nc.scalar.activation(self.hi[:, j % 2], self.raw[:, j], ACT.Copy).then_inc(self.M["w_hi"], 1)

    def rest(self, pool, i, j):
        pool.wait_ge(self.M["w_hi"], i * 4 + j + 1)
        self.nc.gpsimd.tensor_tensor(self.lo[:, j % 2], self.raw[:, j], self.hi[:, j % 2].bitcast(F32),
                                     ALU.subtract).then_inc(self.M["w_lo"], 1)

    def times(self, pe, i, j, out, xh, xl, k0=0, first=True, last=True):
        pe.wait_ge(self.M["w_lo"], i * 4 + j + 5)
        hi, lo = self.hi[:, j % 2], self.lo[:, j % 2]
        for k in range(self.kt):
            w = slice(k * P, (k + 1) * P)
            self.nc.tensor.matmul(out, hi[:, w], xh[:, k0 + k], start=first and k == 0, stop=False)
            self.nc.tensor.matmul(out, hi[:, w], xl[:, k0 + k], start=False, stop=False)
            mm = self.nc.tensor.matmul(out, lo[:, w], xh[:, k0 + k], start=False, stop=last and k == self.kt - 1)
        mm.then_inc(self.M["w_mm"], 1)


def square_sums(nc, T, act, pe, M, sq, ps, rstd):
    for k in range(KD):
        if act is not None:
            if k >= 2:
                act.wait_ge(M["n_sum"], k - 1)
            nc.scalar.activation(sq[:, k % 2], T.xT[:, k], ACT.Square).then_inc(M["n_sq"], 1)
        if pe is not None:
            pe.wait_ge(M["n_sq"], k + 1)
            nc.tensor.matmul(ps, T.const[:, C_ONES:C_ONES + P], sq[:, k % 2],
                             start=k == 0, stop=k == KD - 1).then_inc(M["n_sum"], 1)
    if act is not None:
        act.wait_ge(M["n_sum"], KD)
        nc.scalar.activation(rstd, ps, ACT.Sqrt, bias=T.eps[:, 0:1]).then_inc(M["n_root"], 1)


N_SEMS = "n_sq n_sum n_root n_rstd n_t n_h n_hi n_lo "


def norm_split(nc, T, M, rstd, tmp, h, hi, lo, gain, shift, act=None, dve=None, pool=None):
    slots = h.shape[1]
    if dve is not None:
        dve.wait_ge(M["n_root"], 1)
        nc.vector.reciprocal(rstd, rstd).then_inc(M["n_rstd"], 1)
        dve.wait_ge(M["n_rstd"], 1)
    for k in range(KD + 1):
        if dve is not None:
            if k < KD:
                if k >= 2:
                    dve.wait_ge(M["n_h"], k - 1)
                nc.vector.tensor_tensor(tmp[:, k % 2], T.xT[:, k], rstd, ALU.mult).then_inc(M["n_t"], 1)
            if k:
                dve.wait_ge(M["n_h"], k)
                nc.vector.tensor_copy(hi[:, k - 1], h[:, (k - 1) % slots]).then_inc(M["n_hi"], 1)
        if act is not None and k < KD:
            act.wait_ge(M["n_t"], k + 1)
            if slots == 2 and k >= 2:
                act.wait_ge(M["n_lo"], k - 1)
            nc.scalar.activation(h[:, k % slots], tmp[:, k % 2], ACT.Identity, scale=gain[:, k:k + 1],
                                 bias=shift[:, k:k + 1]).then_inc(M["n_h"], 1)
        if pool is not None and k < KD:
            pool.wait_ge(M["n_hi"], k + 1)
            nc.gpsimd.tensor_tensor(lo[:, k], h[:, k % slots], hi[:, k].bitcast(F32),
                                    ALU.subtract).then_inc(M["n_lo"], 1)


def split(nc, M, x, hi, lo, act=None, pool=None, n=KD):
    for k in range(n):
        if act is not None:
            nc.scalar.activation(hi[:, k], x[:, k], ACT.Copy).then_inc(M["x_hi"], 1)
        if pool is not None:
            pool.wait_ge(M["x_hi"], k + 1)
            nc.gpsimd.tensor_tensor(lo[:, k], x[:, k], hi[:, k].bitcast(F32), ALU.subtract).then_inc(M["x_lo"], 1)


def ffn_up(nc, T, layer, which, ah, al):
    m = 2 * which
    with ExitStack() as ctx:
        M = semaphores(nc, ctx, N_SEMS + W_SEMS + "f_silu f_prod f_ahi f_act")
        sb = lambda n, s, t=F32: ctx.enter_context(nc.sbuf_tensor(n + str(which), s, t))
        hh = sb("f_hh", [P, KD, S], F32R)
        hl = sb("f_hl", [P, KD, S], F32R)
        rstd = sb("f_rstd", [P, S])
        sg = sb("f_sg", [P, 2, S])
        a32 = sb("f_a32", [P, 2, S])
        h = sb("f_h", [P, 2, S])
        W = Weights(nc, ctx, M, "u" + str(which), KD,
                    lambda i, j: T.d["gu"][layer * 2 + which, i * 2 + j // 2, j % 2])
        psN = ctx.enter_context(nc.psum_tensor("f_psN" + str(which), [P, S], F32))
        ps = ctx.enter_context(nc.psum_tensor("f_ps" + str(which), [P, 4, S], F32))
        norm = (nc, T, M, rstd[:, :], sg, h, hh, hl, T.gain[:, 8 * m:8 * m + 8], T.mod[:, 24 * m:24 * m + 8])
        with nc.Block() as block:
            @block.sync
            def _(sp):
                with sp.Fori(0, KF // 2) as i:
                    for j in range(4):
                        W.load(sp, i, j)

            @block.gpsimd
            def _(pool):
                pool.sem_inc(M["w_lo"], 4)
                norm_split(*norm, pool=pool)
                with pool.Fori(0, KF // 2) as i:
                    for j in range(4):
                        W.rest(pool, i, j)

            @block.scalar
            def _(act):
                square_sums(nc, T, act, None, M, a32, psN[:, :], rstd[:, :])
                norm_split(*norm, act=act)

                def silu(i, g):
                    act.wait_ge(M["w_mm"], i * 4 + 2 * g + 3)
                    act.wait_ge(M["f_prod"], i * 2 + g + 1)
                    nc.scalar.activation(sg[:, g], ps[:, 2 * g], ACT.Silu).then_inc(M["f_silu"], 1)

                with act.Fori(0, KF // 2) as i:
                    W.round(act, i, 0)
                    W.round(act, i, 1)
                    W.round(act, i, 2)
                    silu(i, 0)
                    W.round(act, i, 3)
                    silu(i, 1)

            @block.tensor
            def _(pe):
                pe.sem_inc(M["w_mm"], 2)
                square_sums(nc, T, None, pe, M, a32, psN[:, :], None)
                pe.wait_ge(M["n_lo"], KD)
                with pe.Fori(0, KF // 2) as i:
                    for j in range(4):
                        pe.wait_ge(M["f_prod"], i * 2 + j // 2 + 1)
                        W.times(pe, i, j, ps[:, j], hh, hl)

            @block.vector
            def _(dve):
                dve.sem_inc(M["f_prod"], 2)
                norm_split(*norm, dve=dve)
                with dve.Fori(0, KF // 2) as i:
                    for g in range(2):
                        dve.wait_ge(M["f_silu"], i * 2 + g + 1)
                        dve.wait_ge(M["w_mm"], i * 4 + 2 * g + 4)
                        nc.vector.tensor_tensor(a32[:, g], sg[:, g], ps[:, 2 * g + 1], ALU.mult).then_inc(M["f_prod"], 1)
                        dve.wait_ge(M["f_prod"], i * 2 + g + 3)
                        nc.vector.tensor_copy(ah[:, i * 2 + g], a32[:, g]).then_inc(M["f_ahi"], 1)
                        dve.wait_ge(M["f_ahi"], i * 2 + g + 1)
                        nc.vector.tensor_tensor(al[:, i * 2 + g], a32[:, g], ah[:, i * 2 + g].bitcast(F32),
                                                ALU.subtract).then_inc(M["f_act"], 1)
        clear(nc, M)


def ffn_down(nc, T, layer, which, ah, al):
    gate = T.mod[:, 48 * which + 16:48 * which + 24]
    H = KF // 2
    per = 6 if which else 12
    mod_layer, col0 = (1 - layer, 0) if which else (layer, 24)
    with ExitStack() as ctx:
        M = semaphores(nc, ctx, W_SEMS + "f_res m_row*3 m_dot m_raw m_passed")
        sb = lambda n, s, t=F32: ctx.enter_context(nc.sbuf_tensor(n + str(which), s, t))
        wrow = sb("m_wrow", [P, 3, 2, D])
        prod = sb("m_prod", [P, D])
        some = sb("m_some", [P, 12])
        W = Weights(nc, ctx, M, "d" + str(which), H,
                    lambda i, j: T.d["dn"][layer * 2 + which, i * 2 + j // 2][:, (j % 2) * H * P:(j % 2 + 1) * H * P])
        ps = ctx.enter_context(nc.psum_tensor("f_psD" + str(which), [P, 2, S], F32))
        with nc.Block() as block:
            @block.sync
            def _(sp):
                rows = mod_dots(nc, T, sp, None, M, wrow, prod, some, mod_layer, col0, KD // 2, per)
                with sp.Fori(0, KD // 2) as i:
                    for j in range(4):
                        W.load(sp, i, j)
                    rows(i)

            @block.gpsimd
            def _(pool):
                pool.sem_inc(M["w_lo"], 4)
                with pool.Fori(0, KD // 2) as i:
                    for j in range(4):
                        W.rest(pool, i, j)

            @block.scalar
            def _(act):
                with act.Fori(0, KD // 2) as i:
                    for j in range(4):
                        W.round(act, i, j)

            @block.tensor
            def _(pe):
                pe.sem_inc(M["w_mm"], 2)
                with pe.Fori(0, KD // 2) as i:
                    for j in range(4):
                        pe.wait_ge(M["f_res"], i * 2 + j // 2 + 1)
                        W.times(pe, i, j, ps[:, j // 2], ah, al, k0=(j % 2) * H, first=j % 2 == 0, last=j % 2 == 1)

            @block.vector
            def _(dve):
                dve.sem_inc(M["f_res"], 2)
                dve.sem_inc(M["m_dot"], 6)
                dots = mod_dots(nc, T, None, dve, M, wrow, prod, some, mod_layer, col0, KD // 2, per)
                with dve.Fori(0, KD // 2) as i:
                    dots(i)
                    for g in range(2):
                        dve.wait_ge(M["w_mm"], i * 4 + 2 * g + 4)
                        x = T.xT[:, i * 2 + g]
                        nc.vector.scalar_tensor_tensor(x, ps[:, g], gate[:, bass.ds(i * 2 + g, 1)], x,
                                                       ALU.mult, ALU.add).then_inc(M["f_res"], 1)
        clear(nc, M)


def ffn(nc, T, layer, which):
    with ExitStack() as ctx:
        ah = ctx.enter_context(nc.sbuf_tensor("f_ah" + str(which), [P, KF, S], F32R))
        al = ctx.enter_context(nc.sbuf_tensor("f_al" + str(which), [P, KF, S], F32R))
        ffn_up(nc, T, layer, which, ah, al)
        ffn_down(nc, T, layer, which, ah, al)


def proj(nc, T, layer):
    with ExitStack() as ctx:
        M = semaphores(nc, ctx, N_SEMS + W_SEMS + "p_rope p_wt p_out p_tmm p_tout")
        sb = lambda n, s, t=F32: ctx.enter_context(nc.sbuf_tensor(n, s, t))
        h = sb("p_h", [P, KD, S])
        hh = sb("p_hh", [P, KD, S], F32R)
        hl = sb("p_hl", [P, KD, S], F32R)
        tmp = sb("p_tmp", [P, 2, S])
        rstd = sb("p_rstd", [P, S])
        wt = sb("p_wt", [P, KD, NTOK])
        W = Weights(nc, ctx, M, "p", KD, lambda i, j: T.d["win"][layer, i * 4 + j])
        psN = ctx.enter_context(nc.psum_tensor("p_psN", [P, S], F32))
        psZ = ctx.enter_context(nc.psum_tensor("p_psZ", [P, 4, S], F32))
        psT = ctx.enter_context(nc.psum_tensor("p_psT", [P, 2, S], F32))
        chunks = ((0, 512), (512, NTOK - 512))
        norm = (nc, T, M, rstd[:, :], tmp, h, hh, hl, T.gain[:, 8:16], T.mod[:, 24:32])
        with nc.Block() as block:
            @block.sync
            def _(sp):
                for j in range(4):
                    W.load(sp, 0, j)
                sp.dma_start(wt[:, :, :], T.d["wtok"][layer]).then_inc(M["p_wt"], 16)
                sp.dma_start(T.rope[:, :], T.d["rope"]).then_inc(M["p_rope"], 16)
                with sp.Fori(1, NZ // 4) as i:
                    for j in range(4):
                        W.load(sp, i, j)
                sp.wait_ge(M["p_rope"], 16)

            @block.gpsimd
            def _(pool):
                pool.sem_inc(M["w_lo"], 4)
                norm_split(*norm, pool=pool)
                with pool.Fori(0, NZ // 4) as i:
                    for j in range(4):
                        W.rest(pool, i, j)

            @block.scalar
            def _(act):
                square_sums(nc, T, act, None, M, h[:, 0:2], psN[:, :], rstd[:, :])
                norm_split(*norm, act=act)
                with act.Fori(0, NZ // 4) as i:
                    for j in range(4):
                        W.round(act, i, j)

            @block.tensor
            def _(pe):
                pe.sem_inc(M["w_mm"], 2)
                square_sums(nc, T, None, pe, M, h[:, 0:2], psN[:, :], None)
                pe.wait_ge(M["n_lo"], KD)
                with pe.Fori(0, NZ // 4) as i:
                    for j in range(4):
                        pe.wait_ge(M["p_out"], i * 4 + j + 1)
                        W.times(pe, i, j, psZ[:, j], hh, hl)
                pe.wait_ge(M["p_wt"], 16)
                for t in range(TT):
                    for c, (c0, cn) in enumerate(chunks):
                        if t:
                            pe.wait_ge(M["p_tout"], 2 * (t - 1) + c + 1)
                        for k in range(KD):
                            mm = nc.tensor.matmul(psT[:, c, 0:cn], h[:, k, t * P:(t + 1) * P],
                                                  wt[:, k, c0:c0 + cn], start=k == 0, stop=k == KD - 1)
                        mm.then_inc(M["p_tmm"], 1)

            @block.vector
            def _(dve):
                dve.sem_inc(M["p_out"], 4)
                norm_split(*norm, dve=dve)
                with dve.Fori(0, NZ // 4) as i:
                    for j in range(4):
                        dve.wait_ge(M["w_mm"], i * 4 + j + 3)
                        nc.vector.tensor_copy(T.z[:, i * 4 + j], psZ[:, j]).then_inc(M["p_out"], 1)
                for t in range(TT):
                    for c, (c0, cn) in enumerate(chunks):
                        dve.wait_ge(M["p_tmm"], 2 * t + c + 1)
                        nc.vector.tensor_copy(T.tok[:, t, c0:c0 + cn], psT[:, c, 0:cn]).then_inc(M["p_tout"], 1)
        clear(nc, M)


def rope_gate_cmp(nc, T, layer):
    NR = 10
    with ExitStack() as ctx:
        M = semaphores(nc, ctx, "r_w r_rot r_rope r_ch r_var r_root r_tri r_vn r_gelu r_v r_sg r_sgo r_sig "
                          "c_pe c_mm1 c_silu c_mm2 c_k c_rot c_fin c_ch")
        sb = lambda n, s: ctx.enter_context(nc.sbuf_tensor(n, s, F32))
        t1 = sb("r_t1", [P, 2, S])
        wsT = sb("r_wsT", [P, 4, P])
        st = sb("r_st", [P, 3, 16])
        sqv = sb("r_sqv", [P, TT, 256])
        w1 = sb("c_w1", [P, 2, 16, 256])
        w2 = sb("c_w2", [P, 2, 2, HD])
        w2d = sb("c_w2d", [P, 2, 2 * HD])
        blk = sb("c_blk", [P, 2, 16, 2, NC])
        hid = sb("c_hid", [P, 2, 2, 2, NC])
        kr = sb("c_kr", [P, NC])
        kt = sb("c_kt", [P, 2, NC])
        psR = ctx.enter_context(nc.psum_tensor("r_psR", [P, 2, S], F32))
        psS = ctx.enter_context(nc.psum_tensor("r_psS", [P, 2, S], F32))
        psH = ctx.enter_context(nc.psum_tensor("c_psH", [P, 2, 2 * NC], F32))
        psK = ctx.enter_context(nc.psum_tensor("c_psK", [P, 4, P], F32))
        roped = [DQ, DQ + 1, DK, DK + 1, NQ, NQ + 1, NQ + 2, NQ + 3, KS, KW]
        v = T.tok[:, :, TG:TG + 256]
        with nc.Block() as block:
            @block.sync
            def _(sp):
                sp.dma_start(wsT[:, :, :], T.d["ws"][layer]).then_inc(M["r_w"], 16)
                sp.dma_start(w1[:, :, :, :], T.d["w1"][layer]).then_inc(M["r_w"], 16)
                sp.dma_start(w2[:, :, :, :], T.d["w2"][layer]).then_inc(M["r_w"], 16)
                sp.dma_start(w2d[:, :, :], T.d["w2d"][layer]).then_inc(M["r_w"], 16)

            @block.gpsimd
            def _(pool):
                pool.wait_ge(M["r_w"], 64)
                nc.gpsimd.affine_select(out=wsT[:, :, :], in_=wsT[:, :, :], compare_op=ALU.is_ge, fill=0.0,
                                        base=0, pattern=[[0, 4], [1, P]], channel_multiplier=-1).then_inc(M["r_tri"], 1)
                pool.wait_ge(M["r_tri"], 1)
                made = 0
                for kv, z in ((0, KC), (1, VC)):
                    for g in range(2):
                        src = T.z[:, z + g, :].rearrange("p (c l two) -> p l c two", two=2, l=8)
                        for par in range(2):
                            rows = slice(64 * par, 64 * par + 64)
                            for lo in range(2):
                                if made:
                                    pool.wait_ge(M["c_pe"], made)
                                made += 1
                                col = P_PE + 16 * kv + 8 * lo
                                pos = T.par[rows, col:col + 8].unsqueeze(2).to_broadcast([64, 8, NC])
                                nc.gpsimd.tensor_tensor(blk[rows, kv, 8 * lo:8 * lo + 8, g, :],
                                                        src[rows, :, lo:lo + NC, par], pos,
                                                        ALU.add).then_inc(M["c_pe"], 1)

            @block.scalar
            def _(act):
                nc.scalar.activation(v, v, ACT.Gelu_apprx_tanh).then_inc(M["r_gelu"], 1)
                nc.scalar.activation(T.z[:, GU:GU + 2], T.z[:, GU:GU + 2], ACT.Gelu_apprx_tanh).then_inc(M["r_gelu"], 1)
                nc.scalar.activation(T.tok[:, :, TGT:TGT + 24], T.tok[:, :, TGT:TGT + 24],
                                     ACT.Sigmoid).then_inc(M["r_sig"], 1)
                act.wait_ge(M["r_var"], 1)
                nc.scalar.activation(st[:, 1], st[:, 1], ACT.Sqrt).then_inc(M["r_root"], 1)
                for kv in range(2):
                    act.wait_ge(M["c_mm1"], kv + 1)
                    nc.scalar.activation(hid[:, kv].rearrange("p a g c -> p (a g c)"),
                                         psH[:, :, :].rearrange("p a c -> p (a c)"), ACT.Silu).then_inc(M["c_silu"], 1)

            @block.tensor
            def _(pe):
                for n, z in enumerate(roped):
                    if n >= 2:
                        pe.wait_ge(M["r_rope"], n - 1)
                    r = C_ROTD if n < 4 else C_ROTN
                    nc.tensor.matmul(psR[:, n % 2], T.const[:, r:r + P], T.z[:, z], start=True,
                                     stop=True).then_inc(M["r_rot"], 1)
                pe.wait_ge(M["r_w"], 64)
                pe.wait_ge(M["c_pe"], 16)
                for kv in range(2):
                    if kv:
                        pe.wait_ge(M["c_silu"], 1)
                    for a in range(2):
                        for l in range(16):
                            mm = nc.tensor.matmul(psH[:, a], w1[:, kv, l, a * P:(a + 1) * P],
                                                  blk[:, kv, l].rearrange("p g c -> p (g c)"),
                                                  start=l == 0, stop=l == 15)
                    mm.then_inc(M["c_mm1"], 1)
                pe.wait_ge(M["c_silu"], 2)
                for g in range(2):
                    for a in range(2):
                        nc.tensor.matmul(psK[:, g, 0:NC], w2d[:, a], hid[:, 0, a, g], start=a == 0, stop=a == 1)
                for g in range(2):
                    for a in range(2):
                        mm = nc.tensor.matmul(psK[0:NC, 2 + g, 0:HD], hid[:, 1, a, g], w2[:, 1, a],
                                              start=a == 0, stop=a == 1)
                mm.then_inc(M["c_mm2"], 1)
                pe.wait_ge(M["c_k"], 3)
                nc.tensor.matmul(psH[:, 0, 0:NC], T.const[:, C_ROTN:C_ROTN + P], kr[:, :], start=True,
                                 stop=True).then_inc(M["c_rot"], 1)
                pe.wait_ge(M["r_tri"], 1)
                for t in range(TT):
                    pe.wait_ge(M["r_vn"], t + 1)
                    for g in range(4):
                        mm = nc.tensor.matmul(psS[64 * (g % 2):64 * (g % 2) + 64, g // 2, t * P:(t + 1) * P],
                                              T.tok[:, t, TG + 64 * g:TG + 64 * g + 64], wsT[:, g],
                                              start=True, stop=True)
                mm.then_inc(M["r_sg"], 1)

            @block.vector
            def _(dve):
                link = Chain(dve, M["r_ch"])
                for n, z in enumerate(roped):
                    cos, sin = (C_COSD, C_SIND) if n < 4 else (C_COSN, C_SINN)
                    dve.wait_ge(M["r_rot"], n + 1)
                    link.add(nc.vector.tensor_tensor(t1[:, n % 2], psR[:, n % 2], T.rope[:, sin:sin + S], ALU.mult))
                    link(nc.vector.tensor_tensor(T.z[:, z], T.z[:, z], T.rope[:, cos:cos + S], ALU.mult))
                    nc.vector.tensor_tensor(T.z[:, z], T.z[:, z], t1[:, n % 2], ALU.add).then_inc(M["r_rope"], 1)
                dve.wait_ge(M["r_gelu"], 2)
                v4 = v.rearrange("p t (g d) -> p t g d", g=4)
                mu = st[:, 0].rearrange("p (t g) -> p t g", t=TT)
                va = st[:, 1].rearrange("p (t g) -> p t g", t=TT)
                q4 = sqv[:, :, :].rearrange("p t (g d) -> p t g d", g=4)
                for t in range(TT):
                    link.add(nc.vector.tensor_reduce(mu[:, t], v4[:, t], X, ALU.add))
                link.wait()
                link(nc.vector.tensor_scalar(st[:, 0], st[:, 0], 1.0 / HD, None, ALU.mult))
                for t in range(TT):
                    link.add(nc.vector.tensor_tensor(v4[:, t], v4[:, t],
                                                     mu[:, t].unsqueeze(2).to_broadcast([P, 4, HD]), ALU.subtract))
                link.wait()
                for t in range(TT):
                    link.add(nc.vector.tensor_tensor(q4[:, t], v4[:, t], v4[:, t], ALU.mult))
                link.wait()
                for t in range(TT):
                    link.add(nc.vector.tensor_reduce(va[:, t], q4[:, t], X, ALU.add))
                link.wait()
                nc.vector.tensor_scalar(st[:, 1], st[:, 1], 1.0 / HD, EPS, ALU.mult, ALU.add).then_inc(M["r_var"], 1)
                dve.wait_ge(M["r_root"], 1)
                link(nc.vector.reciprocal(st[:, 2], st[:, 1]))
                rs = st[:, 2].rearrange("p (t g) -> p t g", t=TT)
                lng = T.par[:, P_LNG:P_LNG + 256].rearrange("p (g d) -> p g d", g=4)
                for t in range(TT):
                    link.add(nc.vector.tensor_tensor(v4[:, t], v4[:, t],
                                                     rs[:, t].unsqueeze(2).to_broadcast([P, 4, HD]), ALU.mult))
                link.wait()
                for t in range(TT):
                    nc.vector.tensor_tensor(v4[:, t], v4[:, t], lng, ALU.mult).then_inc(M["r_vn"], 1)
                dve.wait_ge(M["c_mm2"], 1)
                nc.vector.tensor_copy(kr[0:64, :], psK[0:64, 0, 0:NC]).then_inc(M["c_k"], 1)
                nc.vector.tensor_copy(kr[64:128, :], psK[64:128, 1, 0:NC]).then_inc(M["c_k"], 1)
                nc.vector.tensor_copy(T.vcmp[0:NC, :, :], psK[0:NC, 2:4, 0:HD]).then_inc(M["c_k"], 1)
                dve.wait_ge(M["c_rot"], 1)
                dve.wait_ge(M["c_k"], 3)
                ends = slice(31, 31 + 16 * (NC - 1) + 1, 16)
                cosn = T.rope[:, C_COSN:C_COSN + S]
                sinn = T.rope[:, C_SINN:C_SINN + S]
                link.add(nc.vector.tensor_tensor(kt[:, 0], psH[:, 0, 0:NC], sinn[:, ends], ALU.mult))
                link(nc.vector.tensor_tensor(kt[:, 1], kr[:, :], cosn[:, ends], ALU.mult))
                link(nc.vector.tensor_tensor(T.kcmp[:, :], kt[:, 0], kt[:, 1], ALU.add))
                dve.wait_ge(M["r_sg"], 1)
                for a in range(2):
                    b = T.par[:, P_BS + a * P:P_BS + (a + 1) * P]
                    s4 = t1[:, a].rearrange("p (n t) -> p n t", n=TT)
                    link.add(nc.vector.tensor_tensor(s4, psS[:, a].rearrange("p (n t) -> p n t", n=TT),
                                                     b.unsqueeze(1).to_broadcast([P, TT, P]), ALU.add))
                link.wait()
                for a in range(2):
                    link.add(nc.vector.tensor_tensor(T.y[:, a], T.z[:, GU + a], t1[:, a], ALU.mult))
        clear(nc, M)


def soft_attention(nc, T, layer, kind):
    da = kind == "da"
    TILES = 2 if da else 4
    ST = 2 if da else 1
    scale = 32 ** -0.5 if da else 64 ** -0.5
    NP_ = 1 if da else 2
    SLOTS = 4
    LAG = 2
    with ExitStack() as ctx:
        M = semaphores(nc, ctx, "a_st a_vst a_s a_nm a_e a_pr a_ch a_t a_te a_pv a_o a_cs a_cm a_ce a_cp a_ct a_cte")
        sb = lambda n, s: ctx.enter_context(nc.sbuf_tensor(n, s, F32))
        qs = sb("a_q" + kind, [P, S])
        ks = sb("a_k" + kind, [P, S])
        vs = sb("a_v" + kind, [P, TT, 2, HD])
        pb = sb("a_p" + kind, [P, SLOTS, 2, S])
        PT = sb("a_pt" + kind, [P, 2, NP_, TT, S])
        mx = sb("a_mx" + kind, [P, SLOTS, 2])
        nm = sb("a_nm" + kind, [P, SLOTS, 2])
        sm = sb("a_sm" + kind, [P, SLOTS, 2])
        rc = sb("a_rc" + kind, [P, SLOTS, 2])
        cs = sb("a_cs" + kind, [P, TT, NC])
        cst = sb("a_cst" + kind, [P, 3, TT])
        ctp = sb("a_ctp" + kind, [NC, 2, S])
        oT = sb("a_o" + kind, [P, 2, S])
        psS = ctx.enter_context(nc.psum_tensor("a_psS" + kind, [P, 2, 2, S], F32))
        psT = ctx.enter_context(nc.psum_tensor("a_psT" + kind, [P, 2, S], F32))
        psO = ctx.enter_context(nc.psum_tensor("a_psO" + kind, [P, S], F32))
        psC = ctx.enter_context(nc.psum_tensor("a_psC" + kind, [P, S], F32))
        U = 2 * TT
        units = [(r, i) for r in range(2) for i in range(TT)]
        mask = T.const[:, C_MASK:C_MASK + P]
        with nc.Block() as block:
            @block.gpsimd
            def _(pool):
                pool.sem_inc(M["a_st"], 1)
                with pool.Fori(0, TILES) as t:
                    pool.wait_ge(M["a_s"], t * U + 1)
                    if not da:
                        pool.wait_ge(M["a_cs"], t * 2 + 1)
                    pool.wait_ge(M["a_st"], t * ST + 1)
                    if da:
                        nc.gpsimd.tensor_copy(qs[:, :], T.z[:, t + DQ]).then_inc(M["a_st"], 1)
                        pool.wait_ge(M["a_st"], t * ST + 2)
                        nc.gpsimd.tensor_copy(ks[:, :], T.z[:, t + DK]).then_inc(M["a_st"], 1)
                        pool.wait_ge(M["a_pv"], t * 2 + 1)
                        pool.wait_ge(M["a_st"], t * ST + 3)
                        nc.gpsimd.tensor_copy(vs[:, :].rearrange("p t r d -> p t (r d)"),
                                              T.tok[:, :, bass.ds(t * P + TD, P)]).then_inc(M["a_vst"], 1)
                        pool.wait_ge(M["a_vst"], t + 1)
                    else:
                        nc.gpsimd.tensor_copy(qs[:, :], T.z[:, t + NQ]).then_inc(M["a_st"], 1)

            @block.tensor
            def _(pe):
                pe.sem_inc(M["a_pv"], 1)
                pe.sem_inc(M["a_s"], 1)
                if not da:
                    pe.sem_inc(M["a_cs"], 1)
                pe.sem_inc(M["a_t"], 1)
                pe.sem_inc(M["a_ct"], 1)
                with pe.Fori(0, TILES) as t:
                    pe.wait_ge(M["a_st"], t * ST + ST + 1)

                    def cmp_scores(r):
                        if r:
                            pe.wait_ge(M["a_cte"], t * 2 + r + 1)
                        else:
                            pe.wait_ge(M["a_cte"], t * 2 + 1)
                        for i in range(TT):
                            mm = nc.tensor.matmul(psC[:, 32 * i:32 * i + NC],
                                                  qs[64 * r:64 * r + 64, i * P:(i + 1) * P],
                                                  T.kcmp[64 * r:64 * r + 64, :], start=True, stop=True)
                        mm.then_inc(M["a_cs"], 1)

                    def scores(u):
                        r, i = units[u]
                        pe.wait_ge(M["a_e"], t * 2 * U + (2 * (u - 1) if u >= 2 else 0) + 1)
                        n = P * (i + 1)
                        for m in range(2):
                            if da:
                                p0 = 64 * r + 32 * m
                                lhs, rhs = qs[p0:p0 + 32, i * P:(i + 1) * P], ks[p0:p0 + 32, 0:n]
                                tp = (p0, 0)
                            else:
                                p0 = 64 * r
                                lhs = qs[p0:p0 + 64, i * P:(i + 1) * P]
                                rhs = T.z[p0:p0 + 64, (KS, KW)[m], 0:n]
                                tp = (p0, 0)
                            mm = nc.tensor.matmul(psS[:, u % 2, m, 0:n], lhs, rhs, start=True, stop=True,
                                                  tile_position=tp)
                        mm.then_inc(M["a_s"], 1)

                    def turn_probs(u):
                        r, i = units[u]
                        for b in range(NP_):
                            n = NP_ * u + b
                            pe.wait_ge(M["a_pr"], t * NP_ * U + n + 1)
                            if n >= 2:
                                pe.wait_ge(M["a_te"], t * NP_ * U + n - 1 + 1)
                            else:
                                pe.wait_ge(M["a_te"], t * NP_ * U + 1)
                            for k in range(i + 1):
                                mm = nc.tensor.transpose(psT[:, n % 2, k * P:(k + 1) * P],
                                                         pb[:, u % SLOTS, b, k * P:(k + 1) * P],
                                                         T.const[:, C_IDENT:C_IDENT + P])
                            mm.then_inc(M["a_t"], 1)

                    def cmp_turn(r):
                        pe.wait_ge(M["a_cp"], t * 2 + r + 1)
                        for i in range(TT):
                            mm = nc.tensor.transpose(psC[0:NC, i * P:(i + 1) * P], cs[:, i, :],
                                                     T.const[:, C_IDENT:C_IDENT + P])
                        mm.then_inc(M["a_ct"], 1)

                    def values(r):
                        pe.wait_ge(M["a_te"], t * NP_ * U + NP_ * TT * (r + 1) + 1)
                        if da:
                            pe.wait_ge(M["a_vst"], t + 1)
                        pe.wait_ge(M["a_o"], t + 1)
                        o = psO[64 * r:64 * r + 64, :]
                        for b in range(NP_):
                            for k in range(TT):
                                lhs = vs[:, k, r] if da else \
                                    T.tok[:, k, (TVS, TVW)[b] + 64 * r:(TVS, TVW)[b] + 64 * r + 64]
                                mm = nc.tensor.matmul(o[:, k * P:S], lhs, PT[:, r, b, k, k * P:S],
                                                      start=b == 0 and k == 0,
                                                      stop=da and k == TT - 1, skip_group_check=True)
                        if not da:
                            pe.wait_ge(M["a_cte"], t * 2 + r + 2)
                            mm = nc.tensor.matmul(o, T.vcmp[0:NC, r, :], ctp[:, r, :], start=False, stop=True,
                                                  skip_group_check=True)
                        mm.then_inc(M["a_pv"], 1)

                    for u in range(U + LAG):
                        if u < U:
                            scores(u)
                        if not da and u % TT == 0 and u < U:
                            cmp_scores(u // TT)
                        if u >= LAG:
                            turn_probs(u - LAG)
                        if not da and u % TT == 2:
                            cmp_turn(u // TT)
                        if u == TT + LAG:
                            values(0)
                    values(1)

            @block.scalar
            def _(act):
                act.sem_inc(M["a_e"], 1)
                act.sem_inc(M["a_te"], 1)
                with act.Fori(0, TILES) as t:
                    def exps(u):
                        r, i = units[u]
                        n = P * (i + 1)
                        act.wait_ge(M["a_nm"], t * U + u + 1)
                        if u >= SLOTS:
                            act.wait_ge(M["a_t"], t * NP_ * U + NP_ * (u - SLOTS + 1) + 1)
                        else:
                            act.wait_ge(M["a_t"], t * NP_ * U + 1)
                        for m in range(2):
                            nc.scalar.activation(pb[:, u % SLOTS, m, 0:n], psS[:, u % 2, m, 0:n], ACT.Exp,
                                                 bias=nm[:, u % SLOTS, m:m + 1], scale=scale,
                                                 accum_out=sm[:, u % SLOTS, m:m + 1]).then_inc(M["a_e"], 1)

                    def take_turned(u):
                        r, i = units[u]
                        for b in range(NP_):
                            n = NP_ * u + b
                            act.wait_ge(M["a_t"], t * NP_ * U + n + 2)
                            act.wait_ge(M["a_pv"], t * 2 + 1)
                            nc.scalar.activation(PT[:, r, b, 0:i + 1, i * P:(i + 1) * P],
                                                 psT[:, n % 2, 0:(i + 1) * P].rearrange("p (k q) -> p k q", q=P),
                                                 ACT.Copy).then_inc(M["a_te"], 1)

                    for u in range(U + LAG):
                        if u < U:
                            exps(u)
                        if not da and u % TT == 1 and u < U:
                            act.wait_ge(M["a_cm"], t * 2 + u // TT + 1)
                            nc.scalar.activation(cs[:, :, :], cs[:, :, :], ACT.Exp, scale=scale).then_inc(M["a_ce"], 1)
                        if u >= LAG:
                            take_turned(u - LAG)

            @block.vector
            def _(dve):
                dve.sem_inc(M["a_cte"], 1)
                dve.sem_inc(M["a_o"], 1)
                link = Chain(dve, M["a_ch"])
                per = 5 * U if da else 4 * U + 2 * 6
                with dve.Fori(0, TILES) as t:
                    link.enter(t, per)

                    def maxima(u):
                        r, i = units[u]
                        n = P * (i + 1)
                        dve.wait_ge(M["a_s"], t * U + u + 2)
                        d = psS[:, u % 2, :, i * P:n]
                        link(nc.vector.tensor_tensor(d, d, mask.unsqueeze(1).to_broadcast([P, 2, P]), ALU.add))
                        link(nc.vector.tensor_reduce(mx[:, u % SLOTS], psS[:, u % 2, :, 0:n], X, ALU.max))
                        nc.vector.tensor_scalar(nm[:, u % SLOTS], mx[:, u % SLOTS], -scale, None,
                                                ALU.mult).then_inc(M["a_nm"], 1)

                    def weigh(u):
                        r, i = units[u]
                        n = P * (i + 1)
                        dve.wait_ge(M["a_e"], t * 2 * U + 2 * u + 2 + 1)
                        link(nc.vector.reciprocal(rc[:, u % SLOTS], sm[:, u % SLOTS]))
                        if da:
                            link(nc.vector.tensor_tensor(rc[:, u % SLOTS, 1:2], rc[:, u % SLOTS, 1:2], T.lam[:, 0:1], ALU.mult))
                            link(nc.vector.tensor_scalar(pb[:, u % SLOTS, 1, 0:n], pb[:, u % SLOTS, 1, 0:n],
                                                         rc[:, u % SLOTS, 1:2], None, ALU.mult))
                            nc.vector.scalar_tensor_tensor(pb[:, u % SLOTS, 0, 0:n], pb[:, u % SLOTS, 0, 0:n],
                                                           rc[:, u % SLOTS, 0:1], pb[:, u % SLOTS, 1, 0:n],
                                                           ALU.mult, ALU.subtract).then_inc(M["a_pr"], 1)
                        else:
                            link(nc.vector.tensor_tensor(rc[:, u % SLOTS], rc[:, u % SLOTS],
                                                         T.tok[:, i, bass.ds(t * 3 + TGT + 12 * r + 1, 2)], ALU.mult))
                            nc.vector.tensor_scalar(pb[:, u % SLOTS, 0, 0:n], pb[:, u % SLOTS, 0, 0:n],
                                                    rc[:, u % SLOTS, 0:1], None, ALU.mult).then_inc(M["a_pr"], 1)
                            nc.vector.tensor_scalar(pb[:, u % SLOTS, 1, 0:n], pb[:, u % SLOTS, 1, 0:n],
                                                    rc[:, u % SLOTS, 1:2], None, ALU.mult).then_inc(M["a_pr"], 1)

                    def cmp_maxima(r):
                        dve.wait_ge(M["a_cs"], t * 2 + r + 2)
                        dve.wait_ge(M["a_ct"], t * 2 + r + 1)
                        add = T.const[:, C_CADD:C_CADD + TT * NC].rearrange("p (i c) -> p i c", i=TT)
                        sc = psC[:, 0:TT * 32].rearrange("p (i c) -> p i c", i=TT)[:, :, 0:NC]
                        link(nc.vector.tensor_tensor(cs[:, :, :], sc, add, ALU.add))
                        link(nc.vector.tensor_reduce(cst[:, 0], cs[:, :, :], X, ALU.max))
                        nc.vector.tensor_tensor(cs[:, :, :], cs[:, :, :],
                                                cst[:, 0].unsqueeze(2).to_broadcast([P, TT, NC]),
                                                ALU.subtract).then_inc(M["a_cm"], 1)

                    def cmp_weigh(r):
                        dve.wait_ge(M["a_ce"], t * 2 + r + 1)
                        link(nc.vector.tensor_reduce(cst[:, 1], cs[:, :, :], X, ALU.add))
                        link(nc.vector.reciprocal(cst[:, 2], cst[:, 1]))
                        g = T.tok[:, :, bass.ds(t * 3 + TGT + 12 * r, 1)]
                        link(nc.vector.tensor_tensor(cst[:, 2].unsqueeze(2), cst[:, 2].unsqueeze(2), g, ALU.mult))
                        mul = T.const[:, C_CMUL:C_CMUL + TT * NC].rearrange("p (i c) -> p i c", i=TT)
                        link(nc.vector.tensor_tensor(cs[:, :, :], cs[:, :, :], mul, ALU.mult))
                        nc.vector.tensor_tensor(cs[:, :, :], cs[:, :, :],
                                                cst[:, 2].unsqueeze(2).to_broadcast([P, TT, NC]),
                                                ALU.mult).then_inc(M["a_cp"], 1)

                    for u in range(U + 1):
                        if u < U:
                            maxima(u)
                        if not da and u % TT == 0 and u < U:
                            cmp_maxima(u // TT)
                        if u:
                            weigh(u - 1)
                        if not da and u % TT == 1 and u < U:
                            cmp_weigh(u // TT)
                        if not da and u % TT == 3:
                            dve.wait_ge(M["a_ct"], t * 2 + u // TT + 2)
                            dve.wait_ge(M["a_pv"], t * 2 + 1)
                            nc.vector.tensor_copy(ctp[:, u // TT, :], psC[0:NC, :]).then_inc(M["a_cte"], 1)
                    dve.wait_ge(M["a_pv"], t * 2 + 2 + 1)
                    if not da:
                        nc.vector.tensor_copy(T.y[:, t + 4], psO[:, :]).then_inc(M["a_o"], 1)
                    else:
                        nc.vector.tensor_copy(oT[:, t], psO[:, :]).then_inc(M["a_o"], 1)
                    link.leave(TILES)
        clear(nc, M)
        if not da:
            return
        N = semaphores(nc, ctx, "b_sq b_mm b_root b_ch")
        with nc.Block() as block:
            @block.scalar
            def _(act):
                for a in range(2):
                    nc.scalar.activation(pb[:, 0, a], oT[:, a], ACT.Square).then_inc(N["b_sq"], 1)
                for a in range(2):
                    act.wait_ge(N["b_mm"], a + 1)
                    nc.scalar.activation(pb[:, 1, a], psS[:, 0, a], ACT.Sqrt,
                                         bias=T.eps[:, 0:1]).then_inc(N["b_root"], 1)

            @block.tensor
            def _(pe):
                for a in range(2):
                    pe.wait_ge(N["b_sq"], a + 1)
                    nc.tensor.matmul(psS[:, 0, a], T.const[:, C_BLK:C_BLK + P], pb[:, 0, a], start=True,
                                     stop=True).then_inc(N["b_mm"], 1)

            @block.vector
            def _(dve):
                link = Chain(dve, N["b_ch"])
                for a in range(2):
                    dve.wait_ge(N["b_root"], a + 1)
                    link(nc.vector.reciprocal(pb[:, 1, a], pb[:, 1, a]))
                    link(nc.vector.scalar_tensor_tensor(T.y[:, 2 + a], oT[:, a], T.lam[:, 1:2], pb[:, 1, a],
                                                        ALU.mult, ALU.mult))
        clear(nc, N)


def out_proj(nc, T, w_of, first, tag):
    with ExitStack() as ctx:
        M = semaphores(nc, ctx, W_SEMS + "x_hi x_lo o_res")
        yh = ctx.enter_context(nc.sbuf_tensor("o_yh" + tag, [P, KD, S], F32R))
        yl = ctx.enter_context(nc.sbuf_tensor("o_yl" + tag, [P, KD, S], F32R))
        W = Weights(nc, ctx, M, "o" + tag, KD, lambda i, j: w_of(i * 4 + j))
        ps = ctx.enter_context(nc.psum_tensor("o_ps" + tag, [P, 4, S], F32))
        with nc.Block() as block:
            @block.sync
            def _(sp):
                with sp.Fori(0, KD // 4) as i:
                    for j in range(4):
                        W.load(sp, i, j)

            @block.scalar
            def _(act):
                split(nc, M, T.y, yh, yl, act=act)
                with act.Fori(0, KD // 4) as i:
                    for j in range(4):
                        W.round(act, i, j)

            @block.gpsimd
            def _(pool):
                pool.sem_inc(M["w_lo"], 4)
                split(nc, M, T.y, yh, yl, pool=pool)
                with pool.Fori(0, KD // 4) as i:
                    for j in range(4):
                        W.rest(pool, i, j)

            @block.tensor
            def _(pe):
                pe.sem_inc(M["w_mm"], 2)
                pe.wait_ge(M["x_lo"], KD)
                with pe.Fori(0, KD // 4) as i:
                    for j in range(4):
                        pe.wait_ge(M["o_res"], i * 4 + j + 1)
                        W.times(pe, i, j, ps[:, j], yh, yl)

            @block.vector
            def _(dve):
                dve.sem_inc(M["o_res"], 4)
                with dve.Fori(0, KD // 4) as i:
                    for j in range(4):
                        dve.wait_ge(M["w_mm"], i * 4 + j + 3)
                        xt = T.xT[:, i * 4 + j]
                        if first:
                            nc.vector.scalar_tensor_tensor(xt, ps[:, j], T.mod[:, bass.ds(i * 4 + j + 40, 1)],
                                                           xt, ALU.mult, ALU.add).then_inc(M["o_res"], 1)
                        else:
                            nc.vector.scalar_tensor_tensor(xt, xt, ALPHA, ps[:, j],
                                                           ALU.mult, ALU.add).then_inc(M["o_res"], 1)
        clear(nc, M)


def final_norm(nc, T):
    with ExitStack() as ctx:
        M = semaphores(nc, ctx, "n_sq n_sum n_root n_rstd n_t n_h")
        sb = lambda n, s: ctx.enter_context(nc.sbuf_tensor(n, s, F32))
        sq = sb("z_sq", [P, 2, S])
        tmp = sb("z_tmp", [P, 2, S])
        rstd = sb("z_rstd", [P, S])
        psN = ctx.enter_context(nc.psum_tensor("z_psN", [P, S], F32))
        with nc.Block() as block:
            @block.scalar
            def _(act):
                square_sums(nc, T, act, None, M, sq, psN[:, :], rstd[:, :])

            @block.tensor
            def _(pe):
                square_sums(nc, T, None, pe, M, sq, psN[:, :], None)

            @block.vector
            def _(dve):
                dve.wait_ge(M["n_root"], 1)
                nc.vector.reciprocal(rstd[:, :], rstd[:, :]).then_inc(M["n_rstd"], 1)
                dve.wait_ge(M["n_rstd"], 1)
                for k in range(KD):
                    nc.vector.scalar_tensor_tensor(T.xT[:, k], T.xT[:, k], T.q1[:, Q_FG + k:Q_FG + k + 1],
                                                   rstd[:, :], ALU.mult, ALU.mult).then_inc(M["n_h"], 1)
        clear(nc, M)


def proj2(nc, T):
    with ExitStack() as ctx:
        M = semaphores(nc, ctx, W_SEMS + "x_hi x_lo p_wt p_out p_tmm p_tout")
        sb = lambda n, s, t=F32: ctx.enter_context(nc.sbuf_tensor(n, s, t))
        wt = sb("p2_wt", [P, KD, 256])
        xh = sb("p2_xh", [P, KD, S], F32R)
        xl = sb("p2_xl", [P, KD, S], F32R)
        W = Weights(nc, ctx, M, "p2", KD, lambda i, j: T.d["win2"][i * 4 + j])
        psZ = ctx.enter_context(nc.psum_tensor("p2_psZ", [P, 4, S], F32))
        psT = ctx.enter_context(nc.psum_tensor("p2_psT", [P, 2, S], F32))
        with nc.Block() as block:
            @block.sync
            def _(sp):
                with sp.Fori(0, 4) as i:
                    for j in range(4):
                        W.load(sp, i, j)
                sp.dma_start(wt[:, :, :], T.d["wtok2"]).then_inc(M["p_wt"], 16)

            @block.scalar
            def _(act):
                split(nc, M, T.xT, xh, xl, act=act)
                with act.Fori(0, 4) as i:
                    for j in range(4):
                        W.round(act, i, j)

            @block.gpsimd
            def _(pool):
                pool.sem_inc(M["w_lo"], 4)
                split(nc, M, T.xT, xh, xl, pool=pool)
                with pool.Fori(0, 4) as i:
                    for j in range(4):
                        W.rest(pool, i, j)

            @block.tensor
            def _(pe):
                pe.sem_inc(M["w_mm"], 2)
                pe.wait_ge(M["x_lo"], KD)
                with pe.Fori(0, 4) as i:
                    for j in range(4):
                        pe.wait_ge(M["p_out"], i * 4 + j + 1)
                        W.times(pe, i, j, psZ[:, j], xh, xl)
                pe.wait_ge(M["p_wt"], 16)
                for t in range(TT):
                    if t >= 2:
                        pe.wait_ge(M["p_tout"], t - 1)
                    for k in range(KD):
                        mm = nc.tensor.matmul(psT[:, t % 2, 0:256], T.xT[:, k, t * P:(t + 1) * P],
                                              wt[:, k, :], start=k == 0, stop=k == KD - 1)
                    mm.then_inc(M["p_tmm"], 1)

            @block.vector
            def _(dve):
                dve.sem_inc(M["p_out"], 4)
                with dve.Fori(0, 4) as i:
                    for j in range(4):
                        dve.wait_ge(M["w_mm"], i * 4 + j + 3)
                        nc.vector.tensor_copy(T.z[:, i * 4 + j], psZ[:, j]).then_inc(M["p_out"], 1)
                for t in range(TT):
                    dve.wait_ge(M["p_tmm"], t + 1)
                    nc.vector.tensor_copy(T.tok[:, t], psT[:, t % 2, 0:256]).then_inc(M["p_tout"], 1)
        clear(nc, M)


def convs(nc, T):
    A, G, PI, CH, GB, GC = 0, 2, 4, 6, 8, 10
    W31, PADA, PADP, PADC = 31, 32, 16, 2
    with ExitStack() as ctx:
        M = semaphores(nc, ctx, "v_w v_sig v_pad v_ch v_conv v_mu v_sq v_var v_root v_cen v_nrm v_pool v_pmm")
        sb = lambda n, s: ctx.enter_context(nc.sbuf_tensor(n, s, F32))
        u = sb("v_u", [P, 2, PADA + S])
        h = sb("v_h", [P, 2, S])
        sq = sb("v_sq", [P, 2, S])
        rstd = sb("v_rstd", [P, S])
        wa = sb("v_wa", [P, 2, PADP + S])
        wb = sb("v_wb", [P, 2, PADP + S])
        pin = sb("v_pin", [P, 2, PADP + S])
        pooled = sb("v_pooled", [P, 2, S])
        first = sb("v_first", [P, 16])
        cp = sb("v_cp", [P, 2, PADC + S])
        ch = sb("v_ch_", [P, 2, S])
        pw = sb("v_pw", [P, 2, HD])
        psM = ctx.enter_context(nc.psum_tensor("v_psM", [P, 2, S], F32))
        psP = ctx.enter_context(nc.psum_tensor("v_psP", [P, 2, S], F32))
        q1 = T.q1
        with nc.Block() as block:
            @block.sync
            def _(sp):
                sp.dma_start(pw[:, :, :], T.d["pw"]).then_inc(M["v_w"], 16)

            @block.gpsimd
            def _(pool):
                for n, (buf, pad) in enumerate(((u, PADA), (wa, PADP), (wb, PADP), (pin, PADP), (cp, PADC))):
                    if n:
                        pool.wait_ge(M["v_pad"], n)
                    nc.gpsimd.memset(buf[:, :, 0:pad], 0.0).then_inc(M["v_pad"], 1)

            @block.scalar
            def _(act):
                nc.scalar.activation(T.z[:, G:G + 2], T.z[:, G:G + 2], ACT.Sigmoid).then_inc(M["v_sig"], 1)
                act.wait_ge(M["v_cen"], 1)
                for a in range(2):
                    nc.scalar.activation(sq[:, a], h[:, a], ACT.Square).then_inc(M["v_sq"], 1)
                act.wait_ge(M["v_var"], 1)
                nc.scalar.activation(rstd[:, :], psM[:, 1], ACT.Sqrt, bias=T.eps[:, 1:2]).then_inc(M["v_root"], 1)
                act.wait_ge(M["v_nrm"], 2)
                for a in range(2):
                    nc.scalar.activation(T.y[:, a], h[:, a], ACT.Silu, scale=q1[:, Q_NG + a:Q_NG + a + 1],
                                         bias=q1[:, Q_NB + a:Q_NB + a + 1])

            @block.tensor
            def _(pe):
                c256 = T.const[:, C_BLK256:C_BLK256 + P]
                pe.wait_ge(M["v_conv"], 2 * W31)
                for a in range(2):
                    mm = nc.tensor.matmul(psM[:, 0], c256, h[:, a], start=a == 0, stop=a == 1)
                mm.then_inc(M["v_mu"], 1)
                pe.wait_ge(M["v_w"], 16)
                pe.wait_ge(M["v_pool"], 1)
                for a in range(2):
                    for r in (0, 64):
                        mm = nc.tensor.matmul(psP[r:r + 64, a], pw[r:r + 64, a], pooled[r:r + 64, a],
                                              start=True, stop=True)
                mm.then_inc(M["v_pmm"], 1)
                pe.wait_ge(M["v_sq"], 2)
                for a in range(2):
                    mm = nc.tensor.matmul(psM[:, 1], c256, sq[:, a], start=a == 0, stop=a == 1)
                mm.then_inc(M["v_var"], 1)

            @block.vector
            def _(dve):
                link = Chain(dve, M["v_ch"])
                dve.wait_ge(M["v_sig"], 1)
                link(nc.vector.tensor_tensor(u[:, :, PADA:], T.z[:, A:A + 2], T.z[:, G:G + 2], ALU.mult))
                dve.wait_ge(M["v_pad"], 5)
                for n in range(2 * W31):
                    tap, a = divmod(n, 2)
                    src = u[:, a, PADA - 30 + tap:PADA - 30 + tap + S]
                    w = q1[:, Q_CAW + 31 * a + tap:Q_CAW + 31 * a + tap + 1]
                    if tap == 0:
                        ins = nc.vector.tensor_scalar(h[:, a], src, w, q1[:, Q_CAB + a:Q_CAB + a + 1],
                                                      ALU.mult, ALU.add)
                    else:
                        dve.wait_ge(M["v_conv"], n - 1)
                        ins = nc.vector.scalar_tensor_tensor(h[:, a], src, w, h[:, a], ALU.mult, ALU.add)
                    ins.then_inc(M["v_conv"], 1)
                link(nc.vector.tensor_copy(pin[:, :, PADP:], T.z[:, PI:PI + 2]))
                win = ((pin, wa, 1, 0, 0), (wa, wb, 2, 64, 0), (wb, wa, 4, 0, 1), (wa, wb, 8, 64, 1))
                for n, (src, dst, back, r, a) in enumerate(win):
                    link(nc.vector.tensor_tensor(dst[:, :, PADP:], src[:, :, PADP:],
                                                 src[:, :, PADP - back:PADP + S - back], ALU.add))
                    rows = slice(r, r + 64)
                    inv = T.const[rows, C_INVC + 16 * a:C_INVC + 16 * a + 16]
                    link(nc.vector.scalar_tensor_tensor(pooled[rows, a], dst[rows, a, PADP:], inv[:, 15:16],
                                                        T.z[rows, PI + a], ALU.mult, ALU.subtract))
                    link(nc.vector.tensor_tensor(first[rows, :], dst[rows, a, PADP:PADP + 16], inv, ALU.mult))
                    link(nc.vector.tensor_tensor(pooled[rows, a, 0:16], first[rows, :],
                                                 T.z[rows, PI + a, 0:16], ALU.subtract))
                dve.wait_ge(M["v_mu"], 1)
                for a in range(2):
                    link(nc.vector.tensor_tensor(h[:, a], h[:, a], psM[:, 0], ALU.subtract))
                nc.vector.memset(first[:, 0:1], 0.0).then_inc(M["v_cen"], 1)
                nc.vector.memset(first[:, 1:2], 0.0).then_inc(M["v_pool"], 1)
                link(nc.vector.tensor_tensor(cp[:, :, PADC:], T.z[:, GC:GC + 2], T.z[:, CH:CH + 2], ALU.mult))
                for a in range(2):
                    for tap in range(3):
                        src = cp[:, a, tap:tap + S]
                        w = q1[:, Q_CCW + 3 * a + tap:Q_CCW + 3 * a + tap + 1]
                        if tap == 0:
                            link(nc.vector.tensor_scalar(ch[:, a], src, w, None, ALU.mult))
                        else:
                            link(nc.vector.scalar_tensor_tensor(ch[:, a], src, w, ch[:, a], ALU.mult, ALU.add))
                    link(nc.vector.tensor_tensor(T.y[:, 4 + a], ch[:, a], T.z[:, GB + a], ALU.mult))
                dve.wait_ge(M["v_pmm"], 1)
                for a in range(2):
                    link(nc.vector.tensor_scalar(T.y[:, 2 + a], psP[:, a], q1[:, Q_PSC + a:Q_PSC + a + 1], None,
                                                 ALU.mult))
                dve.wait_ge(M["v_root"], 1)
                link(nc.vector.reciprocal(rstd[:, :], rstd[:, :]))
                for a in range(2):
                    nc.vector.tensor_tensor(h[:, a], h[:, a], rstd[:, :], ALU.mult).then_inc(M["v_nrm"], 1)
        clear(nc, M)


def stick_attention(nc, T):
    Q, K = 12, 14
    scale = HD ** -0.5
    H = 2
    with ExitStack() as ctx:
        M = semaphores(nc, ctx, "k_st k_vst k_s k_z k_abs k_exp k_ln k_ch k_cst k_add k_sp k_sub k_w k_lw "
                               "k_p k_t k_te k_pv k_o")
        sb = lambda n, s: ctx.enter_context(nc.sbuf_tensor(n, s, F32))
        qs = sb("k_q", [P, S])
        ks = sb("k_k", [P, S])
        vs = sb("k_v", [P, TT, 2, HD])
        zs = sb("k_zs", [P, H, TT, S])
        e = sb("k_e", [P, H, TT, S])
        sp_ = sb("k_sp", [P, TT, S])
        cum = sb("k_cum", [P, H, TT, S])
        ones = sb("k_ones", [P, S])
        nmask = sb("k_nmask", [P, P])
        tot = sb("k_tot", [P, H, TT])
        PT = sb("k_pt", [P, TT, S])
        psS = ctx.enter_context(nc.psum_tensor("k_psS", [P, TT, S], F32))
        psT = ctx.enter_context(nc.psum_tensor("k_psT", [P, 2, S], F32))
        psO = ctx.enter_context(nc.psum_tensor("k_psO", [P, S], F32))
        strict = T.const[:, C_STRICT:C_STRICT + P]
        with nc.Block() as block:
            @block.gpsimd
            def _(pool):
                pool.sem_inc(M["k_st"], 1)
                with pool.Fori(0, 2) as t:
                    pool.wait_ge(M["k_s"], t * H * TT + 1)
                    pool.wait_ge(M["k_st"], t * 2 + 1)
                    nc.gpsimd.tensor_copy(qs[:, :], T.z[:, t + Q]).then_inc(M["k_st"], 1)
                    pool.wait_ge(M["k_st"], t * 2 + 2)
                    nc.gpsimd.tensor_copy(ks[:, :], T.z[:, t + K]).then_inc(M["k_st"], 1)
                    for r in range(H):
                        b = t * H * TT + r * TT
                        for i in range(TT):
                            n = P * (i + 1)
                            pool.wait_ge(M["k_sp"], b + i + 1)
                            nc.gpsimd.tensor_tensor(zs[:, r, i, 0:n], zs[:, r, i, 0:n], sp_[:, i, 0:n],
                                                    ALU.subtract).then_inc(M["k_sub"], 1)
                        for i in range(TT):
                            d = slice(i * P, (i + 1) * P)
                            pool.wait_ge(M["k_sub"], b + i + 1)
                            if not r and not i:
                                pool.wait_ge(M["k_cst"], 2)
                            nc.gpsimd.tensor_tensor(zs[:, r, i, d], zs[:, r, i, d], nmask[:, :],
                                                    ALU.add).then_inc(M["k_w"], 1)
                        if not r:
                            pool.wait_ge(M["k_pv"], t * H + 1)
                            nc.gpsimd.tensor_copy(vs[:, :, :, :].rearrange("p t r d -> p t (r d)"),
                                                  T.tok[:, :, bass.ds(t * P, P)]).then_inc(M["k_vst"], 1)

            @block.tensor
            def _(pe):
                pe.sem_inc(M["k_s"], 1)
                pe.sem_inc(M["k_pv"], 1)
                pe.sem_inc(M["k_t"], 1)
                with pe.Fori(0, 2) as t:
                    pe.wait_ge(M["k_st"], t * 2 + 2 + 1)
                    for r in range(H):
                        rows = slice(64 * r, 64 * r + 64)
                        for i in range(TT):
                            pe.wait_ge(M["k_z"], (t * H + r) * TT + (i + 1 - TT if r else 0) + 1)
                            nc.tensor.matmul(psS[:, i, 0:P * (i + 1)], qs[rows, i * P:(i + 1) * P],
                                             ks[rows, 0:P * (i + 1)], start=True, stop=True).then_inc(M["k_s"], 1)
                    for r in range(H):
                        rows = slice(64 * r, 64 * r + 64)
                        for i in range(TT):
                            pe.wait_ge(M["k_p"], t * H * TT + r * TT + i + 2)
                            n = r * TT + i
                            if n >= 2:
                                pe.wait_ge(M["k_te"], t * H * TT + n - 1 + 1)
                            else:
                                pe.wait_ge(M["k_te"], t * H * TT + 1)
                            for k in range(i + 1):
                                mm = nc.tensor.transpose(psT[:, n % 2, k * P:(k + 1) * P],
                                                         e[:, r, i, k * P:(k + 1) * P],
                                                         T.const[:, C_IDENT:C_IDENT + P])
                            mm.then_inc(M["k_t"], 1)
                        pe.wait_ge(M["k_te"], t * H * TT + (r + 1) * TT + 1)
                        pe.wait_ge(M["k_vst"], t + 1)
                        pe.wait_ge(M["k_o"], t + 1)
                        for k in range(TT):
                            mm = nc.tensor.matmul(psO[rows, k * P:S], vs[:, k, r], PT[:, k, k * P:S],
                                                  start=k == 0, stop=k == TT - 1, skip_group_check=True)
                        mm.then_inc(M["k_pv"], 1)

            @block.scalar
            def _(act):
                act.sem_inc(M["k_z"], 1)
                act.sem_inc(M["k_te"], 1)
                act.sem_inc(M["k_p"], 1)
                with act.Fori(0, 2) as t:
                    for r in range(H):
                        b = t * H * TT + r * TT
                        if not r:
                            act.wait_ge(M["k_t"], b + 1)
                        for i in range(TT):
                            n = P * (i + 1)
                            act.wait_ge(M["k_s"], b + i + 2)
                            nc.scalar.activation(zs[:, r, i, 0:n], psS[:, i, 0:n], ACT.Copy,
                                                 scale=scale).then_inc(M["k_z"], 1)
                        for i in range(TT):
                            n = P * (i + 1)
                            act.wait_ge(M["k_z"], b + i + 2)
                            nc.scalar.activation(e[:, r, i, 0:n], zs[:, r, i, 0:n], ACT.Abs).then_inc(M["k_abs"], 1)
                        for i in range(TT):
                            n = P * (i + 1)
                            act.wait_ge(M["k_abs"], b + i + 1)
                            nc.scalar.activation(e[:, r, i, 0:n], e[:, r, i, 0:n], ACT.Exp,
                                                 scale=-1.0).then_inc(M["k_exp"], 1)
                        for i in range(TT):
                            n = P * (i + 1)
                            act.wait_ge(M["k_exp"], b + i + 1)
                            nc.scalar.activation(e[:, r, i, 0:n], e[:, r, i, 0:n], ACT.Ln,
                                                 bias=1.0).then_inc(M["k_ln"], 1)
                    for r in range(H):
                        b = t * H * TT + r * TT
                        for i in range(TT):
                            n = P * (i + 1)
                            act.wait_ge(M["k_lw"], b + i + 1)
                            nc.scalar.activation(e[:, r, i, 0:n], cum[:, r, i, 0:n], ACT.Exp,
                                                 bias=tot[:, r, i:i + 1]).then_inc(M["k_p"], 1)
                        for i in range(TT):
                            act.wait_ge(M["k_t"], b + i + 2)
                            act.wait_ge(M["k_pv"], t * H + r + 1)
                            nc.scalar.activation(PT[:, 0:i + 1, i * P:(i + 1) * P],
                                                 psT[:, (r * TT + i) % 2, 0:(i + 1) * P].rearrange(
                                                     "p (k q) -> p k q", q=P), ACT.Copy).then_inc(M["k_te"], 1)

            @block.vector
            def _(dve):
                dve.sem_inc(M["k_o"], 1)
                nc.vector.memset(ones[:, :], 1.0).then_inc(M["k_cst"], 1)
                nc.vector.tensor_scalar(nmask[:, :], strict, 1.0, -NEG, ALU.subtract, ALU.mult).then_inc(M["k_cst"], 1)
                dve.wait_ge(M["k_cst"], 2)
                link = Chain(dve, M["k_ch"])
                with dve.Fori(0, 2) as t:
                    link.enter(t, 2 * H * TT)
                    for r in range(H):
                        b = t * H * TT + r * TT
                        for i in range(TT):
                            n = P * (i + 1)
                            dve.wait_ge(M["k_ln"], b + i + 1)
                            nc.vector.scalar_tensor_tensor(sp_[:, i, 0:n], zs[:, r, i, 0:n], 0.0, e[:, r, i, 0:n],
                                                           ALU.max, ALU.add).then_inc(M["k_add"], 1)
                        for i in range(TT):
                            d = slice(i * P, (i + 1) * P)
                            dve.wait_ge(M["k_add"], b + i + 1)
                            nc.vector.tensor_tensor(sp_[:, i, d], sp_[:, i, d], strict,
                                                    ALU.mult).then_inc(M["k_sp"], 1)
                        dve.wait_ge(M["k_p"], t * H * TT + 1)
                        for i in range(TT):
                            n = P * (i + 1)
                            dve.wait_ge(M["k_sp"], b + i + 1)
                            link.add(nc.vector.tensor_tensor_scan(cum[:, r, i, 0:n], ones[:, 0:n], sp_[:, i, 0:n], 0.0,
                                                                  ALU.mult, ALU.add))
                        link.wait()
                        for i in range(TT):
                            n = P * (i + 1)
                            link.add(nc.vector.tensor_scalar(tot[:, r, i:i + 1], cum[:, r, i, n - 1:n], -1.0, None,
                                                             ALU.mult))
                        link.wait()
                        for i in range(TT):
                            n = P * (i + 1)
                            dve.wait_ge(M["k_w"], b + i + 1)
                            nc.vector.tensor_tensor(cum[:, r, i, 0:n], cum[:, r, i, 0:n], zs[:, r, i, 0:n],
                                                    ALU.add).then_inc(M["k_lw"], 1)
                    dve.wait_ge(M["k_pv"], t * H + H + 1)
                    nc.vector.tensor_copy(T.y[:, t + 6], psO[:, :]).then_inc(M["k_o"], 1)
                    link.leave(2)
        clear(nc, M)


def layer_norm_features(nc, T):
    with ExitStack() as ctx:
        M = semaphores(nc, ctx, "l_mu l_cen l_sq l_sum l_root l_r l_t l_x")
        sb = lambda n, s: ctx.enter_context(nc.sbuf_tensor(n, s, F32))
        sq = sb("l_sqb", [P, 2, S])
        tmp = sb("l_tmp", [P, 2, S])
        rstd = sb("l_rstd", [P, S])
        ps = ctx.enter_context(nc.psum_tensor("l_ps", [P, 2, S], F32))
        ones = T.const[:, C_ONES:C_ONES + P]
        with nc.Block() as block:
            @block.tensor
            def _(pe):
                for k in range(KD):
                    mm = nc.tensor.matmul(ps[:, 0], ones, T.xT[:, k], start=k == 0, stop=k == KD - 1)
                mm.then_inc(M["l_mu"], 1)
                for k in range(KD):
                    pe.wait_ge(M["l_sq"], k + 1)
                    nc.tensor.matmul(ps[:, 1], ones, sq[:, k % 2], start=k == 0,
                                     stop=k == KD - 1).then_inc(M["l_sum"], 1)

            @block.scalar
            def _(act):
                for k in range(KD):
                    act.wait_ge(M["l_cen"], k + 1)
                    if k >= 2:
                        act.wait_ge(M["l_sum"], k - 1)
                    nc.scalar.activation(sq[:, k % 2], T.xT[:, k], ACT.Square).then_inc(M["l_sq"], 1)
                act.wait_ge(M["l_sum"], KD)
                nc.scalar.activation(rstd[:, :], ps[:, 1], ACT.Sqrt, bias=T.eps[:, 1:2]).then_inc(M["l_root"], 1)

            @block.vector
            def _(dve):
                dve.wait_ge(M["l_mu"], 1)
                for k in range(KD):
                    nc.vector.tensor_tensor(T.xT[:, k], T.xT[:, k], ps[:, 0], ALU.subtract).then_inc(M["l_cen"], 1)
                dve.wait_ge(M["l_root"], 1)
                nc.vector.reciprocal(rstd[:, :], rstd[:, :]).then_inc(M["l_r"], 1)
                dve.wait_ge(M["l_r"], 1)
                for k in range(KD):
                    if k >= 2:
                        dve.wait_ge(M["l_x"], k - 1)
                    nc.vector.tensor_tensor(tmp[:, k % 2], T.xT[:, k], rstd[:, :], ALU.mult).then_inc(M["l_t"], 1)
                    dve.wait_ge(M["l_t"], k + 1)
                    nc.vector.tensor_scalar(T.xT[:, k], tmp[:, k % 2], T.q1[:, Q_L1G + k:Q_L1G + k + 1],
                                            T.q1[:, Q_L1B + k:Q_L1B + k + 1], ALU.mult,
                                            ALU.add).then_inc(M["l_x"], 1)
        clear(nc, M)


def peer_keys(nc, T):
    with ExitStack() as ctx:
        M = semaphores(nc, ctx, W_SEMS + "x_hi x_lo e_keys e_passed e_q e_sc e_top e_ch e_x e_xo")
        sb = lambda n, s, t=F32: ctx.enter_context(nc.sbuf_tensor(n, s, t))
        keys = sb("e_keysb", [P, 2 * PH, KEYS])
        q = sb("e_qb", [P, 4, S])
        rest = sb("e_rest", [P, TT, KEYS])
        tv = sb("e_tv", [P, TT, TOP])
        ti = sb("e_ti", [P, TT, TOP], U32)
        xh = sb("e_xh", [P, KD, S], F32R)
        xl = sb("e_xl", [P, KD, S], F32R)
        W = Weights(nc, ctx, M, "e", KD, lambda i, j: T.d["wq"][i * 4 + j])
        psQ = ctx.enter_context(nc.psum_tensor("e_psQ", [P, 4, S], F32))
        psS = ctx.enter_context(nc.psum_tensor("e_psS", [P, 2, S], F32))
        psX = ctx.enter_context(nc.psum_tensor("e_psX", [P, 2, S], F32))
        with nc.Block() as block:
            @block.sync
            def _(sp):
                sp.dma_start(keys[:, :, :], T.d["keys"]).then_inc(M["e_keys"], 16)
                with sp.Fori(0, PH // 2) as i:
                    for j in range(4):
                        W.load(sp, i, j)

            @block.gpsimd
            def _(pool):
                pool.sem_inc(M["w_lo"], 4)
                split(nc, M, T.xT, xh, xl, pool=pool)
                with pool.Fori(0, PH // 2) as i:
                    for j in range(4):
                        W.rest(pool, i, j)

            @block.tensor
            def _(pe):
                pe.sem_inc(M["w_mm"], 2)
                pe.sem_inc(M["e_sc"], 4)
                for k in range(KD):
                    if k >= 2:
                        pe.wait_ge(M["e_xo"], k - 1)
                    for t in range(TT):
                        mm = nc.tensor.transpose(psX[:, k % 2, t * P:(t + 1) * P], T.xT[:, k, t * P:(t + 1) * P],
                                                 T.const[:, C_IDENT:C_IDENT + P])
                    mm.then_inc(M["e_x"], 1)
                pe.wait_ge(M["e_keys"], 16)
                pe.wait_ge(M["x_lo"], KD)
                with pe.Fori(0, PH // 2) as i:
                    def scores(j):
                        pe.wait_ge(M["e_q"], i * 4 + j + 5)
                        pe.wait_ge(M["e_top"], i * 4 + j + 1)
                        for t in range(TT):
                            mm = nc.tensor.matmul(psS[:, j % 2, t * P:(t + 1) * P], q[:, j, t * P:(t + 1) * P],
                                                  keys[:, i * 4 + j], start=True, stop=True)
                        mm.then_inc(M["e_sc"], 1)

                    for j in range(4):
                        pe.wait_ge(M["e_q"], i * 4 + j + 1)
                        W.times(pe, i, j, psQ[:, j], xh, xl)
                        if j:
                            scores(j - 1)
                    scores(3)

            @block.scalar
            def _(act):
                act.sem_inc(M["e_q"], 4)
                split(nc, M, T.xT, xh, xl, act=act)
                for k in range(KD):
                    act.wait_ge(M["e_x"], k + 1)
                    nc.scalar.activation(T.xtok[:, :, k * P:(k + 1) * P],
                                         psX[:, k % 2].rearrange("p (t d) -> p t d", d=P),
                                         ACT.Copy).then_inc(M["e_xo"], 1)
                with act.Fori(0, PH // 2) as i:
                    def queries(j):
                        act.wait_ge(M["w_mm"], i * 4 + j + 3)
                        act.wait_ge(M["e_sc"], i * 4 + j + 1)
                        nc.scalar.activation(q[:, j], psQ[:, j], ACT.Copy).then_inc(M["e_q"], 1)

                    W.round(act, i, 0)
                    W.round(act, i, 1)
                    queries(0)
                    W.round(act, i, 2)
                    queries(1)
                    W.round(act, i, 3)
                    queries(2)
                    queries(3)

            @block.vector
            def _(dve):
                dve.sem_inc(M["e_top"], 2)
                topv = T.topv[:, 0:2 * TT * PH].rearrange("p (t h) k -> p t h k", t=TT)
                topi = T.topi[:, 0:2 * TT * PH].rearrange("p (t h) k -> p t h k", t=TT)
                link = Chain(dve, M["e_ch"], M["e_passed"])
                with dve.Fori(0, PH // 2) as i:
                    link.enter(i, 4 * (5 * TT + 1))
                    for j in range(4):
                        dve.wait_ge(M["e_sc"], i * 4 + j + 5)
                        dve.sem_inc(M["e_passed"], 1)
                        sc = [psS[:, j % 2, t * P:(t + 1) * P] for t in range(TT)]
                        for t in range(TT):
                            link.add(nc.vector.max(tv[:, t, 0:8], sc[t]))
                        link.wait()
                        for t in range(TT):
                            link.add(nc.vector.max_index(ti[:, t, 0:8], tv[:, t, 0:8], sc[t]))
                        for t in range(TT):
                            link.add(nc.vector.match_replace(rest[:, t], tv[:, t, 0:8], sc[t], -3e38))
                        link.wait()
                        for t in range(TT):
                            link.add(nc.vector.max(tv[:, t, 8:16], rest[:, t]))
                        link.wait()
                        for t in range(TT):
                            link.add(nc.vector.max_index(ti[:, t, 8:16], tv[:, t, 8:16], rest[:, t]))
                        link.wait()
                        link.add(nc.vector.tensor_copy(topv[:, :, i * 4 + j], tv[:, :, :]))
                        nc.vector.tensor_copy(topi[:, :, i * 4 + j], ti[:, :, :]).then_inc(M["e_top"], 1)
                        dve.wait_ge(M["e_top"], i * 4 + j + 3)
                    link.leave(PH // 2)
        clear(nc, M)


def choose(nc, T, B, link, dve, M, n):
    full = [P, TOP, TOP]
    link(nc.vector.tensor_copy(B["tv"], T.topv[:, bass.ds(n * 2, 2)]))
    link.add(nc.vector.tensor_tensor(B["cand"].rearrange("p (a b) -> p a b", b=TOP),
                                     B["tv"][:, 0].unsqueeze(2).to_broadcast(full),
                                     B["tv"][:, 1].unsqueeze(1).to_broadcast(full), ALU.add))
    link(nc.vector.tensor_copy(B["ti"], T.topi[:, bass.ds(n * 2, 2)]))
    link(nc.vector.max(B["best"][:, 0:8], B["cand"]))
    link.add(nc.vector.max_index(B["pos"][:, 0:8], B["best"][:, 0:8], B["cand"]))
    link(nc.vector.match_replace(B["rest"], B["best"][:, 0:8], B["cand"], -3e38))
    link(nc.vector.max(B["best"][:, 8:16], B["rest"]))
    link(nc.vector.max_index(B["pos"][:, 8:16], B["best"][:, 8:16], B["rest"]))
    nc.vector.tensor_scalar(B["dif"], B["best"], B["best"][:, 0:1], None, ALU.subtract).then_inc(M["h_dif"], 1)
    link.add(nc.vector.tensor_scalar(B["part"][:, 0], B["pos"], 4, None, ALU.logical_shift_right))
    link(nc.vector.tensor_scalar(B["part"][:, 1], B["pos"], 15, None, ALU.bitwise_and))
    link(nc.vector.tensor_copy(B["partf"], B["part"]))
    eq = B["eq"]
    iota = T.const[:, C_IOTA:C_IOTA + TOP].unsqueeze(1).to_broadcast(full)
    for m in range(2):
        link.add(nc.vector.tensor_tensor(eq[:, m], B["partf"][:, m].unsqueeze(2).to_broadcast(full), iota,
                                         ALU.is_equal))
    link.wait()
    for m in range(2):
        link.add(nc.vector.tensor_tensor(eq[:, m], eq[:, m], B["ti"][:, m].unsqueeze(1).to_broadcast(full),
                                         ALU.mult))
    link.wait()
    link(nc.vector.tensor_reduce(B["key"], eq, X, ALU.add))
    link(nc.vector.scalar_tensor_tensor(B["key"][:, 0], B["key"][:, 0], float(KEYS), B["key"][:, 1],
                                        ALU.mult, ALU.add))
    link.add(nc.vector.tensor_copy(T.idx[:, n], B["key"][:, 0]))
    dve.wait_ge(M["h_exp"], n + 1)
    link(nc.vector.tensor_reduce(B["sum"], B["dif"], X, ALU.add))
    link(nc.vector.reciprocal(B["sum"], B["sum"]))
    link(nc.vector.tensor_scalar(T.gates[:, n], B["dif"], B["sum"], None, ALU.mult))
    dve.sem_inc(M["h_pick"], 1)


CHOOSE_STEPS = 21
LEAD = 2


def peer_experts(nc, T):
    G, SETS = 4, 4
    NG = NSEL // (G * SETS)
    W = G * SETS
    assert NG == PH
    with ExitStack() as ctx:
        M = semaphores(nc, ctx, f"g_idx g_passed g_passed_v g_x g_u*{2 * G} g_v*{W} g_dot g_gelu g_w g_diag "
                                "g_mm g_r g_ln g_al g_ch g_free g_cp g_rt g_out g_fin h_dif h_exp h_pick h_zero")
        sb = lambda n, s, t=F32: ctx.enter_context(nc.sbuf_tensor(n, s, t))
        ub = sb("g_ub", [P, 2, G, D])
        vb = sb("g_vb", [P, SETS, G, D])
        ix = sb("g_ix", [P, SETS, G], U32)
        prod = sb("g_prod", [P, D])
        xrow = sb("g_xrow", [P, D])
        dot = sb("g_dotb", [P, SETS, G])
        wgt = sb("g_wgt", [P, SETS, G])
        diag = sb("g_diagb", [P, SETS, G, P])
        aid = sb("g_aid", [P, P])
        r = sb("g_rb", [P, D])
        lnp = sb("g_lnp", [P, 2, D])
        st = sb("g_st", [P, 2, 6])
        mv = sb("g_mv", [P, 4])
        B = {"tv": sb("h_tv", [P, 2, TOP])[:, :, :], "ti": sb("h_ti", [P, 2, TOP])[:, :, :],
             "cand": sb("h_cand", [P, TOP * TOP])[:, :], "rest": sb("h_rest", [P, TOP * TOP])[:, :],
             "best": sb("h_best", [P, TOP])[:, :], "pos": sb("h_pos", [P, TOP], U32)[:, :],
             "dif": sb("h_difb", [P, TOP])[:, :], "part": sb("h_part", [P, 2, TOP], U32)[:, :, :],
             "partf": sb("h_partf", [P, 2, TOP])[:, :, :], "eq": sb("h_eq", [P, 2, TOP, TOP])[:, :, :, :],
             "key": sb("h_key", [P, 2, TOP])[:, :, :], "sum": sb("h_sum", [P, 1])[:, :]}
        psF = ctx.enter_context(nc.psum_tensor("g_psF", [P, 2, S], F32))
        ident = T.const[:, C_IDENT:C_IDENT + P]
        with nc.Block() as block:
            @block.gpsimd
            def _(pool):
                with pool.Fori(0, TT) as t:
                    with pool.Fori(0, NG) as g:
                        n = t * NG + g
                        pool.wait_ge(M["h_pick"], n + 1)
                        for s in range(SETS):
                            pool.wait_ge(M["g_dot"], n * W + (s + 1) * G)
                            pool.wait_ge(M["g_mm"], n * SETS + s + 1)
                            if s:
                                pool.wait_ge(M["g_idx"], n * SETS + s)
                            nc.gpsimd.tensor_copy(ix[:, s], T.idx[:, n, s * G:s * G + G]).then_inc(M["g_idx"], 1)
                            pool.wait_ge(M["g_idx"], n * SETS + s + 1)
                            pool.sem_inc(M["g_passed"], 1)
                            for k in range(G):
                                nc.gpsimd.indirect_dma_start(
                                    ub[:, s % 2, k], None, T.d["u"],
                                    bass.IndirectOffsetOnAxis(ap=ix[:, s, k:k + 1], axis=0)
                                ).then_inc(M["g_u"][s % 2 * G + k], 16)
                            for k in range(G):
                                nc.gpsimd.indirect_dma_start(
                                    vb[:, s, k], None, T.d["v"],
                                    bass.IndirectOffsetOnAxis(ap=ix[:, s, k:k + 1], axis=0)
                                ).then_inc(M["g_v"][s * G + k], 16)

            @block.sync
            def _(sp):
                sp.sem_inc(M["g_free"], 1)
                sp.dma_start(lnp[:, :, :], T.d["ln2"]).then_inc(M["g_ln"], 16)
                with sp.Fori(0, TT) as t:
                    sp.wait_ge(M["g_fin"], t + 1)
                    sp.dma_start(T.d["out"][t], r[:, :]).then_inc(M["g_out"], 16)
                    sp.wait_ge(M["g_out"], t * 16 + 16)
                    sp.sem_inc(M["g_free"], 1)
                sp.wait_ge(M["g_out"], 16 * TT)

            @block.vector
            def _(dve):
                dve.sem_inc(M["g_dot"], 2 * G)
                dve.sem_inc(M["g_cp"], 1)
                nc.vector.tensor_scalar(aid[:, :], ident, ALPHA, None, ALU.mult).then_inc(M["g_al"], 1)
                nc.vector.memset(T.topv[:, 2 * TT * PH:], 0.0).then_inc(M["h_zero"], 1)
                nc.vector.memset(T.topi[:, 2 * TT * PH:], 0.0).then_inc(M["h_zero"], 1)
                dve.wait_ge(M["h_zero"], 2)
                link = Chain(dve, M["g_ch"], M["g_passed_v"])
                with dve.Fori(0, LEAD) as h:
                    link.enter(h, CHOOSE_STEPS)
                    choose(nc, T, B, link, dve, M, h)
                    link.leave(LEAD)
                dve.wait_ge(M["g_ln"], 16)
                with dve.Fori(0, TT) as t:
                    dve.wait_ge(M["g_dot"], t * (NG * W) + 2 * G)
                    nc.vector.tensor_copy(xrow[:, :], T.xtok[:, t]).then_inc(M["g_x"], 1)
                    dve.wait_ge(M["g_x"], t + 1)
                    dve.sem_inc(M["g_passed_v"], 1)
                    with dve.Fori(0, NG) as g:
                        n = t * NG + g
                        link.base = t * (NG * CHOOSE_STEPS + 7) + (g * CHOOSE_STEPS + LEAD * CHOOSE_STEPS)
                        link.n = 0
                        choose(nc, T, B, link, dve, M, n + LEAD)
                        assert link.n == CHOOSE_STEPS, link.n
                        for s in range(SETS):
                            for k in range(G):
                                dve.wait_ge(M["g_u"][s % 2 * G + k], n * 32 + 16 * (s // 2) + 16)
                                dve.wait_ge(M["g_dot"], n * W + s * G + k + 2 * G)
                                nc.vector.tensor_tensor_reduce(prod[:, :], ub[:, s % 2, k], xrow[:, :], 1.0, 0.0,
                                                               ALU.mult, ALU.add,
                                                               dot[:, s, k:k + 1]).then_inc(M["g_dot"], 1)
                            dve.wait_ge(M["g_gelu"], n * SETS + s + 1)
                            nc.vector.tensor_tensor(wgt[:, s], dot[:, s],
                                                    T.gates[:, n, s * G:s * G + G],
                                                    ALU.mult).then_inc(M["g_w"], 1)
                    link.base, link.n = t * (NG * CHOOSE_STEPS + 7) + (NG + LEAD) * CHOOSE_STEPS, 0
                    dve.wait_ge(M["g_r"], t + 1)
                    for c in range(2):
                        dve.wait_ge(M["g_free"], t + 1)
                        link(nc.vector.tensor_copy(r[:, c * S:(c + 1) * S], psF[:, c]))
                        link(nc.vector.bn_stats(st[:, c], r[:, c * S:(c + 1) * S]))
                    nc.vector.bn_aggr(mv[:, 0:2], st[:, :, :]).then_inc(M["g_cp"], 1)
                    dve.wait_ge(M["g_rt"], t + 1)
                    link(nc.vector.reciprocal(mv[:, 3:4], mv[:, 2:3]))
                    link(nc.vector.tensor_scalar(r[:, :], r[:, :], mv[:, 0:1], mv[:, 3:4], ALU.subtract, ALU.mult))
                    link(nc.vector.tensor_tensor(r[:, :], r[:, :], lnp[:, 0], ALU.mult))
                    nc.vector.tensor_tensor(r[:, :], r[:, :], lnp[:, 1], ALU.add).then_inc(M["g_fin"], 1)
                    assert link.n == 7, link.n

            @block.scalar
            def _(act):
                def exponents(n):
                    act.wait_ge(M["h_dif"], n + 1)
                    nc.scalar.activation(B["dif"], B["dif"], ACT.Exp).then_inc(M["h_exp"], 1)

                with act.Fori(0, LEAD) as h:
                    exponents(h)
                with act.Fori(0, TT) as t:
                    with act.Fori(0, NG) as g:
                        n = t * NG + g
                        exponents(n + LEAD)
                        for s in range(SETS):
                            act.wait_ge(M["g_dot"], n * W + (s + 1) * G + 2 * G)
                            nc.scalar.activation(dot[:, s], dot[:, s], ACT.Gelu_apprx_tanh).then_inc(M["g_gelu"], 1)
                            act.wait_ge(M["g_w"], n * SETS + s + 1)
                            act.wait_ge(M["g_mm"], n * SETS + s + 1)
                            for k in range(G):
                                nc.scalar.activation(diag[:, s, k], ident, ACT.Copy,
                                                     scale=wgt[:, s, k:k + 1]).then_inc(M["g_diag"], 1)
                    act.wait_ge(M["g_cp"], t + 2)
                    nc.scalar.activation(mv[:, 2:3], mv[:, 1:2], ACT.Sqrt, bias=T.eps[:, 1:2]).then_inc(M["g_rt"], 1)

            @block.tensor
            def _(pe):
                pe.sem_inc(M["g_mm"], SETS)
                pe.wait_ge(M["g_al"], 1)
                with pe.Fori(0, TT) as t:
                    pe.wait_ge(M["g_cp"], t + 1)
                    for c in range(2):
                        nc.tensor.matmul(psF[:, c], aid[:, :], T.xtok[:, t, c * S:(c + 1) * S], start=True,
                                         stop=False, skip_group_check=True)
                    with pe.Fori(0, NG) as g:
                        n = t * NG + g
                        for s in range(SETS):
                            for k in range(G):
                                pe.wait_ge(M["g_v"][s * G + k], n * 16 + 16)
                                pe.wait_ge(M["g_diag"], n * W + s * G + k + 1)
                                for c in range(2):
                                    mm = nc.tensor.matmul(psF[:, c], diag[:, s, k], vb[:, s, k, c * S:(c + 1) * S],
                                                          start=False, stop=False, skip_group_check=True)
                            mm.then_inc(M["g_mm"], 1)
                    for c in range(2):
                        mm = nc.tensor.matmul(psF[:, c], T.zero[:, :], T.xtok[:, t, c * S:(c + 1) * S], start=False,
                                              stop=True, skip_group_check=True)
                    mm.then_inc(M["g_r"], 1)


class Tensors:
    pass


def build(nc, d, dbg=None):
    T = Tensors()
    T.d = d
    with ExitStack() as ctx:
        sb = lambda n, s: ctx.enter_context(nc.sbuf_tensor(n, s, F32))
        T.const = sb("const", [P, C_ALL])
        T.xT = sb("xT", [P, KD, S])
        T.q1 = sb("q1", [P, Q_ALL])
        T.eps = sb("eps", [P, 2])
        T.zero = sb("zero", [P, P])
        with ExitStack() as c1:
            s1 = lambda n, s: c1.enter_context(nc.sbuf_tensor(n, s, F32))
            T.crow = s1("crow", [P, D])
            T.par = s1("par", [P, P_ALL])
            T.mod = s1("mod", [P, 72])
            T.gain = s1("gain", [P, 24])
            T.raw = s1("raw", [P, 72])
            T.lam = s1("lam", [P, 2])
            load_constants(nc, T)
            first_modulation(nc, T)
            with nc.Fori(0, L) as layer:
                modulation(nc, T, layer, [0])
                ffn(nc, T, layer, 0)
                modulation(nc, T, layer, [1, 2])
                with ExitStack() as c2:
                    s2 = lambda n, s: c2.enter_context(nc.sbuf_tensor(n, s, F32))
                    T.z = s2("z", [P, NZ, S])
                    T.tok = s2("tok", [P, TT, NTOK])
                    T.kcmp = s2("kcmp", [P, NC])
                    T.vcmp = s2("vcmp", [NC, 2, HD])
                    T.rope = s2("rope", [P, 4 * S])
                    proj(nc, T, layer)
                    T.y = s2("y", [P, KD, S])
                    rope_gate_cmp(nc, T, layer)
                    soft_attention(nc, T, layer, "da")
                    soft_attention(nc, T, layer, "nsa")
                    if dbg:
                        dbg(nc, T, "y")
                    out_proj(nc, T, lambda n: T.d["wout"][layer, n], True, "1")
                ffn(nc, T, layer, 1)
            final_norm(nc, T)
            if dbg:
                dbg(nc, T, "xT")
        second_block(nc, T, ctx, dbg)


def second_block(nc, T, ctx, dbg):
    with ExitStack() as c2:
        s2 = lambda n, s: c2.enter_context(nc.sbuf_tensor(n, s, F32))
        T.z = s2("z2", [P, 16, S])
        T.tok = s2("tok2", [P, TT, 256])
        T.y = s2("y2", [P, KD, S])
        proj2(nc, T)
        convs(nc, T)
        stick_attention(nc, T)
        if dbg:
            dbg(nc, T, "y")
        out_proj(nc, T, lambda n: T.d["wout2"][n], False, "2")
    layer_norm_features(nc, T)
    sb = lambda n, s, t=F32: ctx.enter_context(nc.sbuf_tensor(n, s, t))
    T.xtok = sb("xtok", [P, TT, D])
    T.idx = sb("idx", [P, TT * PH + LEAD, TOP], U32)
    T.gates = sb("gates", [P, TT * PH + LEAD, TOP])
    T.topv = sb("topv", [P, 2 * (TT * PH + LEAD), TOP])
    T.topi = sb("topi", [P, 2 * (TT * PH + LEAD), TOP])
    peer_keys(nc, T)
    if dbg:
        dbg(nc, T, "xtok")
        dbg(nc, T, "idx")
        dbg(nc, T, "gates")
    peer_experts(nc, T)


def constants():
    c = np.zeros((P, C_ALL), np.float32)
    rope = np.zeros((P, 4 * S), np.float32)
    p = np.arange(P)
    c[:, C_IDENT:C_IDENT + P] = np.eye(P)
    c[:, C_ONES:C_ONES + P] = 1.0 / D
    c[:, C_BLK:C_BLK + P] = (p[:, None] // HD == p[None] // HD) / HD
    c[:, C_MASK:C_MASK + P] = np.where(p[None] <= p[:, None], 0.0, NEG)
    c[:, C_STRICT:C_STRICT + P] = p[None] < p[:, None]
    c[:, C_BLK256:C_BLK256 + P] = 1.0 / 256
    for at, cos, sin, half in ((C_ROTD, C_COSD, C_SIND, 16), (C_ROTN, C_COSN, C_SINN, 32)):
        inv = np.float32(10000.0) ** (-np.arange(half, dtype=np.float32) / np.float32(half))
        ang = np.arange(S, dtype=np.float32)[:, None] * inv[None].astype(np.float32)
        rope[:, cos:cos + S] = np.cos(ang)[:, p % half].T
        rope[:, sin:sin + S] = np.sin(ang)[:, p % half].T
        low = p % (2 * half) < half
        rot = np.zeros((P, P), np.float32)
        rot[p[low], p[low] + half] = -1.0
        rot[p[~low], p[~low] - half] = 1.0
        c[:, at:at + P] = rot.T
    q = np.arange(TT)[None, :, None] * P + p[:, None, None]
    ok = 16 * np.arange(NC)[None, None] + 31 <= q
    c[:, C_CADD:C_CADD + TT * NC] = np.where(ok, 0.0, NEG).reshape(P, -1)
    c[:, C_CMUL:C_CMUL + TT * NC] = ok.reshape(P, -1)
    for l in range(L):
        li = 0.8 - 0.6 * math.exp(-0.3 * l)
        c[:, C_LAM + 2 * l] = li
        c[:, C_LAM + 2 * l + 1] = 1.0 - li
    for t in range(16):
        for a in range(2):
            win = np.where(p < 64, (2, 8)[a], (4, 16)[a])
            c[:, C_INVC + 16 * a + t] = 1.0 / np.minimum(t + 1, win)
    c[:, C_IOTA:C_IOTA + 16] = np.arange(16)[None]
    return c, rope


def tiles(w, cols):
    k, n = w.shape[0] // P, len(cols) // P
    return w[:, cols].reshape(k, P, n, P).transpose(2, 1, 0, 3).reshape(n, P, k * P)


def columns(v):
    return v.reshape(-1, P).T


def layouts(i):
    a = {}
    c = np.ascontiguousarray
    a["const"], a["rope"] = constants()
    a["xT"] = c(i["x"][0].T.reshape(KD, P, S).transpose(1, 0, 2))
    a["c"] = c(np.broadcast_to(i["c"], (P, D)))
    a["ada"] = c(i["w_ada"].transpose(0, 2, 1).reshape(L, 36, 2, P, D).transpose(0, 1, 3, 2, 4))
    alln = np.arange
    a["gu"] = c(np.stack([np.stack([tiles(i[w][l, f], alln(FF)) for w in ("ffn_w_gate", "ffn_w_up")], 1)
                          for l in range(L) for f in range(2)]))
    a["dn"] = c(np.stack([tiles(i["ffn_w_down"][l, f], alln(D)) for l in range(L) for f in range(2)]))
    par = np.zeros((L, P, P_ALL), np.float32)
    for l in range(L):
        par[l, :, P_BADA:P_BADA + 72] = columns(i["b_ada"][l])
        for n in range(3):
            par[l, :, P_NG + 8 * n:P_NG + 8 * n + 8] = columns(i["norm_g"][l, n])
        par[l, :, P_LNG:P_LNG + 256] = i["gm_ln_g"][l][None]
        par[l, :, P_BS:P_BS + 256] = np.repeat(i["gm_b_s"][l].reshape(2, 2, P), 64, axis=1).transpose(1, 0, 2).reshape(P, 256)
        par[l, :, P_SUBG] = np.tile(i["da_sub_g"][l], 2)
        par[l, :, P_LAMV:P_LAMV + 128] = i["da_lambda"][l].reshape(1, 128)
        par[l, :, P_PE:P_PE + 32] = i["nsa_cmp_pe"][l].reshape(2, 16, 2, HD).transpose(2, 3, 0, 1).reshape(P, 32)
    a["par"] = par
    r = np.arange
    o = 1280
    q = [np.concatenate([r(o + 64 * t, o + 64 * t + 64), r(o + 64 * (t + 4), o + 64 * (t + 4) + 64)]) for t in range(4)]
    dup = lambda s: np.concatenate([r(s, s + 64)] * 2 + [r(s + 64, s + 128)] * 2)
    zc = np.concatenate([r(0, 256), r(512, 768), r(768, 1024)] + q + [dup(1792), dup(1920), r(2048, 2176), r(2304, 2432)])
    a["win"] = c(np.stack([tiles(i["w_in"][l], zc) for l in range(L)]))
    tc = np.concatenate([r(256, 512), r(1024, 1280), r(2176, 2304), r(2432, 2560), r(2560, 2584)])
    a["wtok"] = c(i["w_in"][:, :, tc].reshape(L, KD, P, NTOK).transpose(0, 2, 1, 3))
    a["ws"] = c(i["gm_w_s"].transpose(0, 3, 1, 2))
    a["w1"] = c(i["nsa_cmp_w1"].reshape(L, 2, 16, P, 256).transpose(0, 3, 1, 2, 4))
    w2 = i["nsa_cmp_w2"].reshape(L, 2, 2, P, HD).transpose(0, 3, 1, 2, 4)
    a["w2"] = c(w2)
    a["w2d"] = c(np.concatenate([w2[:, :, 0], w2[:, :, 0]], -1))
    yr = np.concatenate([r(0, 512)] + [x - o + 512 for x in q])
    a["wout"] = c(np.stack([tiles(i["w_out"][l][yr], r(D)) for l in range(L)]))
    p2(i, a)
    return a


def p2(i, a):
    c = np.ascontiguousarray
    r = np.arange
    q1 = np.zeros((P, Q_ALL), np.float32)
    q1[:, Q_CAW:Q_CAW + 62] = i["conv_a_w_2"][0].reshape(31, 2, P).transpose(2, 1, 0).reshape(P, 62)
    q1[:, Q_CCW:Q_CCW + 6] = i["conv_c_w_2"][0].reshape(3, 2, P).transpose(2, 1, 0).reshape(P, 6)
    for at, n in ((Q_CAB, "conv_a_b_2"), (Q_NG, "norm_a_g_2"), (Q_NB, "norm_a_b_2"), (Q_PSC, "pool_scale_2"),
                  (Q_L1G, "ln1_g_2"), (Q_L1B, "ln1_b_2")):
        v = columns(i[n][0])
        q1[:, at:at + v.shape[1]] = v
    q1[:, Q_FG:Q_FG + 8] = columns(i["final_g"])
    a["q1"] = q1
    w = i["w_in_2"][0]
    a["win2"] = c(tiles(w, r(2048)))
    a["wtok2"] = c(w[:, 2048:].reshape(KD, P, 256).transpose(1, 0, 2))
    a["pw"] = c(i["pool_w_2"][0].reshape(2, P, HD).transpose(1, 0, 2))
    a["wout2"] = c(tiles(i["w_out_2"][0], r(D)))
    a["wq"] = c(tiles(i["peer_wq_2"][0], r(2048)))
    a["keys"] = c(i["peer_keys_2"][0].transpose(3, 0, 1, 2).reshape(P, 16, KEYS))
    a["u"] = i["peer_u_2"][0]
    a["v"] = i["peer_v_2"][0]
    a["ln2"] = c(np.broadcast_to(np.stack([i["ln2_g_2"][0], i["ln2_b_2"][0]])[None], (P, 2, D)))


def kernel(**inputs):
    from concourse import bacc
    from concourse.bass_utils import run_bass_kernel_spmd

    nc = bacc.Bacc("TRN2", target_bir_lowering=False, num_devices=1)
    arrays, d = {}, {}
    for n, v in layouts({k: np.asarray(v) for k, v in inputs.items()}).items():
        arrays["in_" + n] = v
        d[n] = nc.dram_tensor("in_" + n, v.shape, F32, kind="ExternalInput").ap()
    d["out"] = nc.dram_tensor("out", (TT, P, D), F32, kind="ExternalOutput").ap()
    build(nc, d)
    got = run_bass_kernel_spmd(nc, [arrays], core_ids=[0])
    return got.results[0]["out"].reshape(1, S, D)
```

```python
import math
from contextlib import ExitStack

import numpy as np
import concourse.bass as bass
from concourse import mybir

F32 = mybir.dt.float32
U32 = mybir.dt.uint32
F32R = mybir.dt.float32r
ALU = mybir.AluOpType
ACT = mybir.ActivationFunctionType
X = mybir.AxisListType.X

P = 128
D = 1024
S = 512
L = 2
KD = D // P
TT = S // P
FF = 2816
KF = FF // P
HD = 64
NC = (S - 32) // 16 + 1
EPS = 1e-6
LN_EPS = 1e-5
NEG = -1e30
ALPHA = 2 ** 0.25
KEYS = 128
TOP = 16
PH = 8
NSEL = PH * TOP

C_IDENT, C_ONES, C_BLK, C_MASK, C_ROTD, C_ROTN = 0, 128, 256, 384, 512, 640
C_CADD, C_CMUL, C_LAM, C_STRICT, C_BLK256, C_INVC, C_IOTA = 768, 892, 1016, 1020, 1148, 1276, 1308
C_ALL = 1324
C_COSD, C_SIND, C_COSN, C_SINN = 0, 512, 1024, 1536

P_BADA, P_NG, P_LNG, P_BS, P_SUBG, P_LAMV, P_PE, P_ALL = 0, 72, 96, 352, 608, 609, 737, 769
Q_CAW, Q_CAB, Q_NG, Q_NB, Q_PSC, Q_CCW, Q_L1G, Q_L1B, Q_FG, Q_ALL = 0, 62, 64, 66, 68, 70, 76, 84, 92, 100

GU, DQ, DK, NQ, KC, VC, KS, KW, NZ = 0, 2, 4, 6, 10, 12, 14, 15, 16
TG, TD, TVS, TVW, TGT, NTOK = 0, 256, 512, 640, 768, 792


class Chain:

    def __init__(self, eng, sem, passed=None):
        self.eng, self.sem, self.base, self.n, self.passed = eng, sem, 0, 0, passed

    def __call__(self, ins):
        self.add(ins)
        self.wait()

    def add(self, ins):
        ins.then_inc(self.sem, 1)
        self.n += 1

    def wait(self):
        self.eng.wait_ge(self.sem, self.base + self.n)
        if self.passed is not None:
            self.eng.sem_inc(self.passed, 1)

    def enter(self, i, per):
        self.outer, self.n, self.per = self.n, 0, per
        self.base = i * per + self.outer

    def leave(self, turns):
        assert self.n == self.per, (self.n, self.per)
        self.base, self.n = 0, self.outer + turns * self.per


def semaphores(nc, ctx, names):
    sems = {}
    for n in names.split():
        n, _, many = n.partition("*")
        own = [ctx.enter_context(nc.semaphore(f"{n}{k}" if many else n)) for k in range(int(many or 1))]
        sems[n] = own if many else own[0]
    return sems


def clear(nc, sems):
    with nc.Block() as block:
        @block.sync
        def _(sp):
            for own in sems.values():
                for s in own if isinstance(own, list) else [own]:
                    sp.sem_clear(s)


def mod_dots(nc, T, sp, dve, M, wrow, prod, some, layer, col0, turns, per):
    RING = 3

    def load(i):
        for j in range(per // 2):
            sp.wait_ge(M["m_dot"], i * per + 2 * j + 2)
            sp.sem_inc(M["m_passed"], 1)
            sp.dma_start(wrow[:, j % RING], T.d["ada"][layer, i * (per // 2) + (col0 // 2 + j)]
                         ).then_inc(M["m_row"][j % RING], 16)

    def dots(i):
        for j in range(per // 2):
            dve.wait_ge(M["m_row"][j % RING], i * (16 * (per // 2 // RING)) + 16 * (j // RING) + 16)
            for h in range(2):
                dve.wait_ge(M["m_dot"], i * per + 2 * j + h + 2 * RING)
                nc.vector.tensor_tensor_reduce(prod[:, :], wrow[:, j % RING, h], T.crow[:, :], 1.0, 0.0,
                                               ALU.mult, ALU.add,
                                               some[:, 2 * j + h:2 * j + h + 1]).then_inc(M["m_dot"], 1)
        dve.wait_ge(M["m_dot"], i * per + per + 2 * RING)
        nc.vector.tensor_copy(T.raw[:, bass.ds(i * per + col0, per)], some[:, 0:per]).then_inc(M["m_raw"], 1)
        dve.wait_ge(M["m_raw"], i + 1)

    return load if sp is not None else dots


def first_modulation(nc, T):
    with ExitStack() as ctx:
        M = semaphores(nc, ctx, "lc_c lc_silu lc_loaded m_row*3 m_dot m_raw m_passed")
        wrow = ctx.enter_context(nc.sbuf_tensor("m0_wrow", [P, 3, 2, D], F32))
        prod = ctx.enter_context(nc.sbuf_tensor("m0_prod", [P, D], F32))
        some = ctx.enter_context(nc.sbuf_tensor("m0_some", [P, 12], F32))
        with nc.Block() as block:
            @block.sync
            def _(sp):
                sp.dma_start(T.crow[:, :], T.d["c"]).then_inc(M["lc_c"], 16)
                load = mod_dots(nc, T, sp, None, M, wrow, prod, some, 0, 0, 2, 12)
                with sp.Fori(0, 2) as i:
                    load(i)
                sp.dma_start(T.const[:, :], T.d["const"]).then_inc(M["lc_loaded"], 16)
                sp.dma_start(T.xT[:, :, :], T.d["xT"]).then_inc(M["lc_loaded"], 16)
                sp.dma_start(T.q1[:, :], T.d["q1"]).then_inc(M["lc_loaded"], 16)
                sp.wait_ge(M["lc_loaded"], 48)

            @block.scalar
            def _(act):
                act.wait_ge(M["lc_c"], 16)
                nc.scalar.activation(T.crow[:, :], T.crow[:, :], ACT.Silu).then_inc(M["lc_silu"], 1)

            @block.vector
            def _(dve):
                nc.vector.memset(T.eps[:, 0:1], EPS)
                nc.vector.memset(T.eps[:, 1:2], LN_EPS)
                nc.vector.memset(T.zero[:, :], 0.0)
                dve.sem_inc(M["m_dot"], 6)
                dve.wait_ge(M["lc_silu"], 1)
                dots = mod_dots(nc, T, None, dve, M, wrow, prod, some, 0, 0, 2, 12)
                with dve.Fori(0, 2) as i:
                    dots(i)
        clear(nc, M)


def modulation(nc, T, layer, chunks):
    with ExitStack() as ctx:
        M = semaphores(nc, ctx, "mo_par mo_chain mo_lam mo_exp")
        tag = str(chunks[0])
        prod = ctx.enter_context(nc.sbuf_tensor("mo_prod" + tag, [P, 32], F32))
        lt = ctx.enter_context(nc.sbuf_tensor("mo_lt" + tag, [P, 4], F32))
        with nc.Block() as block:
            @block.sync
            def _(sp):
                if 0 in chunks:
                    sp.dma_start(T.par[:, :], T.d["par"][layer]).then_inc(M["mo_par"], 16)

            @block.vector
            def _(dve):
                if 0 in chunks:
                    dve.wait_ge(M["mo_par"], 16)
                link = Chain(dve, M["mo_chain"])
                for n in chunks:
                    c = slice(24 * n, 24 * n + 24)
                    link(nc.vector.tensor_tensor(T.mod[:, c], T.raw[:, c], T.par[:, P_BADA + 24 * n:P_BADA + 24 * n + 24],
                                                 ALU.add))
                    link(nc.vector.scalar_tensor_tensor(
                        T.gain[:, 8 * n:8 * n + 8], T.mod[:, 24 * n + 8:24 * n + 16], 1.0,
                        T.par[:, P_NG + 8 * n:P_NG + 8 * n + 8], ALU.add, ALU.mult))
                    if n != 1:
                        link(nc.vector.tensor_scalar(T.mod[:, 24 * n + 16:24 * n + 24],
                                                     T.mod[:, 24 * n + 16:24 * n + 24], 0.5, None, ALU.mult))
                if 0 not in chunks:
                    return
                lv = T.par[:, P_LAMV:P_LAMV + 128]
                for m in range(2):
                    link(nc.vector.tensor_tensor_reduce(prod[:, 0:32], lv[:, 64 * m:64 * m + 32],
                                                        lv[:, 64 * m + 32:64 * m + 64], 1.0, 0.0,
                                                        ALU.mult, ALU.add, lt[:, m:m + 1]))
                nc.vector.memset(lt[:, 2:3], 0.0).then_inc(M["mo_lam"], 1)
                dve.wait_ge(M["mo_exp"], 1)
                link(nc.vector.tensor_tensor(lt[:, 2:3], lt[:, 0:1], lt[:, 1:2], ALU.subtract))
                link(nc.vector.tensor_tensor(T.lam[:, 0:1], lt[:, 2:3],
                                             T.const[:, bass.ds(layer * 2 + C_LAM, 1)], ALU.add))
                link(nc.vector.tensor_tensor(T.lam[:, 1:2], T.par[:, P_SUBG:P_SUBG + 1],
                                             T.const[:, bass.ds(layer * 2 + C_LAM + 1, 1)], ALU.mult))

            @block.scalar
            def _(act):
                if 0 in chunks:
                    act.wait_ge(M["mo_lam"], 1)
                    nc.scalar.activation(lt[:, 0:2], lt[:, 0:2], ACT.Exp).then_inc(M["mo_exp"], 1)
        clear(nc, M)


W_SEMS = "w_in*4 w_hi w_lo w_mm "


class Weights:
    def __init__(self, nc, ctx, M, tag, kt, w_of):
        self.nc, self.M, self.kt, self.w_of = nc, M, kt, w_of
        self.raw = ctx.enter_context(nc.sbuf_tensor("wraw" + tag, [P, 4, kt * P], F32))
        self.hi = ctx.enter_context(nc.sbuf_tensor("whi" + tag, [P, 2, kt * P], F32R))
        self.lo = ctx.enter_context(nc.sbuf_tensor("wlo" + tag, [P, 2, kt * P], F32R))

    def load(self, sp, i, j):
        sp.wait_ge(self.M["w_lo"], i * 4 + j + 1)
        sp.dma_start(self.raw[:, j], self.w_of(i, j)).then_inc(self.M["w_in"][j], 16)

    def round(self, act, i, j):
        act.wait_ge(self.M["w_in"][j], i * 16 + 16)
        act.wait_ge(self.M["w_mm"], i * 4 + j + 1)
        self.nc.scalar.activation(self.hi[:, j % 2], self.raw[:, j], ACT.Copy).then_inc(self.M["w_hi"], 1)

    def rest(self, pool, i, j):
        pool.wait_ge(self.M["w_hi"], i * 4 + j + 1)
        self.nc.gpsimd.tensor_tensor(self.lo[:, j % 2], self.raw[:, j], self.hi[:, j % 2].bitcast(F32),
                                     ALU.subtract).then_inc(self.M["w_lo"], 1)

    def first(self, step, eng):
        step(eng, 0, 0)
        step(eng, 0, 1)

    def others(self, step, eng, turns):
        if turns > 1:
            with eng.Fori(0, turns - 1) as i:
                step(eng, i, 2)
                step(eng, i, 3)
                step(eng, i + 1, 0)
                step(eng, i + 1, 1)
        step(eng, turns - 1, 2)
        step(eng, turns - 1, 3)

    def times(self, pe, i, j, out, xh, xl, k0=0, first=True, last=True, x_split=None):
        pe.wait_ge(self.M["w_lo"], i * 4 + j + 5)
        hi, lo = self.hi[:, j % 2], self.lo[:, j % 2]
        for k in range(self.kt):
            w = slice(k * P, (k + 1) * P)
            if x_split is not None and j == 0:
                pe.wait_ge(x_split, k0 + k + 1)
            self.nc.tensor.matmul(out, hi[:, w], xh[:, k0 + k], start=first and k == 0, stop=False)
            self.nc.tensor.matmul(out, hi[:, w], xl[:, k0 + k], start=False, stop=False)
            mm = self.nc.tensor.matmul(out, lo[:, w], xh[:, k0 + k], start=False, stop=last and k == self.kt - 1)
        mm.then_inc(self.M["w_mm"], 1)


def square_sums(nc, T, act, pe, M, sq, ps, rstd):
    for k in range(KD):
        if act is not None:
            if k >= 2:
                act.wait_ge(M["n_sum"], k - 1)
            nc.scalar.activation(sq[:, k % 2], T.xT[:, k], ACT.Square).then_inc(M["n_sq"], 1)
        if pe is not None:
            pe.wait_ge(M["n_sq"], k + 1)
            nc.tensor.matmul(ps, T.const[:, C_ONES:C_ONES + P], sq[:, k % 2],
                             start=k == 0, stop=k == KD - 1).then_inc(M["n_sum"], 1)
    if act is not None:
        act.wait_ge(M["n_sum"], KD)
        nc.scalar.activation(rstd, ps, ACT.Sqrt, bias=T.eps[:, 0:1]).then_inc(M["n_root"], 1)


N_SEMS = "n_sq n_sum n_root n_rstd n_t n_h n_hi n_lo "


def norm_split(nc, T, M, rstd, tmp, h, hi, lo, gain, shift, act=None, dve=None, pool=None):
    slots = h.shape[1]
    if dve is not None:
        dve.wait_ge(M["n_root"], 1)
        nc.vector.reciprocal(rstd, rstd).then_inc(M["n_rstd"], 1)
        dve.wait_ge(M["n_rstd"], 1)
    for k in range(KD + 1):
        if dve is not None:
            if k < KD:
                if k >= 2:
                    dve.wait_ge(M["n_h"], k - 1)
                nc.vector.tensor_tensor(tmp[:, k % 2], T.xT[:, k], rstd, ALU.mult).then_inc(M["n_t"], 1)
            if k:
                dve.wait_ge(M["n_h"], k)
                nc.vector.tensor_copy(hi[:, k - 1], h[:, (k - 1) % slots]).then_inc(M["n_hi"], 1)
        if act is not None and k < KD:
            act.wait_ge(M["n_t"], k + 1)
            if slots == 2 and k >= 2:
                act.wait_ge(M["n_lo"], k - 1)
            nc.scalar.activation(h[:, k % slots], tmp[:, k % 2], ACT.Identity, scale=gain[:, k:k + 1],
                                 bias=shift[:, k:k + 1]).then_inc(M["n_h"], 1)
        if pool is not None and k < KD:
            pool.wait_ge(M["n_hi"], k + 1)
            nc.gpsimd.tensor_tensor(lo[:, k], h[:, k % slots], hi[:, k].bitcast(F32),
                                    ALU.subtract).then_inc(M["n_lo"], 1)


def split(nc, M, x, hi, lo, act=None, dve=None, W=None):
    for k in range(KD):
        if act is not None:
            if k == 3:
                W.first(W.round, act)
            nc.scalar.activation(hi[:, k], x[:, k], ACT.Copy).then_inc(M["x_hi"], 1)
        if dve is not None:
            dve.wait_ge(M["x_hi"], k + 1)
            nc.vector.tensor_tensor(lo[:, k], x[:, k], hi[:, k].bitcast(F32), ALU.subtract).then_inc(M["x_lo"], 1)


def ffn_up(nc, T, layer, which, ah, al):
    m = 2 * which
    with ExitStack() as ctx:
        M = semaphores(nc, ctx, N_SEMS + W_SEMS + "f_silu f_prod f_ahi f_act")
        sb = lambda n, s, t=F32: ctx.enter_context(nc.sbuf_tensor(n + str(which), s, t))
        hh = sb("f_hh", [P, KD, S], F32R)
        hl = sb("f_hl", [P, KD, S], F32R)
        rstd = sb("f_rstd", [P, S])
        sg = sb("f_sg", [P, 2, S])
        a32 = sb("f_a32", [P, 2, S])
        h = sb("f_h", [P, 2, S])
        W = Weights(nc, ctx, M, "u" + str(which), KD,
                    lambda i, j: T.d["gu"][layer * 2 + which, i * 2 + j // 2, j % 2])
        psN = ctx.enter_context(nc.psum_tensor("f_psN" + str(which), [P, S], F32))
        ps = ctx.enter_context(nc.psum_tensor("f_ps" + str(which), [P, 4, S], F32))
        norm = (nc, T, M, rstd[:, :], sg, h, hh, hl, T.gain[:, 8 * m:8 * m + 8], T.mod[:, 24 * m:24 * m + 8])
        with nc.Block() as block:
            @block.sync
            def _(sp):
                with sp.Fori(0, KF // 2) as i:
                    for j in range(4):
                        W.load(sp, i, j)

            @block.gpsimd
            def _(pool):
                pool.sem_inc(M["w_lo"], 4)
                W.first(W.rest, pool)
                norm_split(*norm, pool=pool)
                W.others(W.rest, pool, KF // 2)

            @block.scalar
            def _(act):
                W.first(W.round, act)
                square_sums(nc, T, act, None, M, a32, psN[:, :], rstd[:, :])
                norm_split(*norm, act=act)

                def silu(i, g):
                    act.wait_ge(M["w_mm"], i * 4 + 2 * g + 3)
                    act.wait_ge(M["f_prod"], i * 2 + g + 1)
                    nc.scalar.activation(sg[:, g], ps[:, 2 * g], ACT.Silu).then_inc(M["f_silu"], 1)

                def turn(i, more):
                    W.round(act, i, 2)
                    silu(i, 0)
                    W.round(act, i, 3)
                    if more:
                        W.round(act, i + 1, 0)
                    silu(i, 1)
                    if more:
                        W.round(act, i + 1, 1)

                with act.Fori(0, KF // 2 - 1) as i:
                    turn(i, True)
                turn(KF // 2 - 1, False)

            @block.tensor
            def _(pe):
                pe.sem_inc(M["w_mm"], 2)
                square_sums(nc, T, None, pe, M, a32, psN[:, :], None)
                with pe.Fori(0, KF // 2) as i:
                    for j in range(4):
                        pe.wait_ge(M["f_prod"], i * 2 + j // 2 + 1)
                        W.times(pe, i, j, ps[:, j], hh, hl, x_split=M["n_lo"])

            @block.vector
            def _(dve):
                dve.sem_inc(M["f_prod"], 2)
                norm_split(*norm, dve=dve)
                with dve.Fori(0, KF // 2) as i:
                    for g in range(2):
                        dve.wait_ge(M["f_silu"], i * 2 + g + 1)
                        dve.wait_ge(M["w_mm"], i * 4 + 2 * g + 4)
                        nc.vector.tensor_tensor(a32[:, g], sg[:, g], ps[:, 2 * g + 1], ALU.mult).then_inc(M["f_prod"], 1)
                        dve.wait_ge(M["f_prod"], i * 2 + g + 3)
                        nc.vector.tensor_copy(ah[:, i * 2 + g], a32[:, g]).then_inc(M["f_ahi"], 1)
                        dve.wait_ge(M["f_ahi"], i * 2 + g + 1)
                        nc.vector.tensor_tensor(al[:, i * 2 + g], a32[:, g], ah[:, i * 2 + g].bitcast(F32),
                                                ALU.subtract).then_inc(M["f_act"], 1)
        clear(nc, M)


def ffn_down(nc, T, layer, which, ah, al):
    gate = T.mod[:, 48 * which + 16:48 * which + 24]
    H = KF // 2
    per = 6 if which else 12
    mod_layer, col0 = (1 - layer, 0) if which else (layer, 24)
    with ExitStack() as ctx:
        M = semaphores(nc, ctx, W_SEMS + "f_res m_row*3 m_dot m_raw m_passed")
        sb = lambda n, s, t=F32: ctx.enter_context(nc.sbuf_tensor(n + str(which), s, t))
        wrow = sb("m_wrow", [P, 3, 2, D])
        prod = sb("m_prod", [P, D])
        some = sb("m_some", [P, 12])
        W = Weights(nc, ctx, M, "d" + str(which), H,
                    lambda i, j: T.d["dn"][layer * 2 + which, i * 2 + j // 2][:, (j % 2) * H * P:(j % 2 + 1) * H * P])
        ps = ctx.enter_context(nc.psum_tensor("f_psD" + str(which), [P, 2, S], F32))
        with nc.Block() as block:
            @block.sync
            def _(sp):
                rows = mod_dots(nc, T, sp, None, M, wrow, prod, some, mod_layer, col0, KD // 2, per)
                with sp.Fori(0, KD // 2) as i:
                    for j in range(4):
                        W.load(sp, i, j)
                    rows(i)

            @block.gpsimd
            def _(pool):
                pool.sem_inc(M["w_lo"], 4)
                with pool.Fori(0, KD // 2) as i:
                    for j in range(4):
                        W.rest(pool, i, j)

            @block.scalar
            def _(act):
                with act.Fori(0, KD // 2) as i:
                    for j in range(4):
                        W.round(act, i, j)

            @block.tensor
            def _(pe):
                pe.sem_inc(M["w_mm"], 2)
                with pe.Fori(0, KD // 2) as i:
                    for j in range(4):
                        pe.wait_ge(M["f_res"], i * 2 + j // 2 + 1)
                        W.times(pe, i, j, ps[:, j // 2], ah, al, k0=(j % 2) * H, first=j % 2 == 0, last=j % 2 == 1)

            @block.vector
            def _(dve):
                dve.sem_inc(M["f_res"], 2)
                dve.sem_inc(M["m_dot"], 6)
                dots = mod_dots(nc, T, None, dve, M, wrow, prod, some, mod_layer, col0, KD // 2, per)
                with dve.Fori(0, KD // 2) as i:
                    dots(i)
                    for g in range(2):
                        dve.wait_ge(M["w_mm"], i * 4 + 2 * g + 4)
                        x = T.xT[:, i * 2 + g]
                        nc.vector.scalar_tensor_tensor(x, ps[:, g], gate[:, bass.ds(i * 2 + g, 1)], x,
                                                       ALU.mult, ALU.add).then_inc(M["f_res"], 1)
        clear(nc, M)


def ffn(nc, T, layer, which):
    with ExitStack() as ctx:
        ah = ctx.enter_context(nc.sbuf_tensor("f_ah" + str(which), [P, KF, S], F32R))
        al = ctx.enter_context(nc.sbuf_tensor("f_al" + str(which), [P, KF, S], F32R))
        ffn_up(nc, T, layer, which, ah, al)
        ffn_down(nc, T, layer, which, ah, al)


def proj(nc, T, layer):
    with ExitStack() as ctx:
        M = semaphores(nc, ctx, N_SEMS + W_SEMS + "p_rope p_wt p_out p_tmm p_tout")
        sb = lambda n, s, t=F32: ctx.enter_context(nc.sbuf_tensor(n, s, t))
        h = sb("p_h", [P, KD, S])
        hh = sb("p_hh", [P, KD, S], F32R)
        hl = sb("p_hl", [P, KD, S], F32R)
        tmp = sb("p_tmp", [P, 2, S])
        rstd = sb("p_rstd", [P, S])
        wt = sb("p_wt", [P, KD, NTOK])
        W = Weights(nc, ctx, M, "p", KD, lambda i, j: T.d["win"][layer, i * 4 + j])
        psN = ctx.enter_context(nc.psum_tensor("p_psN", [P, S], F32))
        psZ = ctx.enter_context(nc.psum_tensor("p_psZ", [P, 4, S], F32))
        psT = ctx.enter_context(nc.psum_tensor("p_psT", [P, 2, S], F32))
        chunks = ((0, 512), (512, NTOK - 512))
        norm = (nc, T, M, rstd[:, :], tmp, h, hh, hl, T.gain[:, 8:16], T.mod[:, 24:32])
        with nc.Block() as block:
            @block.sync
            def _(sp):
                for j in range(4):
                    W.load(sp, 0, j)
                sp.dma_start(wt[:, :, :], T.d["wtok"][layer]).then_inc(M["p_wt"], 16)
                sp.dma_start(T.rope[:, :], T.d["rope"]).then_inc(M["p_rope"], 16)
                with sp.Fori(1, NZ // 4) as i:
                    for j in range(4):
                        W.load(sp, i, j)
                sp.wait_ge(M["p_rope"], 16)

            @block.gpsimd
            def _(pool):
                pool.sem_inc(M["w_lo"], 4)
                W.first(W.rest, pool)
                norm_split(*norm, pool=pool)
                W.others(W.rest, pool, NZ // 4)

            @block.scalar
            def _(act):
                W.first(W.round, act)
                square_sums(nc, T, act, None, M, h[:, 0:2], psN[:, :], rstd[:, :])
                norm_split(*norm, act=act)
                W.others(W.round, act, NZ // 4)

            @block.tensor
            def _(pe):
                pe.sem_inc(M["w_mm"], 2)
                square_sums(nc, T, None, pe, M, h[:, 0:2], psN[:, :], None)
                with pe.Fori(0, NZ // 4) as i:
                    for j in range(4):
                        pe.wait_ge(M["p_out"], i * 4 + j + 1)
                        W.times(pe, i, j, psZ[:, j], hh, hl, x_split=M["n_lo"])
                pe.wait_ge(M["p_wt"], 16)
                for t in range(TT):
                    for c, (c0, cn) in enumerate(chunks):
                        if t:
                            pe.wait_ge(M["p_tout"], 2 * (t - 1) + c + 1)
                        for k in range(KD):
                            mm = nc.tensor.matmul(psT[:, c, 0:cn], h[:, k, t * P:(t + 1) * P],
                                                  wt[:, k, c0:c0 + cn], start=k == 0, stop=k == KD - 1)
                        mm.then_inc(M["p_tmm"], 1)

            @block.vector
            def _(dve):
                dve.sem_inc(M["p_out"], 4)
                norm_split(*norm, dve=dve)
                with dve.Fori(0, NZ // 4) as i:
                    for j in range(4):
                        dve.wait_ge(M["w_mm"], i * 4 + j + 3)
                        nc.vector.tensor_copy(T.z[:, i * 4 + j], psZ[:, j]).then_inc(M["p_out"], 1)
                for t in range(TT):
                    for c, (c0, cn) in enumerate(chunks):
                        dve.wait_ge(M["p_tmm"], 2 * t + c + 1)
                        nc.vector.tensor_copy(T.tok[:, t, c0:c0 + cn], psT[:, c, 0:cn]).then_inc(M["p_tout"], 1)
        clear(nc, M)


def rope_gate_cmp(nc, T, layer):
    with ExitStack() as ctx:
        M = semaphores(nc, ctx, "r_w r_rot r_rope r_ch r_var r_root r_tri r_vn r_gelu r_v r_sg r_sgo r_sig "
                          "c_pe c_mm1 c_silu c_tr c_hid c_mm2 c_k c_rot c_fin c_ch")
        sb = lambda n, s: ctx.enter_context(nc.sbuf_tensor(n, s, F32))
        t1 = sb("r_t1", [P, 2, S])
        wsT = sb("r_wsT", [P, 4, P])
        st = sb("r_st", [P, 3, 16])
        sqv = sb("r_sqv", [P, TT, 256])
        w1 = sb("c_w1", [P, 2, 16, 256])
        w2 = sb("c_w2", [P, 2, 2, HD])
        w2d = sb("c_w2d", [P, 2, 2 * HD])
        blk = sb("c_blk", [P, 2, 16, 2, NC])
        hidT = sb("c_hidT", [2 * NC, 2, 256])
        hid = sb("c_hid", [P, 2, 2, 2, NC])
        kr = sb("c_kr", [P, NC])
        kt = sb("c_kt", [P, 2, NC])
        psR = ctx.enter_context(nc.psum_tensor("r_psR", [P, 2, S], F32))
        psS = ctx.enter_context(nc.psum_tensor("r_psS", [P, 2, S], F32))
        psG = ctx.enter_context(nc.psum_tensor("c_psG", [2 * NC, 2, 256], F32))
        psH = ctx.enter_context(nc.psum_tensor("c_psH", [P, 2, 2, 2 * NC], F32))
        psK = ctx.enter_context(nc.psum_tensor("c_psK", [P, 4, P], F32))
        roped = [DQ, DQ + 1, DK, DK + 1, NQ, NQ + 1, NQ + 2, NQ + 3, KS, KW]
        v = T.tok[:, :, TG:TG + 256]
        with nc.Block() as block:
            @block.sync
            def _(sp):
                sp.dma_start(wsT[:, :, :], T.d["ws"][layer]).then_inc(M["r_w"], 16)
                sp.dma_start(w1[:, :, :, :], T.d["w1"][layer]).then_inc(M["r_w"], 16)
                sp.dma_start(w2[:, :, :, :], T.d["w2"][layer]).then_inc(M["r_w"], 16)
                sp.dma_start(w2d[:, :, :], T.d["w2d"][layer]).then_inc(M["r_w"], 16)

            @block.gpsimd
            def _(pool):
                made = 0
                for kv, z in ((0, KC), (1, VC)):
                    for g in range(2):
                        src = T.z[:, z + g, :].rearrange("p (c l two) -> p l c two", two=2, l=8)
                        for par in range(2):
                            rows = slice(64 * par, 64 * par + 64)
                            for lo in range(2):
                                if made:
                                    pool.wait_ge(M["c_pe"], made)
                                made += 1
                                col = P_PE + 16 * kv + 8 * lo
                                pos = T.par[rows, col:col + 8].unsqueeze(2).to_broadcast([64, 8, NC])
                                nc.gpsimd.tensor_tensor(blk[rows, kv, 8 * lo:8 * lo + 8, g, :],
                                                        src[rows, :, lo:lo + NC, par], pos,
                                                        ALU.add).then_inc(M["c_pe"], 1)
                pool.wait_ge(M["r_w"], 64)
                pool.wait_ge(M["c_pe"], 16)
                nc.gpsimd.affine_select(out=wsT[:, :, :], in_=wsT[:, :, :], compare_op=ALU.is_ge, fill=0.0,
                                        base=0, pattern=[[0, 4], [1, P]], channel_multiplier=-1).then_inc(M["r_tri"], 1)

            @block.scalar
            def _(act):
                nc.scalar.activation(v, v, ACT.Gelu_apprx_tanh).then_inc(M["r_gelu"], 1)
                nc.scalar.activation(T.z[:, GU:GU + 2], T.z[:, GU:GU + 2], ACT.Gelu_apprx_tanh).then_inc(M["r_gelu"], 1)
                nc.scalar.activation(T.tok[:, :, TGT:TGT + 24], T.tok[:, :, TGT:TGT + 24],
                                     ACT.Sigmoid).then_inc(M["r_sig"], 1)
                act.wait_ge(M["r_var"], 1)
                nc.scalar.activation(st[:, 1], st[:, 1], ACT.Sqrt).then_inc(M["r_root"], 1)
                for kv in range(2):
                    act.wait_ge(M["c_mm1"], kv + 1)
                    nc.scalar.activation(hidT[:, kv], psG[:, kv], ACT.Silu).then_inc(M["c_silu"], 1)
                act.wait_ge(M["c_tr"], 1)
                nc.scalar.activation(hid[:, :, :, :, :].rearrange("p k a g c -> p (k a g c)"),
                                     psH[:, :, :, :].rearrange("p k a c -> p (k a c)"),
                                     ACT.Copy).then_inc(M["c_hid"], 1)

            @block.tensor
            def _(pe):
                for n, z in enumerate(roped):
                    if n >= 2:
                        pe.wait_ge(M["r_rope"], n - 1)
                    r = C_ROTD if n < 4 else C_ROTN
                    nc.tensor.matmul(psR[:, n % 2], T.const[:, r:r + P], T.z[:, z], start=True,
                                     stop=True).then_inc(M["r_rot"], 1)
                pe.wait_ge(M["r_w"], 64)
                pe.wait_ge(M["c_pe"], 16)
                for kv in range(2):
                    if kv:
                        pe.wait_ge(M["c_silu"], 1)
                    for l in range(16):
                        mm = nc.tensor.matmul(psG[:, kv], blk[:, kv, l].rearrange("p g c -> p (g c)"),
                                              w1[:, kv, l, :], start=l == 0, stop=l == 15)
                    mm.then_inc(M["c_mm1"], 1)
                pe.wait_ge(M["c_silu"], 2)
                for kv in range(2):
                    for a in range(2):
                        mm = nc.tensor.transpose(psH[:, kv, a], hidT[:, kv, a * P:(a + 1) * P],
                                                 T.const[0:2 * NC, C_IDENT:C_IDENT + 2 * NC])
                mm.then_inc(M["c_tr"], 1)
                pe.wait_ge(M["c_hid"], 1)
                for g in range(2):
                    for a in range(2):
                        nc.tensor.matmul(psK[:, g, 0:NC], w2d[:, a], hid[:, 0, a, g], start=a == 0, stop=a == 1)
                for g in range(2):
                    for a in range(2):
                        mm = nc.tensor.matmul(psK[0:NC, 2 + g, 0:HD], hid[:, 1, a, g], w2[:, 1, a],
                                              start=a == 0, stop=a == 1)
                mm.then_inc(M["c_mm2"], 1)
                pe.wait_ge(M["c_k"], 3)
                nc.tensor.matmul(psH[:, 0, 0, 0:NC], T.const[:, C_ROTN:C_ROTN + P], kr[:, :], start=True,
                                 stop=True).then_inc(M["c_rot"], 1)
                pe.wait_ge(M["r_tri"], 1)
                for t in range(TT):
                    pe.wait_ge(M["r_vn"], t + 1)
                    for g in range(4):
                        mm = nc.tensor.matmul(psS[64 * (g % 2):64 * (g % 2) + 64, g // 2, t * P:(t + 1) * P],
                                              T.tok[:, t, TG + 64 * g:TG + 64 * g + 64], wsT[:, g],
                                              start=True, stop=True)
                mm.then_inc(M["r_sg"], 1)

            @block.vector
            def _(dve):
                link = Chain(dve, M["r_ch"])
                for n, z in enumerate(roped):
                    cos, sin = (C_COSD, C_SIND) if n < 4 else (C_COSN, C_SINN)
                    dve.wait_ge(M["r_rot"], n + 1)
                    link.add(nc.vector.tensor_tensor(t1[:, n % 2], psR[:, n % 2], T.rope[:, sin:sin + S], ALU.mult))
                    link(nc.vector.tensor_tensor(T.z[:, z], T.z[:, z], T.rope[:, cos:cos + S], ALU.mult))
                    nc.vector.tensor_tensor(T.z[:, z], T.z[:, z], t1[:, n % 2], ALU.add).then_inc(M["r_rope"], 1)
                dve.wait_ge(M["r_gelu"], 2)
                v4 = v.rearrange("p t (g d) -> p t g d", g=4)
                mu = st[:, 0].rearrange("p (t g) -> p t g", t=TT)
                va = st[:, 1].rearrange("p (t g) -> p t g", t=TT)
                q4 = sqv[:, :, :].rearrange("p t (g d) -> p t g d", g=4)
                for t in range(TT):
                    link.add(nc.vector.tensor_reduce(mu[:, t], v4[:, t], X, ALU.add))
                link.wait()
                link(nc.vector.tensor_scalar(st[:, 0], st[:, 0], 1.0 / HD, None, ALU.mult))
                for t in range(TT):
                    link.add(nc.vector.tensor_tensor(v4[:, t], v4[:, t],
                                                     mu[:, t].unsqueeze(2).to_broadcast([P, 4, HD]), ALU.subtract))
                link.wait()
                for t in range(TT):
                    link.add(nc.vector.tensor_tensor(q4[:, t], v4[:, t], v4[:, t], ALU.mult))
                link.wait()
                for t in range(TT):
                    link.add(nc.vector.tensor_reduce(va[:, t], q4[:, t], X, ALU.add))
                link.wait()
                nc.vector.tensor_scalar(st[:, 1], st[:, 1], 1.0 / HD, EPS, ALU.mult, ALU.add).then_inc(M["r_var"], 1)
                dve.wait_ge(M["r_root"], 1)
                link(nc.vector.reciprocal(st[:, 2], st[:, 1]))
                rs = st[:, 2].rearrange("p (t g) -> p t g", t=TT)
                lng = T.par[:, P_LNG:P_LNG + 256].rearrange("p (g d) -> p g d", g=4)
                for t in range(TT):
                    link.add(nc.vector.tensor_tensor(v4[:, t], v4[:, t],
                                                     rs[:, t].unsqueeze(2).to_broadcast([P, 4, HD]), ALU.mult))
                link.wait()
                for t in range(TT):
                    nc.vector.tensor_tensor(v4[:, t], v4[:, t], lng, ALU.mult).then_inc(M["r_vn"], 1)
                dve.wait_ge(M["c_mm2"], 1)
                nc.vector.tensor_copy(kr[0:64, :], psK[0:64, 0, 0:NC]).then_inc(M["c_k"], 1)
                nc.vector.tensor_copy(kr[64:128, :], psK[64:128, 1, 0:NC]).then_inc(M["c_k"], 1)
                nc.vector.tensor_copy(T.vcmp[0:NC, :, :], psK[0:NC, 2:4, 0:HD]).then_inc(M["c_k"], 1)
                dve.wait_ge(M["c_rot"], 1)
                dve.wait_ge(M["c_k"], 3)
                ends = slice(31, 31 + 16 * (NC - 1) + 1, 16)
                cosn = T.rope[:, C_COSN:C_COSN + S]
                sinn = T.rope[:, C_SINN:C_SINN + S]
                link.add(nc.vector.tensor_tensor(kt[:, 0], psH[:, 0, 0, 0:NC], sinn[:, ends], ALU.mult))
                link(nc.vector.tensor_tensor(kt[:, 1], kr[:, :], cosn[:, ends], ALU.mult))
                link(nc.vector.tensor_tensor(T.kcmp[:, :], kt[:, 0], kt[:, 1], ALU.add))
                dve.wait_ge(M["r_sg"], 1)
                for a in range(2):
                    b = T.par[:, P_BS + a * P:P_BS + (a + 1) * P]
                    s4 = t1[:, a].rearrange("p (n t) -> p n t", n=TT)
                    link.add(nc.vector.tensor_tensor(s4, psS[:, a].rearrange("p (n t) -> p n t", n=TT),
                                                     b.unsqueeze(1).to_broadcast([P, TT, P]), ALU.add))
                link.wait()
                for a in range(2):
                    link.add(nc.vector.tensor_tensor(T.y[:, a], T.z[:, GU + a], t1[:, a], ALU.mult))
        clear(nc, M)


def soft_attention(nc, T, layer, kind):
    da = kind == "da"
    TILES = 2 if da else 4
    scale = 32 ** -0.5 if da else 64 ** -0.5
    NP_ = 1 if da else 2
    SLOTS = 4
    LAG = 2
    with ExitStack() as ctx:
        M = semaphores(nc, ctx, "a_st a_kst a_vst a_s a_nm a_e a_pr a_ch a_t a_te a_pv a_o "
                                "a_cs a_cm a_ce a_cp a_ct a_cte b_sq b_mm b_root b_ch")
        sb = lambda n, s: ctx.enter_context(nc.sbuf_tensor(n, s, F32))
        qs = sb("a_q" + kind, [P, S])
        ks = sb("a_k" + kind, [P, S])
        vs = sb("a_v" + kind, [P, TT, 2, HD])
        pb = sb("a_p" + kind, [P, SLOTS, 2, S])
        PT = sb("a_pt" + kind, [P, 2, NP_, TT, S])
        mx = sb("a_mx" + kind, [P, SLOTS, 2])
        nm = sb("a_nm" + kind, [P, SLOTS, 2])
        sm = sb("a_sm" + kind, [P, SLOTS, 2])
        rc = sb("a_rc" + kind, [P, SLOTS, 2])
        cs = sb("a_cs" + kind, [P, TT, NC])
        cst = sb("a_cst" + kind, [P, 3, TT])
        ctp = sb("a_ctp" + kind, [NC, 2, S])
        sq = sb("a_sq" + kind, [P, 2, S if da else 1])
        rstd = sb("a_rstd" + kind, [P, 2, S if da else 1])
        oT = sb("a_o" + kind, [P, 2, S])
        psS = ctx.enter_context(nc.psum_tensor("a_psS" + kind, [P, 2, 2, S], F32))
        psT = ctx.enter_context(nc.psum_tensor("a_psT" + kind, [P, 2, S], F32))
        psO = ctx.enter_context(nc.psum_tensor("a_psO" + kind, [P, S], F32))
        psC = ctx.enter_context(nc.psum_tensor("a_psC" + kind, [P, S], F32))
        U = 2 * TT
        units = [(r, i) for r in range(2) for i in range(TT)]
        mask = T.const[:, C_MASK:C_MASK + P]
        with nc.Block() as block:
            @block.gpsimd
            def _(pool):
                pool.sem_inc(M["a_st"], 1)
                with pool.Fori(0, TILES) as t:
                    pool.wait_ge(M["a_s"], t * U + 1)
                    if not da:
                        pool.wait_ge(M["a_cs"], t * 2 + 1)
                    pool.wait_ge(M["a_st"], t + 1)
                    if da:
                        nc.gpsimd.tensor_copy(qs[:, :], T.z[:, t + DQ]).then_inc(M["a_st"], 1)
                        pool.wait_ge(M["a_pv"], t * 2 + 2)
                        pool.wait_ge(M["a_st"], t + 2)
                        nc.gpsimd.tensor_copy(vs[:, :].rearrange("p t r d -> p t (r d)"),
                                              T.tok[:, :, bass.ds(t * P + TD, P)]).then_inc(M["a_vst"], 1)
                        pool.wait_ge(M["a_vst"], t + 1)
                    else:
                        nc.gpsimd.tensor_copy(qs[:, :], T.z[:, t + NQ]).then_inc(M["a_st"], 1)

            @block.tensor
            def _(pe):
                pe.sem_inc(M["a_pv"], 2)
                pe.sem_inc(M["a_s"], 1)
                if not da:
                    pe.sem_inc(M["a_cs"], 1)
                pe.sem_inc(M["a_t"], SLOTS * NP_)
                pe.sem_inc(M["a_ct"], 1)
                def cmp_scores(t, r):
                    if r:
                        pe.wait_ge(M["a_cte"], t * 2 + r + 1)
                    else:
                        pe.wait_ge(M["a_cte"], t * 2 + 1)
                    for i in range(TT):
                        mm = nc.tensor.matmul(psC[:, 32 * i:32 * i + NC],
                                              qs[64 * r:64 * r + 64, i * P:(i + 1) * P],
                                              T.kcmp[64 * r:64 * r + 64, :], start=True, stop=True)
                    mm.then_inc(M["a_cs"], 1)

                def scores(t, u):
                    r, i = units[u]
                    if not u:
                        pe.wait_ge(M["a_st"], t + 2)
                        if da:
                            pe.wait_ge(M["a_kst"], t + 1)
                    pe.wait_ge(M["a_e"], t * 2 * U + 2 * u + 2)
                    n = P * (i + 1)
                    for m in range(2):
                        if da:
                            p0 = 64 * r + 32 * m
                            lhs, rhs = qs[p0:p0 + 32, i * P:(i + 1) * P], ks[p0:p0 + 32, 0:n]
                            tp = (p0, 0)
                        else:
                            p0 = 64 * r
                            lhs = qs[p0:p0 + 64, i * P:(i + 1) * P]
                            rhs = T.z[p0:p0 + 64, (KS, KW)[m], 0:n]
                            tp = (p0, 0)
                        mm = nc.tensor.matmul(psS[:, u % 2, m, 0:n], lhs, rhs, start=True, stop=True,
                                              tile_position=tp)
                    mm.then_inc(M["a_s"], 1)

                def turn_probs(t, u):
                    r, i = units[u]
                    for b in range(NP_):
                        n = NP_ * u + b
                        pe.wait_ge(M["a_pr"], t * NP_ * U + n + 1)
                        pe.wait_ge(M["a_te"], t * NP_ * U + n + 1)
                        for k in range(i + 1):
                            mm = nc.tensor.transpose(psT[:, n % 2, k * P:(k + 1) * P],
                                                     pb[:, u % SLOTS, b, k * P:(k + 1) * P],
                                                     T.const[:, C_IDENT:C_IDENT + P])
                        mm.then_inc(M["a_t"], 1)

                def cmp_turn(t, r):
                    pe.wait_ge(M["a_cp"], t * 2 + r + 1)
                    for i in range(TT):
                        mm = nc.tensor.transpose(psC[0:NC, i * P:(i + 1) * P], cs[:, i, :],
                                                 T.const[:, C_IDENT:C_IDENT + P])
                    mm.then_inc(M["a_ct"], 1)

                def values(t, r):
                    pe.wait_ge(M["a_te"], t * NP_ * U + NP_ * TT * (r + 1) + 2)
                    if da:
                        pe.wait_ge(M["a_vst"], t + 1)
                    pe.wait_ge(M["a_o"], t + 1)
                    o = psO[64 * r:64 * r + 64, :]
                    for b in range(NP_):
                        for k in range(TT):
                            lhs = vs[:, k, r] if da else \
                                T.tok[:, k, (TVS, TVW)[b] + 64 * r:(TVS, TVW)[b] + 64 * r + 64]
                            mm = nc.tensor.matmul(o[:, k * P:S], lhs, PT[:, r, b, k, k * P:S],
                                                  start=b == 0 and k == 0,
                                                  stop=da and k == TT - 1, skip_group_check=True)
                    if not da:
                        pe.wait_ge(M["a_cte"], t * 2 + r + 2)
                        mm = nc.tensor.matmul(o, T.vcmp[0:NC, r, :], ctp[:, r, :], start=False, stop=True,
                                              skip_group_check=True)
                    mm.then_inc(M["a_pv"], 1)

                def step(t, u):
                    scores(t, u)
                    if not da and u % TT == 0:
                        cmp_scores(t, u // TT)

                def turn(t, more):
                    for u in range(LAG, U + LAG):
                        if u < U:
                            step(t, u)
                        turn_probs(t, u - LAG)
                        if u >= U and more:
                            step(t + 1, u - U)
                        if not da and u % TT == 2:
                            cmp_turn(t, u // TT)
                        if u == TT + LAG + 1:
                            values(t, 0)
                    values(t, 1)

                for u in range(LAG):
                    step(0, u)
                with pe.Fori(0, TILES - 1) as t:
                    turn(t, True)
                turn(TILES - 1, False)
                for n in range(2 if da else 0):
                    pe.wait_ge(M["b_sq"], n + 1)
                    pe.wait_ge(M["a_te"], TILES * U + 2)
                    nc.tensor.matmul((psC[:, :], psT[:, 0])[n], T.const[:, C_BLK:C_BLK + P], sq[:, n], start=True,
                                     stop=True).then_inc(M["b_mm"], 1)

            @block.scalar
            def _(act):
                act.sem_inc(M["a_e"], 4)
                act.sem_inc(M["a_te"], 2)
                def exps(t, u):
                    r, i = units[u]
                    n = P * (i + 1)
                    act.wait_ge(M["a_nm"], t * U + u + 1)
                    act.wait_ge(M["a_t"], t * NP_ * U + NP_ * (u + 1))
                    for m in range(2):
                        nc.scalar.activation(pb[:, u % SLOTS, m, 0:n], psS[:, u % 2, m, 0:n], ACT.Exp,
                                             bias=nm[:, u % SLOTS, m:m + 1], scale=scale,
                                             accum_out=sm[:, u % SLOTS, m:m + 1]).then_inc(M["a_e"], 1)

                def take_turned(t, u):
                    r, i = units[u]
                    for b in range(NP_):
                        n = NP_ * u + b
                        act.wait_ge(M["a_t"], t * NP_ * U + n + 1 + SLOTS * NP_)
                        act.wait_ge(M["a_pv"], t * 2 + r + 1)
                        nc.scalar.activation(PT[:, r, b, 0:i + 1, i * P:(i + 1) * P],
                                             psT[:, n % 2, 0:(i + 1) * P].rearrange("p (k q) -> p k q", q=P),
                                             ACT.Copy).then_inc(M["a_te"], 1)

                def step(t, u):
                    if da and not u:
                        act.wait_ge(M["a_s"], t * U + 1)
                        nc.scalar.activation(ks[:, :], T.z[:, t + DK], ACT.Copy).then_inc(M["a_kst"], 1)
                    exps(t, u)
                    if not da and u % TT == 1:
                        act.wait_ge(M["a_cm"], t * 2 + u // TT + 1)
                        nc.scalar.activation(cs[:, :, :], cs[:, :, :], ACT.Exp, scale=scale).then_inc(M["a_ce"], 1)

                def turn(t, more):
                    for u in range(LAG, U + LAG):
                        if u < U:
                            step(t, u)
                        elif more:
                            step(t + 1, u - U)
                        take_turned(t, u - LAG)

                for u in range(LAG):
                    step(0, u)
                with act.Fori(0, TILES - 1) as t:
                    turn(t, True)
                turn(TILES - 1, False)
                for n in range(2 if da else 0):
                    act.wait_ge(M["a_o"], n + 2)
                    nc.scalar.activation(sq[:, n], oT[:, n], ACT.Square).then_inc(M["b_sq"], 1)
                for n in range(2 if da else 0):
                    act.wait_ge(M["b_mm"], n + 1)
                    nc.scalar.activation(rstd[:, n], (psC[:, :], psT[:, 0])[n], ACT.Sqrt,
                                         bias=T.eps[:, 0:1]).then_inc(M["b_root"], 1)

            @block.vector
            def _(dve):
                dve.sem_inc(M["a_cte"], 1)
                dve.sem_inc(M["a_o"], 1)
                link = Chain(dve, M["a_ch"])
                per = 5 * U if da else 4 * U + 2 * 6
                def maxima(t, u):
                    r, i = units[u]
                    n = P * (i + 1)
                    dve.wait_ge(M["a_s"], t * U + u + 2)
                    d = psS[:, u % 2, :, i * P:n]
                    link(nc.vector.tensor_tensor(d, d, mask.unsqueeze(1).to_broadcast([P, 2, P]), ALU.add))
                    link(nc.vector.tensor_reduce(mx[:, u % SLOTS], psS[:, u % 2, :, 0:n], X, ALU.max))
                    nc.vector.tensor_scalar(nm[:, u % SLOTS], mx[:, u % SLOTS], -scale, None,
                                            ALU.mult).then_inc(M["a_nm"], 1)

                def weigh(t, u):
                    r, i = units[u]
                    n = P * (i + 1)
                    dve.wait_ge(M["a_e"], t * 2 * U + 2 * u + 2 + 4)
                    link(nc.vector.reciprocal(rc[:, u % SLOTS], sm[:, u % SLOTS]))
                    if da:
                        link(nc.vector.tensor_tensor(rc[:, u % SLOTS, 1:2], rc[:, u % SLOTS, 1:2], T.lam[:, 0:1], ALU.mult))
                        link(nc.vector.tensor_scalar(pb[:, u % SLOTS, 1, 0:n], pb[:, u % SLOTS, 1, 0:n],
                                                     rc[:, u % SLOTS, 1:2], None, ALU.mult))
                        nc.vector.scalar_tensor_tensor(pb[:, u % SLOTS, 0, 0:n], pb[:, u % SLOTS, 0, 0:n],
                                                       rc[:, u % SLOTS, 0:1], pb[:, u % SLOTS, 1, 0:n],
                                                       ALU.mult, ALU.subtract).then_inc(M["a_pr"], 1)
                    else:
                        link(nc.vector.tensor_tensor(rc[:, u % SLOTS], rc[:, u % SLOTS],
                                                     T.tok[:, i, bass.ds(t * 3 + TGT + 12 * r + 1, 2)], ALU.mult))
                        nc.vector.tensor_scalar(pb[:, u % SLOTS, 0, 0:n], pb[:, u % SLOTS, 0, 0:n],
                                                rc[:, u % SLOTS, 0:1], None, ALU.mult).then_inc(M["a_pr"], 1)
                        nc.vector.tensor_scalar(pb[:, u % SLOTS, 1, 0:n], pb[:, u % SLOTS, 1, 0:n],
                                                rc[:, u % SLOTS, 1:2], None, ALU.mult).then_inc(M["a_pr"], 1)

                def cmp_maxima(t, r):
                    dve.wait_ge(M["a_cs"], t * 2 + r + 2)
                    dve.wait_ge(M["a_ct"], t * 2 + r + 1)
                    add = T.const[:, C_CADD:C_CADD + TT * NC].rearrange("p (i c) -> p i c", i=TT)
                    sc = psC[:, 0:TT * 32].rearrange("p (i c) -> p i c", i=TT)[:, :, 0:NC]
                    link(nc.vector.tensor_tensor(cs[:, :, :], sc, add, ALU.add))
                    link(nc.vector.tensor_reduce(cst[:, 0], cs[:, :, :], X, ALU.max))
                    nc.vector.tensor_tensor(cs[:, :, :], cs[:, :, :],
                                            cst[:, 0].unsqueeze(2).to_broadcast([P, TT, NC]),
                                            ALU.subtract).then_inc(M["a_cm"], 1)

                def cmp_weigh(t, r):
                    dve.wait_ge(M["a_ce"], t * 2 + r + 1)
                    link(nc.vector.tensor_reduce(cst[:, 1], cs[:, :, :], X, ALU.add))
                    link(nc.vector.reciprocal(cst[:, 2], cst[:, 1]))
                    g = T.tok[:, :, bass.ds(t * 3 + TGT + 12 * r, 1)]
                    link(nc.vector.tensor_tensor(cst[:, 2].unsqueeze(2), cst[:, 2].unsqueeze(2), g, ALU.mult))
                    mul = T.const[:, C_CMUL:C_CMUL + TT * NC].rearrange("p (i c) -> p i c", i=TT)
                    link(nc.vector.tensor_tensor(cs[:, :, :], cs[:, :, :], mul, ALU.mult))
                    nc.vector.tensor_tensor(cs[:, :, :], cs[:, :, :],
                                            cst[:, 2].unsqueeze(2).to_broadcast([P, TT, NC]),
                                            ALU.mult).then_inc(M["a_cp"], 1)

                def step(t, u):
                    maxima(t, u)
                    if not da and u % TT == 0:
                        cmp_maxima(t, u // TT)
                    if u:
                        weigh(t, u - 1)
                    if not da and u % TT == 1:
                        cmp_weigh(t, u // TT)
                    if not da and u % TT == 3:
                        dve.wait_ge(M["a_ct"], t * 2 + u // TT + 2)
                        dve.wait_ge(M["a_pv"], t * 2 + 2)
                        nc.vector.tensor_copy(ctp[:, u // TT, :], psC[0:NC, :]).then_inc(M["a_cte"], 1)

                def turn(t, more):
                    for u in range(LAG, U):
                        step(t, u)
                    for u in range(LAG):
                        if more and u:
                            step(t + 1, u)
                        elif more:
                            maxima(t + 1, 0)
                            if not da:
                                cmp_maxima(t + 1, 0)
                        if not u:
                            weigh(t, U - 1)
                    dve.wait_ge(M["a_pv"], t * 2 + 2 + 2)
                    out = oT[:, t] if da else T.y[:, t + 4]
                    nc.vector.tensor_copy(out, psO[:, :]).then_inc(M["a_o"], 1)

                for u in range(LAG):
                    step(0, u)
                with dve.Fori(0, TILES - 1) as t:
                    link.enter(t, per)
                    turn(t, True)
                    link.leave(TILES - 1)
                turn(TILES - 1, False)
                assert link.n == TILES * per
                for n in range(2 if da else 0):
                    dve.wait_ge(M["b_root"], n + 1)
                    nc.vector.reciprocal(rstd[:, n], rstd[:, n]).then_inc(M["b_ch"], 1)
                    dve.wait_ge(M["b_ch"], n + 1)
                    nc.vector.scalar_tensor_tensor(T.y[:, 2 + n], oT[:, n], T.lam[:, 1:2], rstd[:, n],
                                                   ALU.mult, ALU.mult)
        clear(nc, M)


def out_proj(nc, T, w_of, first, tag):
    with ExitStack() as ctx:
        M = semaphores(nc, ctx, W_SEMS + "x_hi x_lo o_res")
        yh = ctx.enter_context(nc.sbuf_tensor("o_yh" + tag, [P, KD, S], F32R))
        yl = ctx.enter_context(nc.sbuf_tensor("o_yl" + tag, [P, KD, S], F32R))
        W = Weights(nc, ctx, M, "o" + tag, KD, lambda i, j: w_of(i * 4 + j))
        ps = ctx.enter_context(nc.psum_tensor("o_ps" + tag, [P, 4, S], F32))
        with nc.Block() as block:
            @block.sync
            def _(sp):
                with sp.Fori(0, KD // 4) as i:
                    for j in range(4):
                        W.load(sp, i, j)

            @block.scalar
            def _(act):
                split(nc, M, T.y, yh, yl, act=act, W=W)
                W.others(W.round, act, KD // 4)

            @block.gpsimd
            def _(pool):
                pool.sem_inc(M["w_lo"], 4)
                W.first(W.rest, pool)
                W.others(W.rest, pool, KD // 4)

            @block.tensor
            def _(pe):
                pe.sem_inc(M["w_mm"], 2)
                with pe.Fori(0, KD // 4) as i:
                    for j in range(4):
                        pe.wait_ge(M["o_res"], i * 4 + j + 1)
                        W.times(pe, i, j, ps[:, j], yh, yl, x_split=M["x_lo"])

            @block.vector
            def _(dve):
                dve.sem_inc(M["o_res"], 4)
                split(nc, M, T.y, yh, yl, dve=dve)
                with dve.Fori(0, KD // 4) as i:
                    for j in range(4):
                        dve.wait_ge(M["w_mm"], i * 4 + j + 3)
                        xt = T.xT[:, i * 4 + j]
                        if first:
                            nc.vector.scalar_tensor_tensor(xt, ps[:, j], T.mod[:, bass.ds(i * 4 + j + 40, 1)],
                                                           xt, ALU.mult, ALU.add).then_inc(M["o_res"], 1)
                        else:
                            nc.vector.scalar_tensor_tensor(xt, xt, ALPHA, ps[:, j],
                                                           ALU.mult, ALU.add).then_inc(M["o_res"], 1)
        clear(nc, M)


def final_norm(nc, T):
    with ExitStack() as ctx:
        M = semaphores(nc, ctx, "n_sq n_sum n_root n_rstd n_t n_h")
        sb = lambda n, s: ctx.enter_context(nc.sbuf_tensor(n, s, F32))
        sq = sb("z_sq", [P, 2, S])
        rstd = sb("z_rstd", [P, S])
        psN = ctx.enter_context(nc.psum_tensor("z_psN", [P, S], F32))
        with nc.Block() as block:
            @block.scalar
            def _(act):
                square_sums(nc, T, act, None, M, sq, psN[:, :], rstd[:, :])

            @block.tensor
            def _(pe):
                square_sums(nc, T, None, pe, M, sq, psN[:, :], None)

            @block.vector
            def _(dve):
                dve.wait_ge(M["n_root"], 1)
                nc.vector.reciprocal(rstd[:, :], rstd[:, :]).then_inc(M["n_rstd"], 1)
                dve.wait_ge(M["n_rstd"], 1)
                for k in range(KD):
                    nc.vector.scalar_tensor_tensor(T.xT[:, k], T.xT[:, k], T.q1[:, Q_FG + k:Q_FG + k + 1],
                                                   rstd[:, :], ALU.mult, ALU.mult).then_inc(M["n_h"], 1)
        clear(nc, M)


def proj2(nc, T):
    with ExitStack() as ctx:
        M = semaphores(nc, ctx, W_SEMS + "x_hi x_lo p_wt p_out p_tmm p_tout")
        sb = lambda n, s, t=F32: ctx.enter_context(nc.sbuf_tensor(n, s, t))
        wt = sb("p2_wt", [P, KD, 256])
        xh = sb("p2_xh", [P, KD, S], F32R)
        xl = sb("p2_xl", [P, KD, S], F32R)
        W = Weights(nc, ctx, M, "p2", KD, lambda i, j: T.d["win2"][i * 4 + j])
        psZ = ctx.enter_context(nc.psum_tensor("p2_psZ", [P, 4, S], F32))
        psT = ctx.enter_context(nc.psum_tensor("p2_psT", [P, 2, S], F32))
        with nc.Block() as block:
            @block.sync
            def _(sp):
                with sp.Fori(0, 4) as i:
                    for j in range(4):
                        W.load(sp, i, j)
                sp.dma_start(wt[:, :, :], T.d["wtok2"]).then_inc(M["p_wt"], 16)

            @block.scalar
            def _(act):
                split(nc, M, T.xT, xh, xl, act=act, W=W)
                W.others(W.round, act, 4)

            @block.gpsimd
            def _(pool):
                pool.sem_inc(M["w_lo"], 4)
                W.first(W.rest, pool)
                W.others(W.rest, pool, 4)

            @block.tensor
            def _(pe):
                pe.sem_inc(M["w_mm"], 2)
                with pe.Fori(0, 4) as i:
                    for j in range(4):
                        pe.wait_ge(M["p_out"], i * 4 + j + 1)
                        W.times(pe, i, j, psZ[:, j], xh, xl, x_split=M["x_lo"])
                pe.wait_ge(M["p_wt"], 16)
                for t in range(TT):
                    if t >= 2:
                        pe.wait_ge(M["p_tout"], t - 1)
                    for k in range(KD):
                        mm = nc.tensor.matmul(psT[:, t % 2, 0:256], T.xT[:, k, t * P:(t + 1) * P],
                                              wt[:, k, :], start=k == 0, stop=k == KD - 1)
                    mm.then_inc(M["p_tmm"], 1)

            @block.vector
            def _(dve):
                dve.sem_inc(M["p_out"], 4)
                split(nc, M, T.xT, xh, xl, dve=dve)
                with dve.Fori(0, 4) as i:
                    for j in range(4):
                        dve.wait_ge(M["w_mm"], i * 4 + j + 3)
                        nc.vector.tensor_copy(T.z[:, i * 4 + j], psZ[:, j]).then_inc(M["p_out"], 1)
                for t in range(TT):
                    dve.wait_ge(M["p_tmm"], t + 1)
                    nc.vector.tensor_copy(T.tok[:, t], psT[:, t % 2, 0:256]).then_inc(M["p_tout"], 1)
        clear(nc, M)


def convs(nc, T):
    A, G, PI, CH, GB, GC = 0, 2, 4, 6, 8, 10
    TAPS = 18
    W31, PADA, PADP, PADC = 31, 32, 16, 2
    with ExitStack() as ctx:
        M = semaphores(nc, ctx, "v_w v_sig v_pad v_ch v_conv v_mu v_sq v_var v_root v_cen v_nrm v_pool v_pmm "
                               "v_diag v_u v_dmm v_pc v_cp v_win v_sc")
        sb = lambda n, s: ctx.enter_context(nc.sbuf_tensor(n, s, F32))
        u = sb("v_u", [P, 2, PADA + S])
        h = sb("v_h", [P, 2, S])
        sq = sb("v_sq", [P, 2, S])
        rstd = sb("v_rstd", [P, S])
        sums = sb("v_sums", [P, 4, 2, PADP + S])
        diag = sb("v_diagb", [P, 2, W31 - TAPS, P])
        scaled = sb("v_scaled", [P, 3, 2, S])
        pin = sb("v_pin", [P, 2, PADP + S])
        pooled = sb("v_pooled", [P, 2, S])
        first = sb("v_first", [P, 2, 16])
        cp = sb("v_cp", [P, 2, PADC + S])
        ch = sb("v_ch_", [P, 2, S])
        pw = sb("v_pw", [P, 2, HD])
        psD = ctx.enter_context(nc.psum_tensor("v_psD", [P, 2, S], F32))
        psM = ctx.enter_context(nc.psum_tensor("v_psM", [P, 2, S], F32))
        psP = ctx.enter_context(nc.psum_tensor("v_psP", [P, 2, S], F32))
        q1 = T.q1
        with nc.Block() as block:
            @block.sync
            def _(sp):
                sp.dma_start(pw[:, :, :], T.d["pw"]).then_inc(M["v_w"], 16)

            @block.gpsimd
            def _(pool):
                pads = [(u, PADA), (pin, PADP), (cp, PADC)] + [(sums[:, n], PADP) for n in range(3)]
                for n, (buf, pad) in enumerate(pads):
                    nc.gpsimd.memset(buf[:, :, 0:pad], 0.0).then_inc(M["v_pad"], 1)
                link = Chain(pool, M["v_pc"])
                nc.gpsimd.tensor_tensor(cp[:, :, PADC:], T.z[:, GC:GC + 2], T.z[:, CH:CH + 2],
                                        ALU.mult).then_inc(M["v_cp"], 1)
                link(nc.gpsimd.tensor_copy(pin[:, :, PADP:], T.z[:, PI:PI + 2]))
                pool.wait_ge(M["v_pad"], len(pads))
                for n in range(4):
                    src = sums[:, n - 1] if n else pin
                    if n:
                        pool.wait_ge(M["v_win"], n)
                    nc.gpsimd.tensor_tensor(sums[:, n, :, PADP:], src[:, :, PADP:],
                                            src[:, :, PADP - 2 ** n:PADP + S - 2 ** n],
                                            ALU.add).then_inc(M["v_win"], 1)
                pool.wait_ge(M["v_sc"], 6)
                link(nc.gpsimd.tensor_tensor(ch[:, :], scaled[:, 0], scaled[:, 1], ALU.add))
                link(nc.gpsimd.tensor_tensor(ch[:, :], ch[:, :], scaled[:, 2], ALU.add))
                link(nc.gpsimd.tensor_tensor(T.y[:, 4:6], ch[:, :], T.z[:, GB:GB + 2], ALU.mult))

            @block.scalar
            def _(act):
                nc.scalar.activation(T.z[:, G:G + 2], T.z[:, G:G + 2], ACT.Sigmoid).then_inc(M["v_sig"], 1)
                for a in range(2):
                    for tap in range(TAPS, W31):
                        w = q1[:, Q_CAW + 31 * a + tap:Q_CAW + 31 * a + tap + 1]
                        nc.scalar.activation(diag[:, a, tap - TAPS], T.const[:, C_IDENT:C_IDENT + P], ACT.Copy,
                                             scale=w).then_inc(M["v_diag"], 1)
                act.wait_ge(M["v_cp"], 1)
                act.wait_ge(M["v_pad"], 6)
                for a in range(2):
                    for tap in range(3):
                        w = q1[:, Q_CCW + 3 * a + tap:Q_CCW + 3 * a + tap + 1]
                        nc.scalar.activation(scaled[:, tap, a], cp[:, a, tap:tap + S], ACT.Copy,
                                             scale=w).then_inc(M["v_sc"], 1)
                for a in range(2):
                    act.wait_ge(M["v_cen"], a + 1)
                    nc.scalar.activation(sq[:, a], h[:, a], ACT.Square).then_inc(M["v_sq"], 1)
                act.wait_ge(M["v_var"], 1)
                nc.scalar.activation(rstd[:, :], psM[:, 1], ACT.Sqrt, bias=T.eps[:, 1:2]).then_inc(M["v_root"], 1)
                act.wait_ge(M["v_nrm"], 2)
                for a in range(2):
                    nc.scalar.activation(T.y[:, a], h[:, a], ACT.Silu, scale=q1[:, Q_NG + a:Q_NG + a + 1],
                                         bias=q1[:, Q_NB + a:Q_NB + a + 1])

            @block.tensor
            def _(pe):
                c256 = T.const[:, C_BLK256:C_BLK256 + P]
                pe.wait_ge(M["v_u"], 1)
                pe.wait_ge(M["v_pad"], 6)
                for a in range(2):
                    for tap in range(TAPS, W31):
                        pe.wait_ge(M["v_diag"], a * (W31 - TAPS) + tap - TAPS + 1)
                        mm = nc.tensor.matmul(psD[:, a], diag[:, a, tap - TAPS],
                                              u[:, a, PADA - 30 + tap:PADA - 30 + tap + S],
                                              start=tap == TAPS, stop=tap == W31 - 1)
                    mm.then_inc(M["v_dmm"], 1)
                pe.wait_ge(M["v_conv"], 2 * TAPS + 2)
                for a in range(2):
                    mm = nc.tensor.matmul(psM[:, 0], c256, h[:, a], start=a == 0, stop=a == 1)
                mm.then_inc(M["v_mu"], 1)
                pe.wait_ge(M["v_w"], 16)
                pe.wait_ge(M["v_pool"], 4)
                for a in range(2):
                    for r in (0, 64):
                        mm = nc.tensor.matmul(psP[r:r + 64, a], pw[r:r + 64, a], pooled[r:r + 64, a],
                                              start=True, stop=True)
                mm.then_inc(M["v_pmm"], 1)
                pe.wait_ge(M["v_sq"], 2)
                for a in range(2):
                    mm = nc.tensor.matmul(psM[:, 1], c256, sq[:, a], start=a == 0, stop=a == 1)
                mm.then_inc(M["v_var"], 1)

            @block.vector
            def _(dve):
                link = Chain(dve, M["v_ch"])
                dve.wait_ge(M["v_sig"], 1)
                nc.vector.tensor_tensor(u[:, :, PADA:], T.z[:, A:A + 2], T.z[:, G:G + 2],
                                        ALU.mult).then_inc(M["v_u"], 1)
                dve.wait_ge(M["v_u"], 1)
                dve.wait_ge(M["v_pad"], 6)
                for n in range(2 * TAPS):
                    tap, a = divmod(n, 2)
                    src = u[:, a, PADA - 30 + tap:PADA - 30 + tap + S]
                    w = q1[:, Q_CAW + 31 * a + tap:Q_CAW + 31 * a + tap + 1]
                    if tap == 0:
                        ins = nc.vector.tensor_scalar(h[:, a], src, w, q1[:, Q_CAB + a:Q_CAB + a + 1],
                                                      ALU.mult, ALU.add)
                    else:
                        dve.wait_ge(M["v_conv"], n - 1)
                        ins = nc.vector.scalar_tensor_tensor(h[:, a], src, w, h[:, a], ALU.mult, ALU.add)
                    ins.then_inc(M["v_conv"], 1)
                for a in range(2):
                    dve.wait_ge(M["v_dmm"], a + 1)
                    dve.wait_ge(M["v_conv"], 2 * TAPS - 1 + a)
                    nc.vector.tensor_tensor(h[:, a], h[:, a], psD[:, a], ALU.add).then_inc(M["v_conv"], 1)
                parts = [(n, slice(64 * (n % 2), 64 * (n % 2) + 64), n // 2) for n in range(4)]
                for n, rows, a in parts:
                    inv = T.const[rows, C_INVC + 16 * a:C_INVC + 16 * a + 16]
                    dve.wait_ge(M["v_win"], n + 1)
                    link.add(nc.vector.scalar_tensor_tensor(pooled[rows, a], sums[rows, n, a, PADP:], inv[:, 15:16],
                                                            T.z[rows, PI + a], ALU.mult, ALU.subtract))
                    link.add(nc.vector.tensor_tensor(first[rows, a], sums[rows, n, a, PADP:PADP + 16], inv, ALU.mult))
                link.wait()
                for n, rows, a in parts:
                    nc.vector.tensor_tensor(pooled[rows, a, 0:16], first[rows, a], T.z[rows, PI + a, 0:16],
                                            ALU.subtract).then_inc(M["v_pool"], 1)
                dve.wait_ge(M["v_mu"], 1)
                for a in range(2):
                    nc.vector.tensor_tensor(h[:, a], h[:, a], psM[:, 0], ALU.subtract).then_inc(M["v_cen"], 1)
                dve.wait_ge(M["v_pmm"], 1)
                for a in range(2):
                    link.add(nc.vector.tensor_scalar(T.y[:, 2 + a], psP[:, a], q1[:, Q_PSC + a:Q_PSC + a + 1], None,
                                                 ALU.mult))
                dve.wait_ge(M["v_root"], 1)
                link(nc.vector.reciprocal(rstd[:, :], rstd[:, :]))
                dve.wait_ge(M["v_cen"], 2)
                for a in range(2):
                    nc.vector.tensor_tensor(h[:, a], h[:, a], rstd[:, :], ALU.mult).then_inc(M["v_nrm"], 1)
        clear(nc, M)


def stick_attention(nc, T):
    Q, K = 12, 14
    scale = HD ** -0.5
    H = 2
    with ExitStack() as ctx:
        M = semaphores(nc, ctx, "k_st k_vst k_s k_z k_abs k_exp k_ln k_ch k_cst k_add k_sp k_sub k_w k_lw "
                               "k_p k_t k_te k_pv k_o")
        sb = lambda n, s: ctx.enter_context(nc.sbuf_tensor(n, s, F32))
        qs = sb("k_q", [P, S])
        ks = sb("k_k", [P, S])
        vs = sb("k_v", [P, TT, 2, HD])
        zs = sb("k_zs", [P, H, TT, S])
        e = sb("k_e", [P, H, TT, S])
        sp_ = sb("k_sp", [P, TT, S])
        cum = sb("k_cum", [P, H, TT, S])
        ones = sb("k_ones", [P, S])
        nmask = sb("k_nmask", [P, P])
        tot = sb("k_tot", [P, H, TT])
        PT = sb("k_pt", [P, TT, S])
        psS = ctx.enter_context(nc.psum_tensor("k_psS", [P, TT, S], F32))
        psT = ctx.enter_context(nc.psum_tensor("k_psT", [P, 2, S], F32))
        psO = ctx.enter_context(nc.psum_tensor("k_psO", [P, S], F32))
        strict = T.const[:, C_STRICT:C_STRICT + P]
        with nc.Block() as block:
            @block.gpsimd
            def _(pool):
                pool.sem_inc(M["k_st"], 1)
                with pool.Fori(0, 2) as t:
                    pool.wait_ge(M["k_s"], t * H * TT + 1)
                    pool.wait_ge(M["k_st"], t * 2 + 1)
                    nc.gpsimd.tensor_copy(qs[:, :], T.z[:, t + Q]).then_inc(M["k_st"], 1)
                    pool.wait_ge(M["k_st"], t * 2 + 2)
                    nc.gpsimd.tensor_copy(ks[:, :], T.z[:, t + K]).then_inc(M["k_st"], 1)
                    for r in range(H):
                        b = t * H * TT + r * TT
                        for i in range(TT):
                            n = P * (i + 1)
                            pool.wait_ge(M["k_sp"], b + i + 1)
                            nc.gpsimd.tensor_tensor(zs[:, r, i, 0:n], zs[:, r, i, 0:n], sp_[:, i, 0:n],
                                                    ALU.subtract).then_inc(M["k_sub"], 1)
                        for i in range(TT):
                            d = slice(i * P, (i + 1) * P)
                            pool.wait_ge(M["k_sub"], b + i + 1)
                            if not r and not i:
                                pool.wait_ge(M["k_cst"], 2)
                            nc.gpsimd.tensor_tensor(zs[:, r, i, d], zs[:, r, i, d], nmask[:, :],
                                                    ALU.add).then_inc(M["k_w"], 1)
                        if not r:
                            pool.wait_ge(M["k_pv"], t * H + 1)
                            nc.gpsimd.tensor_copy(vs[:, :, :, :].rearrange("p t r d -> p t (r d)"),
                                                  T.tok[:, :, bass.ds(t * P, P)]).then_inc(M["k_vst"], 1)

            @block.tensor
            def _(pe):
                pe.sem_inc(M["k_s"], 1)
                pe.sem_inc(M["k_pv"], 1)
                pe.sem_inc(M["k_t"], 1)
                with pe.Fori(0, 2) as t:
                    pe.wait_ge(M["k_st"], t * 2 + 2 + 1)
                    for r in range(H):
                        rows = slice(64 * r, 64 * r + 64)
                        for i in range(TT):
                            pe.wait_ge(M["k_z"], (t * H + r) * TT + (i + 1 - TT if r else 0) + 1)
                            nc.tensor.matmul(psS[:, i, 0:P * (i + 1)], qs[rows, i * P:(i + 1) * P],
                                             ks[rows, 0:P * (i + 1)], start=True, stop=True).then_inc(M["k_s"], 1)
                    for r in range(H):
                        rows = slice(64 * r, 64 * r + 64)
                        for i in range(TT):
                            pe.wait_ge(M["k_p"], t * H * TT + r * TT + i + 2)
                            n = r * TT + i
                            if n >= 2:
                                pe.wait_ge(M["k_te"], t * H * TT + n - 1 + 1)
                            else:
                                pe.wait_ge(M["k_te"], t * H * TT + 1)
                            for k in range(i + 1):
                                mm = nc.tensor.transpose(psT[:, n % 2, k * P:(k + 1) * P],
                                                         e[:, r, i, k * P:(k + 1) * P],
                                                         T.const[:, C_IDENT:C_IDENT + P])
                            mm.then_inc(M["k_t"], 1)
                        pe.wait_ge(M["k_te"], t * H * TT + (r + 1) * TT + 1)
                        pe.wait_ge(M["k_vst"], t + 1)
                        pe.wait_ge(M["k_o"], t + 1)
                        for k in range(TT):
                            mm = nc.tensor.matmul(psO[rows, k * P:S], vs[:, k, r], PT[:, k, k * P:S],
                                                  start=k == 0, stop=k == TT - 1, skip_group_check=True)
                        mm.then_inc(M["k_pv"], 1)

            @block.scalar
            def _(act):
                act.sem_inc(M["k_z"], 1)
                act.sem_inc(M["k_te"], 1)
                act.sem_inc(M["k_p"], 1)
                with act.Fori(0, 2) as t:
                    for r in range(H):
                        b = t * H * TT + r * TT
                        if not r:
                            act.wait_ge(M["k_t"], b + 1)
                        for i in range(TT):
                            n = P * (i + 1)
                            act.wait_ge(M["k_s"], b + i + 2)
                            nc.scalar.activation(zs[:, r, i, 0:n], psS[:, i, 0:n], ACT.Copy,
                                                 scale=scale).then_inc(M["k_z"], 1)
                        for i in range(TT):
                            n = P * (i + 1)
                            act.wait_ge(M["k_z"], b + i + 2)
                            nc.scalar.activation(e[:, r, i, 0:n], zs[:, r, i, 0:n], ACT.Abs).then_inc(M["k_abs"], 1)
                        for i in range(TT):
                            n = P * (i + 1)
                            act.wait_ge(M["k_abs"], b + i + 1)
                            nc.scalar.activation(e[:, r, i, 0:n], e[:, r, i, 0:n], ACT.Exp,
                                                 scale=-1.0).then_inc(M["k_exp"], 1)
                        for i in range(TT):
                            n = P * (i + 1)
                            act.wait_ge(M["k_exp"], b + i + 1)
                            nc.scalar.activation(e[:, r, i, 0:n], e[:, r, i, 0:n], ACT.Ln,
                                                 bias=1.0).then_inc(M["k_ln"], 1)
                    for r in range(H):
                        b = t * H * TT + r * TT
                        for i in range(TT):
                            n = P * (i + 1)
                            act.wait_ge(M["k_lw"], b + i + 1)
                            nc.scalar.activation(e[:, r, i, 0:n], cum[:, r, i, 0:n], ACT.Exp,
                                                 bias=tot[:, r, i:i + 1]).then_inc(M["k_p"], 1)
                        for i in range(TT):
                            act.wait_ge(M["k_t"], b + i + 2)
                            act.wait_ge(M["k_pv"], t * H + r + 1)
                            nc.scalar.activation(PT[:, 0:i + 1, i * P:(i + 1) * P],
                                                 psT[:, (r * TT + i) % 2, 0:(i + 1) * P].rearrange(
                                                     "p (k q) -> p k q", q=P), ACT.Copy).then_inc(M["k_te"], 1)

            @block.vector
            def _(dve):
                dve.sem_inc(M["k_o"], 1)
                nc.vector.memset(ones[:, :], 1.0).then_inc(M["k_cst"], 1)
                nc.vector.tensor_scalar(nmask[:, :], strict, 1.0, -NEG, ALU.subtract, ALU.mult).then_inc(M["k_cst"], 1)
                dve.wait_ge(M["k_cst"], 2)
                link = Chain(dve, M["k_ch"])
                with dve.Fori(0, 2) as t:
                    link.enter(t, 2 * H * TT)
                    for r in range(H):
                        b = t * H * TT + r * TT
                        for i in range(TT):
                            n = P * (i + 1)
                            dve.wait_ge(M["k_ln"], b + i + 1)
                            nc.vector.scalar_tensor_tensor(sp_[:, i, 0:n], zs[:, r, i, 0:n], 0.0, e[:, r, i, 0:n],
                                                           ALU.max, ALU.add).then_inc(M["k_add"], 1)
                        for i in range(TT):
                            d = slice(i * P, (i + 1) * P)
                            dve.wait_ge(M["k_add"], b + i + 1)
                            nc.vector.tensor_tensor(sp_[:, i, d], sp_[:, i, d], strict,
                                                    ALU.mult).then_inc(M["k_sp"], 1)
                        dve.wait_ge(M["k_p"], t * H * TT + 1)
                        for i in range(TT):
                            n = P * (i + 1)
                            dve.wait_ge(M["k_sp"], b + i + 1)
                            link.add(nc.vector.tensor_tensor_scan(cum[:, r, i, 0:n], ones[:, 0:n], sp_[:, i, 0:n], 0.0,
                                                                  ALU.mult, ALU.add))
                        link.wait()
                        for i in range(TT):
                            n = P * (i + 1)
                            link.add(nc.vector.tensor_scalar(tot[:, r, i:i + 1], cum[:, r, i, n - 1:n], -1.0, None,
                                                             ALU.mult))
                        link.wait()
                        for i in range(TT):
                            n = P * (i + 1)
                            dve.wait_ge(M["k_w"], b + i + 1)
                            nc.vector.tensor_tensor(cum[:, r, i, 0:n], cum[:, r, i, 0:n], zs[:, r, i, 0:n],
                                                    ALU.add).then_inc(M["k_lw"], 1)
                    dve.wait_ge(M["k_pv"], t * H + H + 1)
                    nc.vector.tensor_copy(T.y[:, t + 6], psO[:, :]).then_inc(M["k_o"], 1)
                    link.leave(2)
        clear(nc, M)


def layer_norm_features(nc, T):
    with ExitStack() as ctx:
        M = semaphores(nc, ctx, "l_mu l_cen l_sq l_sum l_root l_r l_t l_x")
        sb = lambda n, s: ctx.enter_context(nc.sbuf_tensor(n, s, F32))
        sq = sb("l_sqb", [P, 2, S])
        tmp = sb("l_tmp", [P, 2, S])
        rstd = sb("l_rstd", [P, S])
        ps = ctx.enter_context(nc.psum_tensor("l_ps", [P, 2, S], F32))
        ones = T.const[:, C_ONES:C_ONES + P]
        with nc.Block() as block:
            @block.tensor
            def _(pe):
                for k in range(KD):
                    mm = nc.tensor.matmul(ps[:, 0], ones, T.xT[:, k], start=k == 0, stop=k == KD - 1)
                mm.then_inc(M["l_mu"], 1)
                for k in range(KD):
                    pe.wait_ge(M["l_sq"], k + 1)
                    nc.tensor.matmul(ps[:, 1], ones, sq[:, k % 2], start=k == 0,
                                     stop=k == KD - 1).then_inc(M["l_sum"], 1)

            @block.scalar
            def _(act):
                for k in range(KD):
                    act.wait_ge(M["l_cen"], k + 1)
                    if k >= 2:
                        act.wait_ge(M["l_sum"], k - 1)
                    nc.scalar.activation(sq[:, k % 2], T.xT[:, k], ACT.Square).then_inc(M["l_sq"], 1)
                act.wait_ge(M["l_sum"], KD)
                nc.scalar.activation(rstd[:, :], ps[:, 1], ACT.Sqrt, bias=T.eps[:, 1:2]).then_inc(M["l_root"], 1)
                for k in range(KD):
                    act.wait_ge(M["l_t"], k + 1)
                    nc.scalar.activation(T.xT[:, k], tmp[:, k % 2], ACT.Identity,
                                         scale=T.q1[:, Q_L1G + k:Q_L1G + k + 1],
                                         bias=T.q1[:, Q_L1B + k:Q_L1B + k + 1]).then_inc(M["l_x"], 1)

            @block.vector
            def _(dve):
                dve.wait_ge(M["l_mu"], 1)
                for k in range(KD):
                    nc.vector.tensor_tensor(T.xT[:, k], T.xT[:, k], ps[:, 0], ALU.subtract).then_inc(M["l_cen"], 1)
                dve.wait_ge(M["l_root"], 1)
                nc.vector.reciprocal(rstd[:, :], rstd[:, :]).then_inc(M["l_r"], 1)
                dve.wait_ge(M["l_r"], 1)
                for k in range(KD):
                    if k >= 2:
                        dve.wait_ge(M["l_x"], k - 1)
                    nc.vector.tensor_tensor(tmp[:, k % 2], T.xT[:, k], rstd[:, :], ALU.mult).then_inc(M["l_t"], 1)
        clear(nc, M)


def peer_keys(nc, T):
    with ExitStack() as ctx:
        M = semaphores(nc, ctx, W_SEMS + "x_hi x_lo e_keys e_passed e_q e_sc e_top e_ch e_x e_xo")
        sb = lambda n, s, t=F32: ctx.enter_context(nc.sbuf_tensor(n, s, t))
        keys = sb("e_keysb", [P, 2 * PH, KEYS])
        q = sb("e_qb", [P, 4, S])
        rest = sb("e_rest", [P, TT, KEYS])
        tv = sb("e_tv", [P, TT, TOP])
        ti = sb("e_ti", [P, TT, TOP], U32)
        xh = sb("e_xh", [P, KD, S], F32R)
        xl = sb("e_xl", [P, KD, S], F32R)
        W = Weights(nc, ctx, M, "e", KD, lambda i, j: T.d["wq"][i * 4 + j])
        psQ = ctx.enter_context(nc.psum_tensor("e_psQ", [P, 4, S], F32))
        psS = ctx.enter_context(nc.psum_tensor("e_psS", [P, 2, S], F32))
        psX = ctx.enter_context(nc.psum_tensor("e_psX", [P, 2, S], F32))
        with nc.Block() as block:
            @block.sync
            def _(sp):
                sp.dma_start(keys[:, :, :], T.d["keys"]).then_inc(M["e_keys"], 16)
                with sp.Fori(0, PH // 2) as i:
                    for j in range(4):
                        W.load(sp, i, j)

            @block.gpsimd
            def _(pool):
                pool.sem_inc(M["w_lo"], 4)
                W.first(W.rest, pool)
                W.others(W.rest, pool, PH // 2)

            @block.tensor
            def _(pe):
                pe.sem_inc(M["w_mm"], 2)
                pe.sem_inc(M["e_sc"], 4)
                pe.wait_ge(M["e_keys"], 16)
                with pe.Fori(0, PH // 2) as i:
                    def scores(j):
                        pe.wait_ge(M["e_q"], i * 4 + j + 5)
                        pe.wait_ge(M["e_top"], i * 4 + j + 1)
                        for t in range(TT):
                            mm = nc.tensor.matmul(psS[:, j % 2, t * P:(t + 1) * P], q[:, j, t * P:(t + 1) * P],
                                                  keys[:, i * 4 + j], start=True, stop=True)
                        mm.then_inc(M["e_sc"], 1)

                    for j in range(4):
                        pe.wait_ge(M["e_q"], i * 4 + j + 1)
                        W.times(pe, i, j, psQ[:, j], xh, xl, x_split=M["x_lo"])
                        if j:
                            scores(j - 1)
                    scores(3)
                for k in range(KD):
                    if k >= 2:
                        pe.wait_ge(M["e_xo"], k - 1)
                    for t in range(TT):
                        mm = nc.tensor.transpose(psX[:, k % 2, t * P:(t + 1) * P], T.xT[:, k, t * P:(t + 1) * P],
                                                 T.const[:, C_IDENT:C_IDENT + P])
                    mm.then_inc(M["e_x"], 1)

            @block.scalar
            def _(act):
                act.sem_inc(M["e_q"], 4)
                split(nc, M, T.xT, xh, xl, act=act, W=W)
                def turn(i, more):
                    def queries(j):
                        act.wait_ge(M["w_mm"], i * 4 + j + 3)
                        act.wait_ge(M["e_sc"], i * 4 + j + 1)
                        nc.scalar.activation(q[:, j], psQ[:, j], ACT.Copy).then_inc(M["e_q"], 1)

                    W.round(act, i, 2)
                    queries(0)
                    W.round(act, i, 3)
                    queries(1)
                    if more:
                        W.round(act, i + 1, 0)
                    queries(2)
                    if more:
                        W.round(act, i + 1, 1)
                    queries(3)

                with act.Fori(0, PH // 2 - 1) as i:
                    turn(i, True)
                turn(PH // 2 - 1, False)
                for k in range(KD):
                    act.wait_ge(M["e_x"], k + 1)
                    nc.scalar.activation(T.xtok[:, :, k * P:(k + 1) * P],
                                         psX[:, k % 2].rearrange("p (t d) -> p t d", d=P),
                                         ACT.Copy).then_inc(M["e_xo"], 1)

            @block.vector
            def _(dve):
                dve.sem_inc(M["e_top"], 2)
                split(nc, M, T.xT, xh, xl, dve=dve)
                topv = T.topv[:, 0:2 * TT * PH].rearrange("p (t h) k -> p t h k", t=TT)
                topi = T.topi[:, 0:2 * TT * PH].rearrange("p (t h) k -> p t h k", t=TT)
                link = Chain(dve, M["e_ch"], M["e_passed"])
                with dve.Fori(0, PH // 2) as i:
                    link.enter(i, 4 * (5 * TT + 1))
                    for j in range(4):
                        dve.wait_ge(M["e_sc"], i * 4 + j + 5)
                        dve.sem_inc(M["e_passed"], 1)
                        sc = [psS[:, j % 2, t * P:(t + 1) * P] for t in range(TT)]
                        for t in range(TT):
                            link.add(nc.vector.max(tv[:, t, 0:8], sc[t]))
                        link.wait()
                        for t in range(TT):
                            link.add(nc.vector.max_index(ti[:, t, 0:8], tv[:, t, 0:8], sc[t]))
                        for t in range(TT):
                            link.add(nc.vector.match_replace(rest[:, t], tv[:, t, 0:8], sc[t], -3e38))
                        link.wait()
                        for t in range(TT):
                            link.add(nc.vector.max(tv[:, t, 8:16], rest[:, t]))
                        link.wait()
                        for t in range(TT):
                            link.add(nc.vector.max_index(ti[:, t, 8:16], tv[:, t, 8:16], rest[:, t]))
                        link.wait()
                        link.add(nc.vector.tensor_copy(topv[:, :, i * 4 + j], tv[:, :, :]))
                        nc.vector.tensor_copy(topi[:, :, i * 4 + j], ti[:, :, :]).then_inc(M["e_top"], 1)
                        dve.wait_ge(M["e_top"], i * 4 + j + 3)
                    link.leave(PH // 2)
        clear(nc, M)


def choose(nc, T, B, link, dve, M, n):
    full = [P, TOP, TOP]
    link(nc.vector.tensor_copy(B["tv"], T.topv[:, bass.ds(n * 2, 2)]))
    link.add(nc.vector.tensor_tensor(B["cand"].rearrange("p (a b) -> p a b", b=TOP),
                                     B["tv"][:, 0].unsqueeze(2).to_broadcast(full),
                                     B["tv"][:, 1].unsqueeze(1).to_broadcast(full), ALU.add))
    link(nc.vector.tensor_copy(B["ti"], T.topi[:, bass.ds(n * 2, 2)]))
    link(nc.vector.max(B["best"][:, 0:8], B["cand"]))
    link.add(nc.vector.max_index(B["pos"][:, 0:8], B["best"][:, 0:8], B["cand"]))
    link(nc.vector.match_replace(B["rest"], B["best"][:, 0:8], B["cand"], -3e38))
    link(nc.vector.max(B["best"][:, 8:16], B["rest"]))
    link(nc.vector.max_index(B["pos"][:, 8:16], B["best"][:, 8:16], B["rest"]))
    nc.vector.tensor_scalar(B["dif"], B["best"], B["best"][:, 0:1], None, ALU.subtract).then_inc(M["h_dif"], 1)
    link.add(nc.vector.tensor_scalar(B["part"][:, 0], B["pos"], 4, None, ALU.logical_shift_right))
    link(nc.vector.tensor_scalar(B["part"][:, 1], B["pos"], 15, None, ALU.bitwise_and))
    link(nc.vector.tensor_copy(B["partf"], B["part"]))
    eq = B["eq"]
    iota = T.const[:, C_IOTA:C_IOTA + TOP].unsqueeze(1).to_broadcast(full)
    for m in range(2):
        link.add(nc.vector.tensor_tensor(eq[:, m], B["partf"][:, m].unsqueeze(2).to_broadcast(full), iota,
                                         ALU.is_equal))
    link.wait()
    for m in range(2):
        link.add(nc.vector.tensor_tensor(eq[:, m], eq[:, m], B["ti"][:, m].unsqueeze(1).to_broadcast(full),
                                         ALU.mult))
    link.wait()
    link(nc.vector.tensor_reduce(B["key"], eq, X, ALU.add))
    link(nc.vector.scalar_tensor_tensor(B["key"][:, 0], B["key"][:, 0], float(KEYS), B["key"][:, 1],
                                        ALU.mult, ALU.add))
    link.add(nc.vector.tensor_copy(T.idx[:, n], B["key"][:, 0]))
    dve.wait_ge(M["h_exp"], n + 1)
    link(nc.vector.tensor_reduce(B["sum"], B["dif"], X, ALU.add))
    link(nc.vector.reciprocal(B["sum"], B["sum"]))
    link(nc.vector.tensor_scalar(T.gates[:, n], B["dif"], B["sum"], None, ALU.mult))
    dve.sem_inc(M["h_pick"], 1)


CHOOSE_STEPS = 21
LEAD = 2


def peer_experts(nc, T):
    G, SETS = 4, 4
    NG = NSEL // (G * SETS)
    W = G * SETS
    assert NG == PH
    with ExitStack() as ctx:
        M = semaphores(nc, ctx, f"g_idx g_passed g_passed_v g_x g_u*{2 * G} g_v*{W} g_dot g_gelu g_w g_diag "
                                "g_mm g_r g_ln g_al g_ch g_free g_cp g_rt g_out g_fin h_dif h_exp h_pick h_zero")
        sb = lambda n, s, t=F32: ctx.enter_context(nc.sbuf_tensor(n, s, t))
        ub = sb("g_ub", [P, 2, G, D])
        vb = sb("g_vb", [P, SETS, G, D])
        ix = sb("g_ix", [P, SETS, G], U32)
        prod = sb("g_prod", [P, D])
        xrow = sb("g_xrow", [P, D])
        dot = sb("g_dotb", [P, SETS, G])
        wgt = sb("g_wgt", [P, SETS, G])
        diag = sb("g_diagb", [P, SETS, G, P])
        aid = sb("g_aid", [P, P])
        r = sb("g_rb", [P, D])
        lnp = sb("g_lnp", [P, 2, D])
        st = sb("g_st", [P, 2, 6])
        mv = sb("g_mv", [P, 4])
        B = {"tv": sb("h_tv", [P, 2, TOP])[:, :, :], "ti": sb("h_ti", [P, 2, TOP])[:, :, :],
             "cand": sb("h_cand", [P, TOP * TOP])[:, :], "rest": sb("h_rest", [P, TOP * TOP])[:, :],
             "best": sb("h_best", [P, TOP])[:, :], "pos": sb("h_pos", [P, TOP], U32)[:, :],
             "dif": sb("h_difb", [P, TOP])[:, :], "part": sb("h_part", [P, 2, TOP], U32)[:, :, :],
             "partf": sb("h_partf", [P, 2, TOP])[:, :, :], "eq": sb("h_eq", [P, 2, TOP, TOP])[:, :, :, :],
             "key": sb("h_key", [P, 2, TOP])[:, :, :], "sum": sb("h_sum", [P, 1])[:, :]}
        psF = ctx.enter_context(nc.psum_tensor("g_psF", [P, 2, S], F32))
        ident = T.const[:, C_IDENT:C_IDENT + P]
        with nc.Block() as block:
            @block.gpsimd
            def _(pool):
                with pool.Fori(0, TT) as t:
                    with pool.Fori(0, NG) as g:
                        n = t * NG + g
                        pool.wait_ge(M["h_pick"], n + 1)
                        for s in range(SETS):
                            pool.wait_ge(M["g_dot"], n * W + (s + 1) * G)
                            pool.wait_ge(M["g_mm"], n * SETS + s + 1)
                            if s:
                                pool.wait_ge(M["g_idx"], n * SETS + s)
                            nc.gpsimd.tensor_copy(ix[:, s], T.idx[:, n, s * G:s * G + G]).then_inc(M["g_idx"], 1)
                            pool.wait_ge(M["g_idx"], n * SETS + s + 1)
                            pool.sem_inc(M["g_passed"], 1)
                            for k in range(G):
                                nc.gpsimd.indirect_dma_start(
                                    ub[:, s % 2, k], None, T.d["u"],
                                    bass.IndirectOffsetOnAxis(ap=ix[:, s, k:k + 1], axis=0)
                                ).then_inc(M["g_u"][s % 2 * G + k], 16)
                            for k in range(G):
                                nc.gpsimd.indirect_dma_start(
                                    vb[:, s, k], None, T.d["v"],
                                    bass.IndirectOffsetOnAxis(ap=ix[:, s, k:k + 1], axis=0)
                                ).then_inc(M["g_v"][s * G + k], 16)

            @block.sync
            def _(sp):
                sp.sem_inc(M["g_free"], 1)
                sp.dma_start(lnp[:, :, :], T.d["ln2"]).then_inc(M["g_ln"], 16)
                with sp.Fori(0, TT) as t:
                    sp.wait_ge(M["g_fin"], t + 1)
                    sp.dma_start(T.d["out"][t], r[:, :]).then_inc(M["g_out"], 16)
                    sp.wait_ge(M["g_out"], t * 16 + 16)
                    sp.sem_inc(M["g_free"], 1)
                sp.wait_ge(M["g_out"], 16 * TT)

            @block.vector
            def _(dve):
                dve.sem_inc(M["g_dot"], 2 * G)
                dve.sem_inc(M["g_cp"], 1)
                nc.vector.tensor_scalar(aid[:, :], ident, ALPHA, None, ALU.mult).then_inc(M["g_al"], 1)
                nc.vector.memset(T.topv[:, 2 * TT * PH:], 0.0).then_inc(M["h_zero"], 1)
                nc.vector.memset(T.topi[:, 2 * TT * PH:], 0.0).then_inc(M["h_zero"], 1)
                dve.wait_ge(M["h_zero"], 2)
                link = Chain(dve, M["g_ch"], M["g_passed_v"])
                with dve.Fori(0, LEAD) as h:
                    link.enter(h, CHOOSE_STEPS)
                    choose(nc, T, B, link, dve, M, h)
                    link.leave(LEAD)
                dve.wait_ge(M["g_ln"], 16)
                with dve.Fori(0, TT) as t:
                    dve.wait_ge(M["g_dot"], t * (NG * W) + 2 * G)
                    nc.vector.tensor_copy(xrow[:, :], T.xtok[:, t]).then_inc(M["g_x"], 1)
                    dve.wait_ge(M["g_x"], t + 1)
                    dve.sem_inc(M["g_passed_v"], 1)
                    with dve.Fori(0, NG) as g:
                        n = t * NG + g
                        link.base = t * (NG * CHOOSE_STEPS + 7) + (g * CHOOSE_STEPS + LEAD * CHOOSE_STEPS)
                        link.n = 0
                        choose(nc, T, B, link, dve, M, n + LEAD)
                        assert link.n == CHOOSE_STEPS, link.n
                        for s in range(SETS):
                            for k in range(G):
                                dve.wait_ge(M["g_u"][s % 2 * G + k], n * 32 + 16 * (s // 2) + 16)
                                dve.wait_ge(M["g_dot"], n * W + s * G + k + 2 * G)
                                nc.vector.tensor_tensor_reduce(prod[:, :], ub[:, s % 2, k], xrow[:, :], 1.0, 0.0,
                                                               ALU.mult, ALU.add,
                                                               dot[:, s, k:k + 1]).then_inc(M["g_dot"], 1)
                            dve.wait_ge(M["g_gelu"], n * SETS + s + 1)
                            nc.vector.tensor_tensor(wgt[:, s], dot[:, s],
                                                    T.gates[:, n, s * G:s * G + G],
                                                    ALU.mult).then_inc(M["g_w"], 1)
                    link.base, link.n = t * (NG * CHOOSE_STEPS + 7) + (NG + LEAD) * CHOOSE_STEPS, 0
                    dve.wait_ge(M["g_r"], t + 1)
                    for c in range(2):
                        dve.wait_ge(M["g_free"], t + 1)
                        link(nc.vector.tensor_copy(r[:, c * S:(c + 1) * S], psF[:, c]))
                        link(nc.vector.bn_stats(st[:, c], r[:, c * S:(c + 1) * S]))
                    nc.vector.bn_aggr(mv[:, 0:2], st[:, :, :]).then_inc(M["g_cp"], 1)
                    dve.wait_ge(M["g_rt"], t + 1)
                    link(nc.vector.reciprocal(mv[:, 3:4], mv[:, 2:3]))
                    link(nc.vector.tensor_scalar(r[:, :], r[:, :], mv[:, 0:1], mv[:, 3:4], ALU.subtract, ALU.mult))
                    link(nc.vector.tensor_tensor(r[:, :], r[:, :], lnp[:, 0], ALU.mult))
                    nc.vector.tensor_tensor(r[:, :], r[:, :], lnp[:, 1], ALU.add).then_inc(M["g_fin"], 1)
                    assert link.n == 7, link.n

            @block.scalar
            def _(act):
                def exponents(n):
                    act.wait_ge(M["h_dif"], n + 1)
                    nc.scalar.activation(B["dif"], B["dif"], ACT.Exp).then_inc(M["h_exp"], 1)

                with act.Fori(0, LEAD) as h:
                    exponents(h)
                with act.Fori(0, TT) as t:
                    with act.Fori(0, NG) as g:
                        n = t * NG + g
                        exponents(n + LEAD)
                        for s in range(SETS):
                            act.wait_ge(M["g_dot"], n * W + (s + 1) * G + 2 * G)
                            nc.scalar.activation(dot[:, s], dot[:, s], ACT.Gelu_apprx_tanh).then_inc(M["g_gelu"], 1)
                            act.wait_ge(M["g_w"], n * SETS + s + 1)
                            act.wait_ge(M["g_mm"], n * SETS + s + 1)
                            for k in range(G):
                                nc.scalar.activation(diag[:, s, k], ident, ACT.Copy,
                                                     scale=wgt[:, s, k:k + 1]).then_inc(M["g_diag"], 1)
                    act.wait_ge(M["g_cp"], t + 2)
                    nc.scalar.activation(mv[:, 2:3], mv[:, 1:2], ACT.Sqrt, bias=T.eps[:, 1:2]).then_inc(M["g_rt"], 1)

            @block.tensor
            def _(pe):
                pe.sem_inc(M["g_mm"], SETS)
                pe.wait_ge(M["g_al"], 1)
                with pe.Fori(0, TT) as t:
                    pe.wait_ge(M["g_cp"], t + 1)
                    for c in range(2):
                        nc.tensor.matmul(psF[:, c], aid[:, :], T.xtok[:, t, c * S:(c + 1) * S], start=True,
                                         stop=False, skip_group_check=True)
                    with pe.Fori(0, NG) as g:
                        n = t * NG + g
                        for s in range(SETS):
                            for k in range(G):
                                pe.wait_ge(M["g_v"][s * G + k], n * 16 + 16)
                                pe.wait_ge(M["g_diag"], n * W + s * G + k + 1)
                                for c in range(2):
                                    mm = nc.tensor.matmul(psF[:, c], diag[:, s, k], vb[:, s, k, c * S:(c + 1) * S],
                                                          start=False, stop=False, skip_group_check=True)
                            mm.then_inc(M["g_mm"], 1)
                    for c in range(2):
                        mm = nc.tensor.matmul(psF[:, c], T.zero[:, :], T.xtok[:, t, c * S:(c + 1) * S], start=False,
                                              stop=True, skip_group_check=True)
                    mm.then_inc(M["g_r"], 1)


class Tensors:
    pass


def build(nc, d):
    T = Tensors()
    T.d = d
    with ExitStack() as ctx:
        sb = lambda n, s: ctx.enter_context(nc.sbuf_tensor(n, s, F32))
        T.const = sb("const", [P, C_ALL])
        T.xT = sb("xT", [P, KD, S])
        T.q1 = sb("q1", [P, Q_ALL])
        T.eps = sb("eps", [P, 2])
        T.zero = sb("zero", [P, P])
        with ExitStack() as c1:
            s1 = lambda n, s: c1.enter_context(nc.sbuf_tensor(n, s, F32))
            T.crow = s1("crow", [P, D])
            T.par = s1("par", [P, P_ALL])
            T.mod = s1("mod", [P, 72])
            T.gain = s1("gain", [P, 24])
            T.raw = s1("raw", [P, 72])
            T.lam = s1("lam", [P, 2])
            first_modulation(nc, T)
            with nc.Fori(0, L) as layer:
                modulation(nc, T, layer, [0])
                ffn(nc, T, layer, 0)
                modulation(nc, T, layer, [1, 2])
                with ExitStack() as c2:
                    s2 = lambda n, s: c2.enter_context(nc.sbuf_tensor(n, s, F32))
                    T.z = s2("z", [P, NZ, S])
                    T.tok = s2("tok", [P, TT, NTOK])
                    T.kcmp = s2("kcmp", [P, NC])
                    T.vcmp = s2("vcmp", [NC, 2, HD])
                    T.rope = s2("rope", [P, 4 * S])
                    proj(nc, T, layer)
                    T.y = s2("y", [P, KD, S])
                    rope_gate_cmp(nc, T, layer)
                    soft_attention(nc, T, layer, "da")
                    soft_attention(nc, T, layer, "nsa")
                    out_proj(nc, T, lambda n: T.d["wout"][layer, n], True, "1")
                ffn(nc, T, layer, 1)
            final_norm(nc, T)
        second_block(nc, T, ctx)


def second_block(nc, T, ctx):
    with ExitStack() as c2:
        s2 = lambda n, s: c2.enter_context(nc.sbuf_tensor(n, s, F32))
        T.z = s2("z2", [P, 16, S])
        T.tok = s2("tok2", [P, TT, 256])
        T.y = s2("y2", [P, KD, S])
        proj2(nc, T)
        convs(nc, T)
        stick_attention(nc, T)
        out_proj(nc, T, lambda n: T.d["wout2"][n], False, "2")
    layer_norm_features(nc, T)
    sb = lambda n, s, t=F32: ctx.enter_context(nc.sbuf_tensor(n, s, t))
    T.xtok = sb("xtok", [P, TT, D])
    T.idx = sb("idx", [P, TT * PH + LEAD, TOP], U32)
    T.gates = sb("gates", [P, TT * PH + LEAD, TOP])
    T.topv = sb("topv", [P, 2 * (TT * PH + LEAD), TOP])
    T.topi = sb("topi", [P, 2 * (TT * PH + LEAD), TOP])
    peer_keys(nc, T)
    peer_experts(nc, T)


def constants():
    c = np.zeros((P, C_ALL), np.float32)
    rope = np.zeros((P, 4 * S), np.float32)
    p = np.arange(P)
    c[:, C_IDENT:C_IDENT + P] = np.eye(P)
    c[:, C_ONES:C_ONES + P] = 1.0 / D
    c[:, C_BLK:C_BLK + P] = (p[:, None] // HD == p[None] // HD) / HD
    c[:, C_MASK:C_MASK + P] = np.where(p[None] <= p[:, None], 0.0, NEG)
    c[:, C_STRICT:C_STRICT + P] = p[None] < p[:, None]
    c[:, C_BLK256:C_BLK256 + P] = 1.0 / 256
    for at, cos, sin, half in ((C_ROTD, C_COSD, C_SIND, 16), (C_ROTN, C_COSN, C_SINN, 32)):
        inv = np.float32(10000.0) ** (-np.arange(half, dtype=np.float32) / np.float32(half))
        ang = np.arange(S, dtype=np.float32)[:, None] * inv[None].astype(np.float32)
        rope[:, cos:cos + S] = np.cos(ang)[:, p % half].T
        rope[:, sin:sin + S] = np.sin(ang)[:, p % half].T
        low = p % (2 * half) < half
        rot = np.zeros((P, P), np.float32)
        rot[p[low], p[low] + half] = -1.0
        rot[p[~low], p[~low] - half] = 1.0
        c[:, at:at + P] = rot.T
    q = np.arange(TT)[None, :, None] * P + p[:, None, None]
    ok = 16 * np.arange(NC)[None, None] + 31 <= q
    c[:, C_CADD:C_CADD + TT * NC] = np.where(ok, 0.0, NEG).reshape(P, -1)
    c[:, C_CMUL:C_CMUL + TT * NC] = ok.reshape(P, -1)
    for l in range(L):
        li = 0.8 - 0.6 * math.exp(-0.3 * l)
        c[:, C_LAM + 2 * l] = li
        c[:, C_LAM + 2 * l + 1] = 1.0 - li
    for t in range(16):
        for a in range(2):
            win = np.where(p < 64, (2, 8)[a], (4, 16)[a])
            c[:, C_INVC + 16 * a + t] = 1.0 / np.minimum(t + 1, win)
    c[:, C_IOTA:C_IOTA + 16] = np.arange(16)[None]
    return c, rope


def tiles(w, cols):
    k, n = w.shape[0] // P, len(cols) // P
    return w[:, cols].reshape(k, P, n, P).transpose(2, 1, 0, 3).reshape(n, P, k * P)


def columns(v):
    return v.reshape(-1, P).T


def layouts(i):
    a = {}
    c = np.ascontiguousarray
    a["const"], a["rope"] = constants()
    a["xT"] = c(i["x"][0].T.reshape(KD, P, S).transpose(1, 0, 2))
    a["c"] = c(np.broadcast_to(i["c"], (P, D)))
    a["ada"] = c(i["w_ada"].transpose(0, 2, 1).reshape(L, 36, 2, P, D).transpose(0, 1, 3, 2, 4))
    alln = np.arange
    a["gu"] = c(np.stack([np.stack([tiles(i[w][l, f], alln(FF)) for w in ("ffn_w_gate", "ffn_w_up")], 1)
                          for l in range(L) for f in range(2)]))
    a["dn"] = c(np.stack([tiles(i["ffn_w_down"][l, f], alln(D)) for l in range(L) for f in range(2)]))
    par = np.zeros((L, P, P_ALL), np.float32)
    for l in range(L):
        par[l, :, P_BADA:P_BADA + 72] = columns(i["b_ada"][l])
        for n in range(3):
            par[l, :, P_NG + 8 * n:P_NG + 8 * n + 8] = columns(i["norm_g"][l, n])
        par[l, :, P_LNG:P_LNG + 256] = i["gm_ln_g"][l][None]
        par[l, :, P_BS:P_BS + 256] = np.repeat(i["gm_b_s"][l].reshape(2, 2, P), 64, axis=1).transpose(1, 0, 2).reshape(P, 256)
        par[l, :, P_SUBG] = np.tile(i["da_sub_g"][l], 2)
        par[l, :, P_LAMV:P_LAMV + 128] = i["da_lambda"][l].reshape(1, 128)
        par[l, :, P_PE:P_PE + 32] = i["nsa_cmp_pe"][l].reshape(2, 16, 2, HD).transpose(2, 3, 0, 1).reshape(P, 32)
    a["par"] = par
    r = np.arange
    o = 1280
    q = [np.concatenate([r(o + 64 * t, o + 64 * t + 64), r(o + 64 * (t + 4), o + 64 * (t + 4) + 64)]) for t in range(4)]
    dup = lambda s: np.concatenate([r(s, s + 64)] * 2 + [r(s + 64, s + 128)] * 2)
    zc = np.concatenate([r(0, 256), r(512, 768), r(768, 1024)] + q + [dup(1792), dup(1920), r(2048, 2176), r(2304, 2432)])
    a["win"] = c(np.stack([tiles(i["w_in"][l], zc) for l in range(L)]))
    tc = np.concatenate([r(256, 512), r(1024, 1280), r(2176, 2304), r(2432, 2560), r(2560, 2584)])
    a["wtok"] = c(i["w_in"][:, :, tc].reshape(L, KD, P, NTOK).transpose(0, 2, 1, 3))
    a["ws"] = c(i["gm_w_s"].transpose(0, 3, 1, 2))
    a["w1"] = c(i["nsa_cmp_w1"].reshape(L, 2, 16, P, 256).transpose(0, 3, 1, 2, 4))
    w2 = i["nsa_cmp_w2"].reshape(L, 2, 2, P, HD).transpose(0, 3, 1, 2, 4)
    a["w2"] = c(w2)
    a["w2d"] = c(np.concatenate([w2[:, :, 0], w2[:, :, 0]], -1))
    yr = np.concatenate([r(0, 512)] + [x - o + 512 for x in q])
    a["wout"] = c(np.stack([tiles(i["w_out"][l][yr], r(D)) for l in range(L)]))
    second_layouts(i, a)
    return a


def second_layouts(i, a):
    c = np.ascontiguousarray
    r = np.arange
    q1 = np.zeros((P, Q_ALL), np.float32)
    q1[:, Q_CAW:Q_CAW + 62] = i["conv_a_w_2"][0].reshape(31, 2, P).transpose(2, 1, 0).reshape(P, 62)
    q1[:, Q_CCW:Q_CCW + 6] = i["conv_c_w_2"][0].reshape(3, 2, P).transpose(2, 1, 0).reshape(P, 6)
    for at, n in ((Q_CAB, "conv_a_b_2"), (Q_NG, "norm_a_g_2"), (Q_NB, "norm_a_b_2"), (Q_PSC, "pool_scale_2"),
                  (Q_L1G, "ln1_g_2"), (Q_L1B, "ln1_b_2")):
        v = columns(i[n][0])
        q1[:, at:at + v.shape[1]] = v
    q1[:, Q_FG:Q_FG + 8] = columns(i["final_g"])
    a["q1"] = q1
    w = i["w_in_2"][0]
    a["win2"] = c(tiles(w, r(2048)))
    a["wtok2"] = c(w[:, 2048:].reshape(KD, P, 256).transpose(1, 0, 2))
    a["pw"] = c(i["pool_w_2"][0].reshape(2, P, HD).transpose(1, 0, 2))
    a["wout2"] = c(tiles(i["w_out_2"][0], r(D)))
    a["wq"] = c(tiles(i["peer_wq_2"][0], r(2048)))
    a["keys"] = c(i["peer_keys_2"][0].transpose(3, 0, 1, 2).reshape(P, 16, KEYS))
    a["u"] = i["peer_u_2"][0]
    a["v"] = i["peer_v_2"][0]
    a["ln2"] = c(np.broadcast_to(np.stack([i["ln2_g_2"][0], i["ln2_b_2"][0]])[None], (P, 2, D)))


def kernel(**inputs):
    from concourse import bacc
    from concourse.bass_utils import run_bass_kernel_spmd

    nc = bacc.Bacc("TRN2", target_bir_lowering=False, num_devices=1)
    arrays, d = {}, {}
    for n, v in layouts({k: np.asarray(v) for k, v in inputs.items()}).items():
        arrays["in_" + n] = v
        d[n] = nc.dram_tensor("in_" + n, v.shape, F32, kind="ExternalInput").ap()
    d["out"] = nc.dram_tensor("out", (TT, P, D), F32, kind="ExternalOutput").ap()
    build(nc, d)
    got = run_bass_kernel_spmd(nc, [arrays], core_ids=[0])
    return got.results[0]["out"].reshape(1, S, D)
```
